# Optimizing a Trainium2 kernel written in Bass

```python
import jax, jax.numpy as jnp
from jax import lax
import numpy as np

D_MODEL = 1024
BATCH = 1
SEQ = 256
DEPTH = 2

D_MIX = D_MODEL
POOL_WIDTH = D_MIX // 4
POOL_WINDOWS = (2, 4, 8, 16)
POOL_GROUP = POOL_WIDTH // len(POOL_WINDOWS)
QK_NOPE = 128
QK_ROPE = 64
V_HEAD = 128
ATTN_WIDTH = D_MIX - POOL_WIDTH
N_HEADS = ATTN_WIDTH // V_HEAD
Q_LORA = 384
KV_LORA = 256
IN_WIDTH = POOL_WIDTH + Q_LORA + KV_LORA + QK_ROPE
ROPE_THETA = 10000.0
Q_BLOCK = 128
N_EXPERTS = 64
TOP_K = 8
N_GROUPS = 8
TOPK_GROUPS = 4
D_EXPERT = D_MODEL // 4
ROUTED_SCALE = 2.5
DISPATCH_BLOCK = 256
DEEPNORM_ALPHA = (2.0 * DEPTH) ** 0.25
DEEPNORM_BETA = (8.0 * DEPTH) ** -0.25
LN_EPS = 1e-5
RMS_EPS = 1e-6

kernel_name = "hybrid_pool_mla_moe_deepnorm_adaln"

def layer_norm(x, g, b):
    xf = x.astype(jnp.float32)
    mu = xf.mean(-1, keepdims=True)
    var = jnp.square(xf - mu).mean(-1, keepdims=True)
    return ((xf - mu) * lax.rsqrt(var + LN_EPS) * g.astype(jnp.float32) + b.astype(jnp.float32)).astype(x.dtype)

def rms_norm(x, g):
    xf = x.astype(jnp.float32)
    return (xf * lax.rsqrt(jnp.mean(xf * xf, -1, keepdims=True) + RMS_EPS) * g.astype(jnp.float32)).astype(x.dtype)

def apply_rope(x, positions):
    half = QK_ROPE // 2
    inv_freq = ROPE_THETA ** (-jnp.arange(half, dtype=jnp.float32) / half)
    ang = positions.astype(jnp.float32)[..., None] * inv_freq
    cos, sin = jnp.cos(ang), jnp.sin(ang)
    if x.ndim == 4:
        cos, sin = cos[:, :, None, :], sin[:, :, None, :]
    xf = x.astype(jnp.float32)
    x1, x2 = xf[..., :half], xf[..., half:]
    return jnp.concatenate([x1 * cos - x2 * sin, x2 * cos + x1 * sin], axis=-1).astype(x.dtype)

def causal_pool_mixer(u, w_pool, pool_scale):
    S = u.shape[1]
    uf = u.astype(jnp.float32)
    t = jnp.arange(S)
    outs = []
    for gi, w in enumerate(POOL_WINDOWS):
        ug = uf[..., gi * POOL_GROUP:(gi + 1) * POOL_GROUP]
        cs = jnp.cumsum(ug, axis=1)
        lagged = jnp.pad(cs, ((0, 0), (w, 0), (0, 0)))[:, :S]
        count = jnp.minimum(t + 1, w).astype(jnp.float32)[None, :, None]
        token_mix = (cs - lagged) / count - ug
        outs.append(jnp.einsum('bsc,cd->bsd', token_mix.astype(u.dtype), w_pool[gi]))
    return jnp.concatenate(outs, axis=-1) * pool_scale

def mla_mixer(q_lat, kv_lat, k_rope, positions, q_norm_g, kv_norm_g, w_uq, w_ukv):
    B, S, _ = q_lat.shape
    q = (rms_norm(q_lat, q_norm_g) @ w_uq).reshape(B, S, N_HEADS, QK_NOPE + QK_ROPE)
    q_nope, q_rope = q[..., :QK_NOPE], apply_rope(q[..., QK_NOPE:], positions)
    kv = (rms_norm(kv_lat, kv_norm_g) @ w_ukv).reshape(B, S, N_HEADS, QK_NOPE + V_HEAD)
    k_nope, v = kv[..., :QK_NOPE], kv[..., QK_NOPE:]
    k_rope = apply_rope(k_rope, positions)
    scale = (QK_NOPE + QK_ROPE) ** -0.5
    outs = []
    for i in range(S // Q_BLOCK):
        q0, q1 = i * Q_BLOCK, (i + 1) * Q_BLOCK
        s = (jnp.einsum('bqhd,bkhd->bhqk', q_nope[:, q0:q1], k_nope[:, :q1])
             + jnp.einsum('bqhr,bkr->bhqk', q_rope[:, q0:q1], k_rope[:, :q1])).astype(jnp.float32) * scale
        causal = jnp.arange(q0, q1)[:, None] >= jnp.arange(q1)[None, :]
        p = jax.nn.softmax(jnp.where(causal, s, -jnp.inf), axis=-1).astype(v.dtype)
        outs.append(jnp.einsum('bhqk,bkhd->bqhd', p, v[:, :q1]))
    return jnp.concatenate(outs, axis=1).reshape(B, S, ATTN_WIDTH)

def swiglu(x, w_gate, w_up, w_down):
    return (jax.nn.silu(x @ w_gate) * (x @ w_up)) @ w_down

def route(ht, w_router, router_bias):
    T = ht.shape[0]
    scores = jax.nn.sigmoid(ht.astype(jnp.float32) @ w_router.astype(jnp.float32))
    choice = (scores + router_bias.astype(jnp.float32)).reshape(T, N_GROUPS, N_EXPERTS // N_GROUPS)
    group_score = lax.top_k(choice, 2)[0].sum(-1)
    _, top_groups = lax.top_k(group_score, TOPK_GROUPS)
    group_mask = jax.nn.one_hot(top_groups, N_GROUPS, dtype=jnp.float32).sum(1) > 0
    masked = jnp.where(group_mask[:, :, None], choice, -jnp.inf).reshape(T, N_EXPERTS)
    _, idx = lax.top_k(masked, TOP_K)
    w = jnp.take_along_axis(scores, idx, axis=-1)
    w = w / w.sum(-1, keepdims=True) * ROUTED_SCALE
    return idx, w

def routed_moe(h, w_router, router_bias, w_gate, w_up, w_down):
    B, S, D = h.shape
    T = B * S
    ht = h.reshape(T, D)
    idx, gates = route(ht, w_router, router_bias)
    A = T * TOP_K
    flat_e = idx.reshape(A)
    flat_tok = (jnp.arange(A) // TOP_K).astype(jnp.int32)
    flat_g = gates.reshape(A)
    order = jnp.argsort(flat_e)
    e_sorted = flat_e[order]
    counts = jnp.bincount(flat_e, length=N_EXPERTS)
    start = jnp.cumsum(counts) - counts
    padded = (counts + DISPATCH_BLOCK - 1) // DISPATCH_BLOCK * DISPATCH_BLOCK
    pad_end = jnp.cumsum(padded)
    pad_start = pad_end - padded
    dest = pad_start[e_sorted] + (jnp.arange(A) - start[e_sorted])
    P = (-(-A // DISPATCH_BLOCK) + N_EXPERTS) * DISPATCH_BLOCK
    NB = P // DISPATCH_BLOCK
    buf_tok = jnp.zeros((P,), jnp.int32).at[dest].set(flat_tok[order])
    buf_gate = jnp.zeros((P,), jnp.float32).at[dest].set(flat_g[order])
    blk_expert = jnp.minimum(jnp.searchsorted(pad_end, jnp.arange(NB) * DISPATCH_BLOCK, side='right'),
                             N_EXPERTS - 1)

    def expert_block(acc, xs):
        e, tok, g = xs
        y = swiglu(ht[tok], w_gate[e], w_up[e], w_down[e])
        return acc.at[tok].add(g[:, None] * y.astype(jnp.float32)), None

    acc, _ = lax.scan(expert_block, jnp.zeros((T, D), jnp.float32),
                      (blk_expert, buf_tok.reshape(NB, DISPATCH_BLOCK), buf_gate.reshape(NB, DISPATCH_BLOCK)))
    return acc.astype(h.dtype).reshape(B, S, D)

def setup_inputs(seed: int = 0) -> dict:
    key = jax.random.key(seed)
    ks = jax.random.split(key, 26)
    L, D, E, F = DEPTH, D_MODEL, N_EXPERTS, D_EXPERT

    def nrm(k, shape, scale):
        return jax.random.normal(k, shape, jnp.float32) * scale

    return {
        "x": nrm(ks[0], (BATCH, SEQ, D), 1.0),
        "c": nrm(ks[1], (BATCH, D), 1.0),
        "positions": (jnp.arange(SEQ, dtype=jnp.int32)[None, :]
                      + jax.random.randint(ks[2], (BATCH, 1), 0, 4096, dtype=jnp.int32)),
        "w_ada": nrm(ks[3], (L, D, 6 * D), D ** -0.5),
        "b_ada": nrm(ks[4], (L, 6 * D), 0.01),
        "w_in": nrm(ks[5], (L, D, IN_WIDTH), D ** -0.5),
        "q_norm_g": 1.0 + nrm(ks[6], (L, Q_LORA), 0.01),
        "kv_norm_g": 1.0 + nrm(ks[7], (L, KV_LORA), 0.01),
        "w_uq": nrm(ks[8], (L, Q_LORA, N_HEADS * (QK_NOPE + QK_ROPE)), Q_LORA ** -0.5),
        "w_ukv": nrm(ks[9], (L, KV_LORA, N_HEADS * (QK_NOPE + V_HEAD)), KV_LORA ** -0.5),
        "w_pool": nrm(ks[10], (L, len(POOL_WINDOWS), POOL_GROUP, POOL_GROUP), POOL_GROUP ** -0.5),
        "pool_scale": 1.0 + nrm(ks[11], (L, POOL_WIDTH), 0.1),
        "w_out": nrm(ks[12], (L, D_MIX, D), DEEPNORM_BETA * D_MIX ** -0.5),
        "ln1_g": 1.0 + nrm(ks[13], (L, D), 0.01),
        "ln1_b": nrm(ks[14], (L, D), 0.01),
        "w_router": nrm(ks[15], (L, D, E), D ** -0.5),
        "router_bias": nrm(ks[16], (L, E), 0.01),
        "w_exp_gate": nrm(ks[17], (L, E, D, F), D ** -0.5),
        "w_exp_up": nrm(ks[18], (L, E, D, F), D ** -0.5),
        "w_exp_down": nrm(ks[19], (L, E, F, D), DEEPNORM_BETA * F ** -0.5),
        "w_sh_gate": nrm(ks[20], (L, D, F), D ** -0.5),
        "w_sh_up": nrm(ks[21], (L, D, F), D ** -0.5),
        "w_sh_down": nrm(ks[22], (L, F, D), DEEPNORM_BETA * F ** -0.5),
        "ln2_g": 1.0 + nrm(ks[23], (L, D), 0.01),
        "ln2_b": nrm(ks[24], (L, D), 0.01),
    }

def reference(x, c, positions, w_ada, b_ada, w_in, q_norm_g, kv_norm_g, w_uq, w_ukv, w_pool, pool_scale,
              w_out, ln1_g, ln1_b, w_router, router_bias, w_exp_gate, w_exp_up, w_exp_down,
              w_sh_gate, w_sh_up, w_sh_down, ln2_g, ln2_b):
    cond = jax.nn.silu(c)
    split_cols = [POOL_WIDTH, POOL_WIDTH + Q_LORA, POOL_WIDTH + Q_LORA + KV_LORA]
    for l in range(DEPTH):
        mod = (cond @ w_ada[l] + b_ada[l])[:, None, :]
        sh1, sc1, g1, sh2, sc2, g2 = jnp.split(mod, 6, axis=-1)
        h = x * (1.0 + sc1) + sh1
        u, q_lat, kv_lat, k_rope = jnp.split(h @ w_in[l], split_cols, axis=-1)
        pooled = causal_pool_mixer(u, w_pool[l], pool_scale[l])
        attn = mla_mixer(q_lat, kv_lat, k_rope, positions, q_norm_g[l], kv_norm_g[l], w_uq[l], w_ukv[l])
        mixed = jnp.concatenate([pooled, attn], axis=-1) @ w_out[l]
        x = layer_norm(DEEPNORM_ALPHA * x + g1 * mixed, ln1_g[l], ln1_b[l])
        h = x * (1.0 + sc2) + sh2
        ffn = (swiglu(h, w_sh_gate[l], w_sh_up[l], w_sh_down[l])
               + routed_moe(h, w_router[l], router_bias[l], w_exp_gate[l], w_exp_up[l], w_exp_down[l]))
        x = layer_norm(DEEPNORM_ALPHA * x + g2 * ffn, ln2_g[l], ln2_b[l])
    return x


_drawn_inputs = setup_inputs


def setup_inputs(seed=0):
    import zlib

    import numpy as np

    out = dict(_drawn_inputs(seed))
    spreads = {}
    factors = {'q_norm_g': 7.072, 'kv_norm_g': 4.11}
    for name, (base, spread) in spreads.items():
        noise = np.random.default_rng([zlib.crc32(name.encode()), seed]).standard_normal(out[name].shape)
        drawn = base * np.exp(spread * noise) if base else spread * noise
        out[name] = __import__('jax').numpy.asarray(drawn.astype(out[name].dtype))
    for name, factor in factors.items():
        out[name] = (out[name] * factor).astype(out[name].dtype)
    return out
```

```python
from contextlib import ExitStack

import numpy as np

import concourse.bass as bass
from concourse import mybir

P = 128
F32 = mybir.dt.float32
I32 = mybir.dt.int32
ALU = mybir.AluOpType
ACT = mybir.ActivationFunctionType
AX_X = mybir.AxisListType.X

NT = 2
T = NT * P
D = 1024
KT = D // P
L = 2
WINDOWS = (2, 4, 8, 16)
POOL = 256
QL, KVL, ROPE, NOPE, VH = 384, 256, 64, 128, 128
HALF = ROPE // 2
H = 6
INW = POOL + QL + KVL + ROPE
HW = INW // 2
QW = NOPE + ROPE
E, NG, TOPG, TOPK = 64, 8, 4, 8
F = 256
FT = F // P
UNIT = 64
RING = 4
ALPHA = (2.0 * L) ** 0.25
LN_EPS, RMS_EPS = 1e-5, 1e-6
ROUTED = 2.5
SCALE = float(QW) ** -0.5
NEG = -1e30
ADA_COLS = 512
ADA_SLOTS = 6
ADA_IT = L * 6 * D // ADA_COLS // ADA_SLOTS
MOD = 6 * D // P
TWO_PI_PARTS = (6.28125, 0.0019350051879882812, 3.0199159819567396e-07)
MAGIC = 12582912.0
SLOT_W = 3 * KT * F
DVE_LINKS = 82
U0 = 2
MAXU = U0 + L * (E + T * TOPK // UNIT + 2)

C_ID = 0
C_MASK = C_ID + P
C_UP = C_MASK + 3 * P
C_ONE = C_UP + P
C_IOTA = C_ONE + P
C_FREQ = C_IOTA + UNIT
C_LT = C_FREQ + HALF
C_N = C_LT + NG * NG


def shape_constants():
    c = np.zeros((P, C_N), np.float32)
    i = np.arange(P)
    c[:, C_ID:C_ID + P] = np.eye(P)
    causal = np.where(i[:, None] >= i[None, :], 0.0, NEG)
    c[:, C_MASK:C_MASK + P] = causal
    c[:, C_MASK + 2 * P:C_MASK + 3 * P] = causal
    c[:, C_UP:C_UP + P] = i[:, None] < i[None, :]
    c[:, C_ONE:C_ONE + P] = 1.0
    c[:, C_IOTA:C_IOTA + UNIT] = np.arange(UNIT)[None, :]
    c[:, C_FREQ:C_FREQ + HALF] = (10000.0 ** (-np.arange(HALF) / HALF)).astype(np.float32)[None, :]
    g = np.arange(NG)
    c[:, C_LT:] = (g[None, :] < g[:, None]).astype(np.float32).reshape(1, -1)
    t = np.arange(T)
    band = np.zeros((len(WINDOWS), T, T), np.float32)
    for k, w in enumerate(WINDOWS):
        inside = (t[:, None] <= t[None, :]) & (t[:, None] > t[None, :] - w)
        band[k] = inside / np.minimum(t + 1, w)[None, :] - np.eye(T)
    first = band[:, :P, :].transpose(1, 0, 2).reshape(P, -1)
    second = band[:, P:, P:].transpose(1, 0, 2).reshape(P, -1)
    return c, np.ascontiguousarray(np.concatenate([first, second], axis=1).astype(np.float32))


def decoder_trunk(nc, x, c, positions, w_ada, b_ada, w_in, q_norm_g, kv_norm_g, w_uq, w_ukv, w_pool,
                  pool_scale, w_out, ln1_g, ln1_b, w_router, router_bias, w_exp_gate, w_exp_up,
                  w_exp_down, w_sh_gate, w_sh_up, w_sh_down, ln2_g, ln2_b, consts_dram, band_dram, out):
    mod_dram = nc.dram_tensor("mod_rows", (L * MOD, P), F32, kind="Internal").ap()
    ds = bass.ds

    with ExitStack() as ctx:
        ctx.enter_context(nc.allow_non_contiguous_dma(reason="short vectors laid on partitions"))

        def sb(name, cols, dt=F32, rows=P):
            return ctx.enter_context(nc.sbuf_tensor(name, [rows, cols], dt))

        def sem(name):
            return ctx.enter_context(nc.semaphore(name))

        ring = sb("ring", RING * SLOT_W)
        w1 = sb("w1", KT * D)
        w2 = sb("w2", 6912)
        router_sb = sb("router_sb", KT * E)
        x_sb = sb("x_sb", NT * D)
        xT = sb("xT", KT * T)
        rows = sb("rows", 5 * D)
        temp = sb("temp", 2 * D)
        const = sb("const", C_N)
        modc = sb("modc", L * MOD)
        modl = sb("modl", MOD)
        small = sb("small", 160)
        colv = sb("colv", 8)
        utab = sb("utab", E + 1, I32, 1)

        x3 = x_sb[:, :].rearrange("p (j d) -> p j d", j=NT)
        xT3 = xT[:, :].rearrange("p (k t) -> p k t", k=KT)
        t3 = temp[:, :].rearrange("p (j d) -> p j d", j=NT)
        g_row, lng_row, lnb_row, sc_row, sh_row = (rows[:, i * D:(i + 1) * D] for i in range(5))
        win3 = w1[:, 0:KT * INW].rearrange("p (k n) -> p k n", k=KT)
        wout3 = w1[:, :].rearrange("p (k n) -> p k n", k=KT)
        uq3 = w2[:, 0:3 * H * QW].rearrange("p (k n) -> p k n", k=3)
        ukv3 = w2[:, 3456:3456 + 2 * H * 256].rearrange("p (k n) -> p k n", k=2)
        router3 = router_sb[:, :].rearrange("p (k e) -> p k e", k=KT)
        ident = const[:, C_ID:C_ID + P]
        mask = const[:, C_MASK:C_MASK + 3 * P]
        upper = const[:, C_UP:C_UP + P]
        ones = const[:, C_ONE:C_ONE + P]
        freq = const[:, C_FREQ:C_FREQ + HALF]

        def gate_w(s):
            return ring[:, s * SLOT_W:s * SLOT_W + KT * F].rearrange("p (k f) -> p k f", k=KT)

        def up_w(s):
            return ring[:, s * SLOT_W + KT * F:s * SLOT_W + 2 * KT * F].rearrange("p (k f) -> p k f", k=KT)

        def down_w(s):
            return ring[:, s * SLOT_W + 2 * KT * F:(s + 1) * SLOT_W].rearrange("p (k d) -> p k d", k=FT)

        ada = [ring[:, s * 4096:(s + 1) * 4096].rearrange("p (k n) -> p k n", k=KT) for s in range(ADA_SLOTS)]

        at = [2 * SLOT_W]

        def carve(n):
            at[0] += n
            return ring[:, at[0] - n:at[0]]

        proj3 = carve(NT * INW).rearrange("p (j n) -> p j n", j=NT)
        qT3 = carve(H * T).rearrange("p (h t) -> p h t", h=H)
        qrT3 = carve(3 * T).rearrange("p (h t) -> p h t", h=3)
        kT3 = carve(H * T).rearrange("p (h t) -> p h t", h=H)
        krT3 = carve(2 * T).rearrange("p (v t) -> p v t", v=2)
        v3 = carve(NT * H * VH).rearrange("p (j n) -> p j n", j=NT)
        latT3 = carve(5 * T).rearrange("p (k t) -> p k t", k=5)
        band_sb = carve(len(WINDOWS) * (T + P))
        band0 = band_sb[:, 0:len(WINDOWS) * T].rearrange("p (g t) -> p g t", t=T)
        band1 = band_sb[:, len(WINDOWS) * T:].rearrange("p (g t) -> p g t", t=P)
        tmT3 = carve(2 * T).rearrange("p (g t) -> p g t", g=2)
        wpool3 = carve(2 * 64).rearrange("p (g d) -> p g d", g=2)
        assert at[0] <= RING * SLOT_W

        qr3 = t3[:, :, 0:H * ROPE]
        qr4 = qr3.rearrange("p j (h r) -> p j h r", h=H)
        krp = t3[:, :, 384:384 + 2 * P].rearrange("p j (v n) -> p j v n", v=2)
        rtmp = t3[:, :, 640:832].rearrange("p j (h r) -> p j h r", h=H)
        ktmp = t3[:, :, 832:864]
        sP = temp[:, 0:768].rearrange("p (b n) -> p b n", b=2)
        PT = temp[:, 768:1536].rearrange("p (b n) -> p b n", b=2)
        junk = temp[:, 1536:1536 + QL]

        mt = [0]

        def moe(n):
            mt[0] += n
            return w2[:, mt[0] - n:mt[0]]

        h2p = moe(NT * D).rearrange("p (j d) -> p j d", j=NT)
        hTu = moe(KT * UNIT).rearrange("p (k n) -> p k n", k=KT)
        yT = moe(KT * 2 * UNIT).rearrange("p (k n) -> p k n", k=KT)
        ysb = moe(D)
        SGT = moe(T)
        S = moe(NT * UNIT).rearrange("p (j n) -> p j n", j=NT)
        SG = moe(NT * 2 * UNIT).rearrange("p (j n) -> p j n", j=NT)
        sil = moe(FT * UNIT)
        mid = moe(FT * UNIT).rearrange("p (k n) -> p k n", k=FT)
        R = moe(NT * E).rearrange("p (j e) -> p j e", j=NT)
        G = moe(NT * E).rearrange("p (j e) -> p j e", j=NT)
        Rc = moe(NT)
        Gc = moe(NT)
        sel = moe(NT * E).rearrange("p (j e) -> p j e", j=NT)
        shmid = moe(FT * T).rearrange("p (k t) -> p k t", k=FT)
        rbias = moe(E)
        assert mt[0] <= 6912
        shsil = temp[:, 1536:2048]

        def rt(i, n=NT * E):
            return temp[:, i:i + n]

        score = rt(0).rearrange("p (j e) -> p j e", j=NT)
        choice = rt(128).rearrange("p (j e) -> p j e", j=NT)
        top2 = rt(256)
        gs = rt(384, NT * NG).rearrange("p (j g) -> p j g", j=NT)
        grank = rt(400, NT * NG).rearrange("p (j g) -> p j g", j=NT)
        cmp1 = rt(512).rearrange("p (j a b) -> p j a b", j=NT, a=NG)
        cmp2 = rt(640).rearrange("p (j a b) -> p j a b", j=NT, a=NG)
        masked = rt(768).rearrange("p (j e) -> p j e", j=NT)
        top8 = rt(896, NT * 8).rearrange("p (j e) -> p j e", j=NT)
        gsum = rt(912, NT)
        grec = rt(914, NT)
        kcnt = temp[0:1, 1024:1024 + E]
        kcum = temp[0:1, 1088:1088 + E]
        kodd = temp[0:1, 1152:1153].bitcast(I32)
        kcnt2 = temp[0:1, 1160:1160 + E]

        posi = small[:, 0:2].bitcast(I32)
        posf = small[:, 2:4]
        eps_ln = small[:, 4:5]
        eps_rms = small[:, 5:6]
        ccol = small[:, 8:16]
        bn = small[:, 16:40].rearrange("p (j s) -> p j s", j=NT)
        mv = small[:, 40:44].rearrange("p (j s) -> p j s", j=NT)
        std = small[:, 44:46]
        rstd = small[:, 46:48]
        nmr = small[:, 48:50]
        ssq = small[:, 50:54].rearrange("p (j s) -> p j s", j=NT)
        rms = small[:, 54:58].rearrange("p (j s) -> p j s", j=NT)
        mx = small[:, 60:72].rearrange("p (h s) -> p h s", h=H)
        nmx = small[:, 72:84].rearrange("p (h s) -> p h s", h=H)
        sm = small[:, 84:96].rearrange("p (h s) -> p h s", h=H)
        rsm = small[:, 96:108].rearrange("p (h s) -> p h s", h=H)
        ubase = small[0:1, 108:109]
        cs = sb("cs", NT * ROPE)
        cosv = cs[:, 0:NT * HALF].rearrange("p (j r) -> p j r", j=NT)
        sinv = cs[:, NT * HALF:].rearrange("p (j r) -> p j r", j=NT)
        c8 = temp[0:KT, 0:P]
        brow = temp[0:L * MOD, 128:256]
        bcol = temp[:, 256:256 + L * MOD]
        modT = temp[0:L * MOD, 384:512]
        ang = temp[:, 512:512 + NT * HALF].rearrange("p (j r) -> p j r", j=NT)
        turns = temp[:, 576:576 + NT * HALF].rearrange("p (j r) -> p j r", j=NT)
        red = temp[:, 640:640 + NT * HALF].rearrange("p (j r) -> p j r", j=NT)

        ps = ctx.enter_context(nc.psum_tensor("ps", [P, 8, 512], F32))
        acc3 = ps[:, 0:4, :].rearrange("p (j h) n -> p j h n", j=NT)
        B_G, B_F, B_Y, B_T = 4, 5, 6, 7

        names = """consts_in x_in c_in b_in pos_in eps_set cT_done ccol_ready bT_done bcol_ready ada_done
        ada_evac mod_ready modT_done modT_ready mod_written
        rope_ready layer_ready xT_done xT_ready win_in proj_done projA_ready projD_ready ssq_ready std_ready
        lat_ready krp_ready band_in tm_done tm_ready lat_done latT_ready krT_done krT_ready vec_in wpool_in pool_done
        pool_ready w2_in jobs_done jobsA_ready jobsD_ready qr_ready qrT_done qrT_ready scores_done s_ready
        exp_ready probs_ready pT_done PT_ready pv_done pv_ready wout_in mix_done rows1_in rows2_in ln_stats
        ln_std ln_coef ln_norm h2_ready h2T_done h2T_ready router_in rbias_in logits_done esc_ready sh_up_done
        shsil_ready shmid_ready sel_ready rank_done table_ready rg_ready
        sh_landed S_ready gath_done hT_ready gu_done sil_ready mid_ready SG_ready down_done yT_ready SGT_done SGT_ready
        T_done y0_ready y1_ready scat_done sh_free out_done ang_ready gc_ready rc_ready pro_link
        dve_link waits_passed dist_ready""".split()
        s = {n: sem(n) for n in names}
        ada_landed = [sem(f"ada_landed{i}") for i in range(ADA_SLOTS)]
        ada_used = [sem(f"ada_used{i}") for i in range(ADA_SLOTS)]
        w_landed = [sem(f"w_landed{i}") for i in range(RING)]
        w_free = [sem(f"w_free{i}") for i in range(RING)]

        def passed(eng):
            eng.sem_inc(s["waits_passed"], 1)

        def units(eng, e):
            begin = eng.value_load(utab[0:1, ds(e, 1)], min_val=0, max_val=MAXU)
            return begin, eng.value_load(utab[0:1, ds(e + 1, 1)], min_val=1, max_val=MAXU)

        block = ctx.enter_context(nc.Block())

        def start_counts(eng, units="", pairs="", ones=()):
            for n in units.split():
                eng.sem_inc(s[n], U0)
            for n in pairs.split():
                eng.sem_inc(s[n], U0 // 2)
            for one in ones:
                eng.sem_inc(one, 1)

        @block.sync
        def _(sp):
            sp.dma_start(c8, c.rearrange("b (k p) -> (b k) p", p=P)).then_inc(s["c_in"], 16)
            sp.dma_start(const[:, :], consts_dram).then_inc(s["consts_in"], 16)
            sp.dma_start(brow, b_ada.rearrange("l (m p) -> (l m) p", p=P)).then_inc(s["b_in"], 16)
            sp.dma_start(posi, positions.rearrange("b (j p) -> p (b j)", p=P)).then_inc(s["pos_in"], 16)
            sp.dma_start(x3, x.rearrange("b (j p) d -> p (b j) d", p=P)).then_inc(s["x_in"], 16)
            flat = w_ada.rearrange("l (k p) (h c n) -> l h p k c n", p=P, h=2, n=ADA_COLS)
            with sp.Fori(0, L) as la, sp.Fori(0, ADA_IT // L) as lh:
                for k in range(ADA_SLOTS):
                    sp.wait_ge(ada_used[k], la * (ADA_IT // L) + lh + 1)
                    src = flat[ds(la, 1), ds(lh, 1), :, :, k, :].rearrange("a h p k n -> p (a h k) n")
                    sp.dma_start(ada[k], src).then_inc(ada_landed[k], 16)
            sp.wait_ge(s["modT_ready"], 1)
            sp.dma_start(mod_dram, modT).then_inc(s["mod_written"], 16)
            sp.wait_ge(s["mod_written"], 16)

            def lay(w, l):
                return w[ds(l, 1)]

            def expert(slot, l, e):
                sp.dma_start(gate_w(slot), w_exp_gate[ds(l, 1), ds(e, 1)].rearrange("a b (p k) f -> p (a b k) f", k=KT)).then_inc(w_landed[slot], 16)
                sp.dma_start(up_w(slot), w_exp_up[ds(l, 1), ds(e, 1)].rearrange("a b (p k) f -> p (a b k) f", k=KT)).then_inc(w_landed[slot], 16)
                sp.dma_start(down_w(slot), w_exp_down[ds(l, 1), ds(e, 1)].rearrange("a b (k p) d -> p (a b k) d", p=P)).then_inc(w_landed[slot], 16)

            def row(dst, src, sm_):
                sp.dma_start(dst, src.to_broadcast([P, D])).then_inc(sm_, 16)

            with sp.Fori(0, L) as l:
                sp.wait_ge(s["mix_done"], l + 1)
                sp.dma_start(win3, lay(w_in, l).rearrange("a (k p) n -> p (a k) n", p=P)).then_inc(s["win_in"], 16)
                sp.wait_ge(s["layer_ready"], l + 1)
                sp.dma_start(colv[:, 0:3], lay(q_norm_g, l).rearrange("a (k p) -> p (a k)", p=P)).then_inc(s["vec_in"], 16)
                sp.dma_start(colv[:, 3:5], lay(kv_norm_g, l).rearrange("a (k p) -> p (a k)", p=P)).then_inc(s["vec_in"], 16)
                sp.dma_start(colv[:, 5:7], lay(pool_scale, l).rearrange("a (k p) -> p (a k)", p=P)).then_inc(s["vec_in"], 16)
                sp.dma_start(band_sb, band_dram).then_inc(s["band_in"], 16)
                sp.dma_start(uq3, lay(w_uq, l).rearrange("a (k p) n -> p (a k) n", p=P)).then_inc(s["w2_in"], 16)
                sp.dma_start(ukv3, lay(w_ukv, l).rearrange("a (k p) n -> p (a k) n", p=P)).then_inc(s["w2_in"], 16)
                for g in range(2):
                    sp.dma_start(wpool3[:, g, :], w_pool[ds(l, 1), 2 * g:2 * g + 2].rearrange("a g c d -> (a g c) d")).then_inc(s["wpool_in"], 16)
                sp.dma_start(router3, lay(w_router, l).rearrange("a (p k) e -> p (a k) e", k=KT)).then_inc(s["router_in"], 16)
                for k, m in ((0, 2), (3, 4), (4, 3)):
                    row(rows[:, k * D:(k + 1) * D], mod_dram[ds(l * MOD + m * KT, KT)].rearrange("k p -> (k p)").unsqueeze(0), s["rows1_in"])
                row(lng_row, lay(ln1_g, l), s["rows1_in"])
                row(lnb_row, lay(ln1_b, l), s["rows1_in"])
                for k in range(2):
                    sp.wait_ge(w_free[k], l * (E // RING) + 1)
                    expert(k, l, k)
                sp.wait_ge(s["proj_done"], l + 1)
                sp.dma_start(wout3, lay(w_out, l).rearrange("a (k p) n -> p (a k) n", p=P)).then_inc(s["wout_in"], 16)
                sp.wait_ge(s["pv_ready"], (l + 1) * H)
                sp.wait_ge(w_free[2], l * (E // RING) + 1)
                expert(2, l, 2)
                sp.dma_start(gate_w(3), lay(w_sh_gate, l).rearrange("a (p k) f -> p (a k) f", k=KT)).then_inc(s["sh_landed"], 16)
                sp.dma_start(up_w(3), lay(w_sh_up, l).rearrange("a (p k) f -> p (a k) f", k=KT)).then_inc(s["sh_landed"], 16)
                sp.dma_start(down_w(3), lay(w_sh_down, l).rearrange("a (k p) d -> p (a k) d", p=P)).then_inc(s["sh_landed"], 16)
                sp.dma_start(rbias, lay(router_bias, l).to_broadcast([P, E])).then_inc(s["rbias_in"], 16)
                sp.wait_ge(s["h2_ready"], (l + 1) * NT)
                row(g_row, mod_dram[ds(l * MOD + 5 * KT, KT)].rearrange("k p -> (k p)").unsqueeze(0), s["rows2_in"])
                row(lng_row, lay(ln2_g, l), s["rows2_in"])
                row(lnb_row, lay(ln2_b, l), s["rows2_in"])
                sp.wait_ge(s["sh_free"], l + 1)
                expert(3, l, 3)
                with sp.Fori(1, E // RING) as i:
                    for k in range(RING):
                        sp.wait_ge(w_free[k], l * (E // RING) + i + 1)
                        expert(k, l, i * RING + k)
            sp.wait_ge(s["layer_ready"], L + 1)
            sp.dma_start(out.rearrange("b (j p) d -> p (b j) d", p=P), x3).then_inc(s["out_done"], 16)
            sp.wait_ge(s["out_done"], 16)

        @block.tensor
        def _(pe):
            mm = nc.tensor.matmul
            start_counts(pe, "gath_done gu_done down_done T_done", "SGT_done scat_done", [s["mix_done"], *ada_used])
            tr = nc.tensor.transpose

            pe.wait_ge(s["consts_in"], 16)
            pe.wait_ge(s["c_in"], 16)
            tr(ps[:, 4, 0:KT], c8, ident[0:KT, 0:KT]).then_inc(s["cT_done"], 1)
            pe.wait_ge(s["b_in"], 16)
            tr(ps[:, 5, 0:L * MOD], brow, ident[0:L * MOD, 0:L * MOD]).then_inc(s["bT_done"], 1)
            pe.wait_ge(s["ccol_ready"], 1)
            with pe.Fori(0, ADA_IT) as it:
                pe.wait_ge(s["ada_evac"], it + 1)
                for k in range(ADA_SLOTS):
                    pe.wait_ge(ada_landed[k], (it + 1) * 16)
                    for m in range(ADA_COLS // P):
                        for kt in range(KT):
                            last = mm(ps[:, 6, k * 4 + m:k * 4 + m + 1], ada[k][:, kt, m * P:(m + 1) * P],
                                      ccol[:, kt:kt + 1], start=kt == 0, stop=kt == KT - 1)
                    last.then_inc(ada_used[k], 1)
            pe.wait_ge(s["mod_ready"], 1)
            tr(ps[0:L * MOD, 7, 0:P], modc[:, :], ident).then_inc(s["modT_done"], 1)
            pe.wait_ge(s["modT_ready"], 1)

            with pe.Fori(0, L) as l:
                pe.wait_ge(s["layer_ready"], l + 1)
                for kt in range(KT):
                    for j in range(NT):
                        last = tr(ps[:, 4 + kt // 2, (kt % 2) * T + j * P:(kt % 2) * T + (j + 1) * P],
                                  x3[:, j, kt * P:(kt + 1) * P], ident)
                    if kt % 2:
                        last.then_inc(s["xT_done"], 1)
                pe.wait_ge(s["win_in"], (l + 1) * 16)
                for kt in range(KT):
                    pe.wait_ge(s["xT_ready"], l * KT + kt + 1)
                    for j in range(NT):
                        for half in range(2):
                            last = mm(ps[:, 2 * j + half, 0:HW], xT3[:, kt, j * P:(j + 1) * P],
                                      win3[:, kt, half * HW:(half + 1) * HW], start=kt == 0, stop=kt == KT - 1)
                last.then_inc(s["proj_done"], 1)
                pe.wait_ge(s["projA_ready"], l + 1)
                pe.wait_ge(s["projD_ready"], l + 1)
                pe.wait_ge(s["band_in"], (l + 1) * 16)
                for g in range(2):
                    for i in range(2):
                        o = ps[i * 64:(i + 1) * 64, 4, :]
                        u = 2 * g + i
                        mm(o[:, g * T:(g + 1) * T], proj3[:, 0, u * 64:(u + 1) * 64], band0[:, u, :], start=True, stop=False)
                        last = mm(o[:, g * T + P:(g + 1) * T], proj3[:, 1, u * 64:(u + 1) * 64], band1[:, u, :], start=False, stop=True)
                last.then_inc(s["tm_done"], 1)
                pe.wait_ge(s["lat_ready"], l + 1)
                for i in range(5):
                    for j in range(NT):
                        last = tr(ps[:, 5 + i // 2, (i % 2) * T + j * P:(i % 2) * T + (j + 1) * P],
                                  proj3[:, j, POOL + i * P:POOL + (i + 1) * P], ident)
                last.then_inc(s["lat_done"], 1)
                pe.wait_ge(s["krp_ready"], l + 1)
                for v in range(2):
                    for j in range(NT):
                        last = tr(ps[:, 0, v * T + j * P:v * T + (j + 1) * P], krp[:, j, v, :], ident)
                last.then_inc(s["krT_done"], 1)
                pe.wait_ge(s["tm_ready"], l + 1)
                pe.wait_ge(s["wpool_in"], (l + 1) * 32)
                passed(pe)
                for g in range(2):
                    for i in range(2):
                        q = slice(i * 64, (i + 1) * 64)
                        last = mm(ps[q, 1, g * T:(g + 1) * T], wpool3[q, g, :], tmT3[q, g, :], start=True, stop=True)
                last.then_inc(s["pool_done"], 1)
                pe.wait_ge(s["w2_in"], (l + 1) * 32)
                pe.wait_ge(s["latT_ready"], (l + 1) * 5)

                def job_bank(n):
                    if n in (6, 7):
                        pe.wait_ge(s["jobsD_ready"], l * 2 + n - 5)
                    elif n >= 8:
                        pe.wait_ge(s["jobsA_ready"], l * 10 + n - 7)
                    return ps[:, 2 + n % 6, :]

                for j in range(NT):
                    o = job_bank(j)[:, 0:H * ROPE].rearrange("p (h r) -> p h r", h=H)
                    for kt in range(3):
                        w = uq3[:, kt, :].rearrange("p (h n) -> p h n", h=H)[:, :, NOPE:QW]
                        last = mm(o, latT3[:, kt, j * P:(j + 1) * P], w, start=kt == 0, stop=kt == 2)
                    last.then_inc(s["jobs_done"], 1)
                n = 2
                for hp in range(H // 2):
                    o = job_bank(n)
                    for i in range(2):
                        h = 2 * hp + i
                        for kt in range(3):
                            last = mm(o[:, i * T:(i + 1) * T], uq3[:, kt, h * QW:h * QW + NOPE], latT3[:, kt, :],
                                      start=kt == 0, stop=kt == 2)
                    last.then_inc(s["jobs_done"], 1)
                    n += 1
                for hp in range(H // 2):
                    o = job_bank(n)
                    for i in range(2):
                        h = 2 * hp + i
                        for kt in range(2):
                            last = mm(o[:, i * T:(i + 1) * T], ukv3[:, kt, h * 256:h * 256 + NOPE], latT3[:, 3 + kt, :],
                                      start=kt == 0, stop=kt == 1)
                    last.then_inc(s["jobs_done"], 1)
                    n += 1
                for j in range(NT):
                    for hh in range(2):
                        o = job_bank(n)[:, 0:3 * VH].rearrange("p (h n) -> p h n", h=3)
                        for kt in range(2):
                            w = ukv3[:, kt, :].rearrange("p (h n) -> p h n", h=H)[:, 3 * hh:3 * hh + 3, NOPE:256]
                            last = mm(o, latT3[:, 3 + kt, j * P:(j + 1) * P], w, start=kt == 0, stop=kt == 1)
                        last.then_inc(s["jobs_done"], 1)
                        n += 1
                pe.wait_ge(s["qr_ready"], (l + 1) * NT)
                pe.wait_ge(s["krT_ready"], l + 1)
                pe.wait_ge(s["pool_ready"], l + 1)
                for i in range(3):
                    for j in range(NT):
                        last = tr(ps[:, i // 2, (i % 2) * T + j * P:(i % 2) * T + (j + 1) * P],
                                  qr3[:, j, i * P:(i + 1) * P], ident)
                last.then_inc(s["qrT_done"], 1)
                pe.wait_ge(s["jobsA_ready"], (l + 1) * 10)
                pe.wait_ge(s["qrT_ready"], l + 1)
                for h in range(H):
                    for j in range(NT):
                        o = ps[:, h, j * P:j * P + (j + 1) * P]
                        mm(o, qT3[:, h, j * P:(j + 1) * P], kT3[:, h, 0:(j + 1) * P], start=True, stop=False)
                        last = mm(o, qrT3[:, h // 2, j * P:(j + 1) * P], krT3[:, h % 2, 0:(j + 1) * P], start=False, stop=True)
                    last.then_inc(s["scores_done"], 1)

                def turn_probs(h):
                    pe.wait_ge(s["probs_ready"], l * H + h + 1)
                    if h >= 2:
                        pe.wait_ge(s["PT_ready"], l * H + h - 1)
                    for i in range(3):
                        last = tr(ps[:, 6 + h % 2, i * P:(i + 1) * P], sP[:, h % 2, i * P:(i + 1) * P], ident)
                    last.then_inc(s["pT_done"], 1)

                turn_probs(0)
                for h in range(H):
                    if h + 1 < H:
                        turn_probs(h + 1)
                    pe.wait_ge(s["PT_ready"], l * H + h + 1)
                    v = [v3[:, j, h * VH:(h + 1) * VH] for j in range(NT)]
                    mm(ps[:, h, 0:P], v[0], PT[:, h % 2, 0:P], start=True, stop=True)
                    mm(ps[:, h, P:2 * P], v[0], PT[:, h % 2, P:2 * P], start=True, stop=False)
                    mm(ps[:, h, P:2 * P], v[1], PT[:, h % 2, 2 * P:3 * P], start=False, stop=True).then_inc(s["pv_done"], 1)
                pe.wait_ge(s["wout_in"], (l + 1) * 16)
                pe.wait_ge(s["pv_ready"], (l + 1) * H)
                for kt in range(KT):
                    for j in range(NT):
                        for half in range(2):
                            last = mm(acc3[:, j, half, :], xT3[:, kt, j * P:(j + 1) * P],
                                      wout3[:, kt, half * 512:(half + 1) * 512], start=kt == 0, stop=kt == KT - 1)
                last.then_inc(s["mix_done"], 1)
                pe.wait_ge(s["h2_ready"], (l + 1) * NT)
                for kt in range(KT):
                    for j in range(NT):
                        last = tr(ps[:, 4 + kt // 2, (kt % 2) * T + j * P:(kt % 2) * T + (j + 1) * P],
                                  h2p[:, j, kt * P:(kt + 1) * P], ident)
                    if kt % 2:
                        last.then_inc(s["h2T_done"], 1)
                pe.wait_ge(s["h2T_ready"], (l + 1) * 4)
                pe.wait_ge(s["router_in"], (l + 1) * 16)
                for j in range(NT):
                    for kt in range(KT):
                        last = mm(ps[:, 4, j * E:(j + 1) * E], xT3[:, kt, j * P:(j + 1) * P], router3[:, kt, :],
                                  start=kt == 0, stop=kt == KT - 1)
                last.then_inc(s["logits_done"], 1)
                pe.wait_ge(s["sh_landed"], (l + 1) * 48)
                for w, b in ((gate_w(3), B_F), (up_w(3), B_Y)):
                    for f in range(FT):
                        for kt in range(KT):
                            last = mm(ps[:, b, f * T:(f + 1) * T], w[:, kt, f * P:(f + 1) * P], xT3[:, kt, :],
                                      start=kt == 0, stop=kt == KT - 1)
                last.then_inc(s["sh_up_done"], 1)
                pe.wait_ge(s["sel_ready"], l + 1)
                mm(ps[:, B_T, 0:E], upper, sel[:, 0, :], start=True, stop=True)
                mm(ps[:, B_T, E:2 * E], ones, sel[:, 0, :], start=True, stop=False)
                mm(ps[:, B_T, E:2 * E], upper, sel[:, 1, :], start=False, stop=True)
                mm(ps[0:1, B_T, 2 * E:3 * E], ones[:, 0:1], sel[:, 0, :], start=True, stop=False)
                mm(ps[0:1, B_T, 2 * E:3 * E], ones[:, 0:1], sel[:, 1, :], start=False, stop=True).then_inc(s["rank_done"], 1)
                pe.wait_ge(s["shmid_ready"], l + 1)
                for f in range(FT):
                    for j in range(NT):
                        for half in range(2):
                            last = mm(acc3[:, j, half, :], shmid[:, f, j * P:(j + 1) * P],
                                      down_w(3)[:, f, half * 512:(half + 1) * 512], start=f == 0, stop=f == FT - 1)
                last.then_inc(s["sh_free"], 1)

                def gather(count):
                    pe.wait_ge(s["S_ready"], count)
                    for kt in range(KT):
                        for j in range(NT):
                            last = mm(ps[:, B_G, kt * UNIT:(kt + 1) * UNIT], h2p[:, j, kt * P:(kt + 1) * P], S[:, j, :],
                                      start=j == 0, stop=j == NT - 1)
                    last.then_inc(s["gath_done"], 1)

                pe.wait_ge(s["table_ready"], l + 1)
                pe.wait_ge(s["esc_ready"], l + 1)
                passed(pe)
                gather(pe.value_load(utab[0:1, 0:1], min_val=0, max_val=MAXU) + l + 1)
                with pe.Fori(0, E // RING) as i:
                    for k in range(RING):
                        begin, end = units(pe, i * RING + k)
                        pe.wait_ge(w_landed[k], (l * (E // RING) + i + 1) * 48)
                        passed(pe)
                        with pe.Fori(begin, end) as u:
                            pe.wait_ge(s["hT_ready"], u + l + 1)
                            pe.wait_ge(s["mid_ready"], u)
                            pe.wait_ge(s["y1_ready"], u >> 1)
                            for f in range(FT):
                                for q, w in enumerate((gate_w(k), up_w(k))):
                                    c0 = (q * FT + f) * UNIT
                                    for kt in range(KT):
                                        last = mm(ps[:, B_F, c0:c0 + UNIT], w[:, kt, f * P:(f + 1) * P], hTu[:, kt, :],
                                                  start=kt == 0, stop=kt == KT - 1)
                            last.then_inc(s["gu_done"], 1)
                            with pe.If((u & 1) == 1):
                                pe.wait_ge(s["SG_ready"], u + 1)
                                pe.wait_ge(s["y0_ready"], u >> 1)
                                for j in range(NT):
                                    last = tr(ps[:, B_T, j * P:(j + 1) * P], SG[:, j, :], ident)
                                last.then_inc(s["SGT_done"], 1)
                            gather(u + l + 2)
                            pe.wait_ge(s["mid_ready"], u + 1)
                            pe.wait_ge(s["yT_ready"], u)
                            for m in range(KT):
                                for f in range(FT):
                                    last = mm(ps[:, B_Y, m * UNIT:(m + 1) * UNIT], down_w(k)[:, f, m * P:(m + 1) * P],
                                              mid[:, f, :], start=f == 0, stop=f == FT - 1)
                            last.then_inc(s["down_done"], 1)
                            with pe.If((u & 1) == 1):
                                pe.wait_ge(s["yT_ready"], u + 1)
                                pe.wait_ge(s["SGT_ready"], (u >> 1) + 1)
                                for half, b in ((0, B_T), (1, B_F)):
                                    for m in range(4):
                                        last = tr(ps[:, b, m * P:(m + 1) * P], yT[:, half * 4 + m, :], ident)
                                    last.then_inc(s["T_done"], 1)
                                for half in range(2):
                                    pe.wait_ge(s[f"y{half}_ready"], (u >> 1) + 1)
                                    for j in range(NT):
                                        last = mm(acc3[:, j, half, :], SGT[:, j * P:(j + 1) * P],
                                                  ysb[:, half * 512:(half + 1) * 512], start=False, stop=True,
                                                  skip_group_check=True)
                                last.then_inc(s["scat_done"], 1)

        @block.scalar
        def _(act):
            fn = nc.scalar.activation
            start_counts(act, "hT_ready sil_ready yT_ready", "y1_ready", w_free)
            act.wait_ge(s["cT_done"], 1)
            fn(ccol, ps[:, 4, 0:KT], ACT.Silu).then_inc(s["ccol_ready"], 1)
            act.wait_ge(s["ang_ready"], 1)
            fn(sinv, ang, ACT.Sin)
            fn(cosv, red, ACT.Sin).then_inc(s["rope_ready"], 1)

            with act.Fori(0, L) as l:
                act.wait_ge(s["layer_ready"], l + 1)
                for kt in range(KT):
                    act.wait_ge(s["xT_done"], l * (KT // 2) + kt // 2 + 1)
                    fn(xT3[:, kt, :], ps[:, 4 + kt // 2, (kt % 2) * T:(kt % 2 + 1) * T], ACT.Identity,
                       scale=modl[:, KT + kt:KT + kt + 1], bias=modl[:, kt:kt + 1]).then_inc(s["xT_ready"], 1)
                act.wait_ge(s["proj_done"], l + 1)
                fn(proj3[:, 0, :].rearrange("p (b n) -> p b n", b=2), ps[:, 0:2, 0:HW], ACT.Copy).then_inc(s["projA_ready"], 1)
                act.wait_ge(s["projA_ready"], l + 1)
                act.wait_ge(s["projD_ready"], l + 1)
                for j in range(NT):
                    fn(junk, proj3[:, j, POOL:POOL + QL], ACT.Square, accum_out=ssq[:, j, 0:1]).then_inc(s["ssq_ready"], 1)
                    act.wait_ge(s["ssq_ready"], l * 4 + 2 * j + 1)
                    fn(junk[:, 0:KVL], proj3[:, j, POOL + QL:POOL + QL + KVL], ACT.Square, accum_out=ssq[:, j, 1:2]).then_inc(s["ssq_ready"], 1)
                    act.wait_ge(s["ssq_ready"], l * 4 + 2 * j + 2)
                fn(rms[:, :, 0], ssq[:, :, 0], ACT.Sqrt, scale=1.0 / QL, bias=eps_rms)
                fn(rms[:, :, 1], ssq[:, :, 1], ACT.Sqrt, scale=1.0 / KVL, bias=eps_rms).then_inc(s["std_ready"], 1)
                act.wait_ge(s["lat_done"], l + 1)
                act.wait_ge(s["vec_in"], (l + 1) * 48)
                for k in range(5):
                    fn(latT3[:, k, :], ps[:, 5 + k // 2, (k % 2) * T:(k % 2 + 1) * T], ACT.Copy,
                       scale=colv[:, k:k + 1]).then_inc(s["latT_ready"], 1)
                act.wait_ge(s["krT_done"], l + 1)
                fn(krT3, ps[:, 0, :].rearrange("p (v t) -> p v t", v=2), ACT.Copy).then_inc(s["krT_ready"], 1)
                for n in range(2, 12):
                    act.wait_ge(s["jobs_done"], l * 12 + n + 1)
                    b = ps[:, 2 + n % 6, :]
                    if n < 5:
                        dst, src = qT3[:, 2 * (n - 2):2 * (n - 2) + 2, :], b.rearrange("p (h t) -> p h t", h=2)
                    elif n < 8:
                        dst, src = kT3[:, 2 * (n - 5):2 * (n - 5) + 2, :], b.rearrange("p (h t) -> p h t", h=2)
                    else:
                        j, hh = divmod(n - 8, 2)
                        dst, src = v3[:, j, hh * 3 * VH:(hh + 1) * 3 * VH], b[:, 0:3 * VH]
                    fn(dst, src, ACT.Copy).then_inc(s["jobsA_ready"], 1)
                act.wait_ge(s["qrT_done"], l + 1)
                fn(qrT3.rearrange("p h t -> p (h t)"), ps[:, 0:2, :].rearrange("p b n -> p (b n)")[:, 0:3 * T], ACT.Copy).then_inc(s["qrT_ready"], 1)

                def exps(h):
                    act.wait_ge(s["s_ready"], l * H + h + 1)
                    fn(sP[:, h % 2, 0:P], sP[:, h % 2, 0:P], ACT.Exp, scale=SCALE, bias=nmx[:, h, 0:1], accum_out=sm[:, h, 0:1])
                    fn(sP[:, h % 2, P:3 * P], sP[:, h % 2, P:3 * P], ACT.Exp, scale=SCALE, bias=nmx[:, h, 1:2],
                       accum_out=sm[:, h, 1:2]).then_inc(s["exp_ready"], 1)

                def mixed(h):
                    act.wait_ge(s["pv_done"], l * H + h + 1)
                    fn(xT3[:, 2 + h, :], ps[:, h, 0:T], ACT.Copy).then_inc(s["pv_ready"], 1)

                exps(0)
                for h in range(H):
                    if h + 1 < H:
                        exps(h + 1)
                    act.wait_ge(s["pT_done"], l * H + h + 1)
                    if h >= 2:
                        act.wait_ge(s["pv_done"], l * H + h - 1)
                    fn(PT[:, h % 2, :], ps[:, 6 + h % 2, 0:3 * P], ACT.Copy).then_inc(s["PT_ready"], 1)
                    if h >= 1:
                        mixed(h - 1)
                mixed(H - 1)

                def norm(which):
                    act.wait_ge(s["ln_stats"], 2 * l + which + 1)
                    fn(std, mv[:, :, 1], ACT.Sqrt, bias=eps_ln).then_inc(s["ln_std"], 1)
                    act.wait_ge(s["ln_coef"], 2 * l + which + 1)
                    for j in range(NT):
                        fn(t3[:, j, :], t3[:, j, :], ACT.Identity, scale=rstd[:, j:j + 1], bias=nmr[:, j:j + 1]).then_inc(s["ln_norm"], 1)

                norm(0)
                for b in range(4):
                    act.wait_ge(s["h2T_done"], l * 4 + b + 1)
                    fn(xT3[:, 2 * b:2 * b + 2, :], ps[:, 4 + b, :].rearrange("p (k t) -> p k t", k=2), ACT.Copy).then_inc(s["h2T_ready"], 1)
                act.wait_ge(s["logits_done"], l + 1)
                fn(score.rearrange("p j e -> p (j e)"), ps[:, 4, 0:NT * E], ACT.Exp, scale=-1.0).then_inc(s["esc_ready"], 1)
                act.wait_ge(s["sh_up_done"], l + 1)
                fn(shsil, ps[:, B_F, :], ACT.Silu).then_inc(s["shsil_ready"], 1)

                def gathered(count):
                    act.wait_ge(s["gath_done"], count)
                    fn(hTu.rearrange("p k n -> p (k n)"), ps[:, B_G, :], ACT.Copy).then_inc(s["hT_ready"], 1)

                act.wait_ge(s["table_ready"], l + 1)
                passed(act)
                gathered(act.value_load(utab[0:1, 0:1], min_val=0, max_val=MAXU) + l + 1)
                with act.Fori(0, E // RING) as i:
                    for k in range(RING):
                        begin, end = units(act, i * RING + k)
                        with act.Fori(begin, end) as u:
                            act.wait_ge(s["gu_done"], u + 1)
                            act.wait_ge(s["mid_ready"], u)
                            fn(sil, ps[:, B_F, 0:FT * UNIT], ACT.Silu).then_inc(s["sil_ready"], 1)
                            gathered(u + l + 2)
                            act.wait_ge(s["down_done"], u + 1)
                            act.wait_ge(s["T_done"], (u >> 1) * 2)
                            fn(yT[:, :, ds((u & 1) * UNIT, UNIT)], ps[:, B_Y, :].rearrange("p (k n) -> p k n", k=KT),
                               ACT.Copy).then_inc(s["yT_ready"], 1)
                            with act.If((u & 1) == 1):
                                act.wait_ge(s["T_done"], u + 1)
                                act.wait_ge(s["scat_done"], u >> 1)
                                fn(ysb[:, 512:D], ps[:, B_F, :], ACT.Copy).then_inc(s["y1_ready"], 1)
                        act.sem_inc(w_free[k], 1)
                norm(1)

        @block.gpsimd
        def _(pool):
            eng = nc.gpsimd
            start_counts(pool, "S_ready SG_ready rc_ready dist_ready")
            eng.memset(eps_ln, LN_EPS)
            eng.memset(eps_rms, RMS_EPS).then_inc(s["eps_set"], 1)
            iota = const[:, C_IOTA:C_IOTA + UNIT].unsqueeze(1).to_broadcast([P, NT, UNIT])
            pool.wait_ge(s["consts_in"], 16)
            with pool.Fori(0, L) as l:
                def one_hot(count):
                    eng.tensor_tensor(S, iota, Rc.unsqueeze(2).to_broadcast([P, NT, UNIT]), ALU.subtract).then_inc(s["dist_ready"], 1)
                    pool.wait_ge(s["dist_ready"], count)
                    passed(pool)
                    return eng.tensor_scalar(S, S, 0.0, None, ALU.is_equal)

                pool.wait_ge(s["table_ready"], l + 1)
                passed(pool)
                with pool.Fori(0, E) as e:
                    begin, end = units(pool, e)
                    pool.wait_ge(s["SG_ready"], begin)
                    pool.wait_ge(s["rc_ready"], l * E + e + begin)
                    passed(pool)
                    eng.tensor_copy(Gc.unsqueeze(2), G[:, :, ds(e, 1)]).then_inc(s["gc_ready"], 1)
                    eng.tensor_copy(Rc.unsqueeze(2), R[:, :, ds(e, 1)]).then_inc(s["rc_ready"], 1)
                    pool.wait_ge(s["gc_ready"], l * E + e + 1)
                    passed(pool)
                    with pool.Fori(begin, end) as u:
                        pool.wait_ge(s["rc_ready"], l * E + e + 1 + u)
                        pool.wait_ge(s["gath_done"], u + l)
                        one_hot(u + l + 1).then_inc(s["S_ready"], 1)
                        pool.wait_ge(s["S_ready"], u + l + 1)
                        pool.wait_ge(s["SGT_done"], u >> 1)
                        eng.tensor_tensor(SG[:, :, ds((u & 1) * UNIT, UNIT)], S, Gc.unsqueeze(2).to_broadcast([P, NT, UNIT]),
                                          ALU.mult).then_inc(s["SG_ready"], 1)
                        eng.tensor_scalar(Rc, Rc, -float(UNIT), None, ALU.add).then_inc(s["rc_ready"], 1)
                last = pool.value_load(utab[0:1, E:E + 1], min_val=1, max_val=MAXU)
                pool.wait_ge(s["rc_ready"], (l + 1) * E + last)
                pool.wait_ge(s["gath_done"], last + l)
                one_hot(last + l + 1).then_inc(s["S_ready"], 1)

        @block.vector
        def _(dve):
            v = nc.vector
            links = [0, 0]
            start_counts(dve, "mid_ready", "SGT_ready y0_ready", [s["ada_evac"]])

            def plink(ins):
                links[0] += 1
                ins.then_inc(s["pro_link"], 1)
                dve.wait_ge(s["pro_link"], links[0])

            plink(v.memset(ubase, float(U0)))
            dve.wait_ge(s["bT_done"], 1)
            plink(v.tensor_copy(bcol, ps[:, 5, 0:L * MOD]))
            dve.wait_ge(s["pos_in"], 16)
            dve.wait_ge(s["consts_in"], 16)
            plink(v.tensor_copy(posf, posi))
            for j in range(NT):
                ins = v.tensor_scalar(ang[:, j, :], freq, posf[:, j:j + 1], None, ALU.mult)
            plink(ins)

            def reduce_angle(dst, quarter):
                plink(v.tensor_scalar(turns, ang, 0.15915494309189535, 0.25 * quarter, ALU.mult, ALU.add))
                plink(v.tensor_scalar(turns, turns, MAGIC, None, ALU.add))
                plink(v.tensor_scalar(turns, turns, -MAGIC, None, ALU.add))
                src = ang
                for part in TWO_PI_PARTS:
                    plink(v.scalar_tensor_tensor(dst, turns, -part, src, ALU.mult, ALU.add))
                    src = dst
                if quarter:
                    plink(v.tensor_scalar(dst, dst, 1.5707963267948966, None, ALU.add))
                return v.tensor_scalar(dst, dst, 3.1415925, -3.1415925, ALU.min, ALU.max)

            plink(reduce_angle(red, 1))
            reduce_angle(ang, 0).then_inc(s["ang_ready"], 1)
            with dve.Fori(0, ADA_IT) as it:
                n = ADA_SLOTS * ADA_COLS // P
                for k in range(ADA_SLOTS):
                    dve.wait_ge(ada_used[k], it + 2)
                v.tensor_tensor(modc[:, ds(it * n, n)], ps[:, 6, 0:n], bcol[:, ds(it * n, n)], ALU.add).then_inc(s["ada_evac"], 1)
            dve.wait_ge(s["ada_evac"], ADA_IT + 1)
            m3 = modc[:, :].rearrange("p (l m) -> p l m", l=L)
            v.tensor_scalar(m3[:, :, KT:2 * KT], m3[:, :, KT:2 * KT], 1.0, None, ALU.add)
            plink(v.tensor_scalar(m3[:, :, 4 * KT:5 * KT], m3[:, :, 4 * KT:5 * KT], 1.0, None, ALU.add))
            v.tensor_copy(modl[:, :], modc[:, 0:MOD]).then_inc(s["mod_ready"], 1)
            dve.wait_ge(s["modT_done"], 1)
            v.tensor_copy(modT, ps[0:L * MOD, 7, 0:P]).then_inc(s["modT_ready"], 1)
            dve.wait_ge(s["rope_ready"], 1)
            dve.wait_ge(s["eps_set"], 1)
            dve.wait_ge(s["mod_written"], 16)
            dve.wait_ge(s["x_in"], 16)

            with dve.Fori(0, L) as l:
                def link(ins, own=False):
                    links[1] += 1
                    ins.then_inc(s["dve_link"], 1)
                    dve.wait_ge(s["dve_link"], l * DVE_LINKS + links[1])
                    if own:
                        passed(dve)

                v.tensor_copy(modl[:, :], modc[:, ds(l * MOD, MOD)]).then_inc(s["layer_ready"], 1)
                dve.wait_ge(s["proj_done"], l + 1)
                v.tensor_copy(proj3[:, 1, :].rearrange("p (b n) -> p b n", b=2), ps[:, 2:4, 0:HW]).then_inc(s["projD_ready"], 1)
                dve.wait_ge(s["std_ready"], l + 1)
                link(v.reciprocal(ssq, rms))
                for j in range(NT):
                    for a, n, k in ((POOL, QL, 0), (POOL + QL, KVL, 1)):
                        ins = v.tensor_scalar(proj3[:, j, a:a + n], proj3[:, j, a:a + n], ssq[:, j, k:k + 1], None, ALU.mult)
                ins.then_inc(s["lat_ready"], 1)
                k1, k2 = proj3[:, :, INW - ROPE:INW - HALF], proj3[:, :, INW - HALF:INW]
                o1, o2 = krp[:, :, 0, 0:HALF], krp[:, :, 0, HALF:ROPE]
                v.memset(krp[:, :, 0, ROPE:P], 0.0)
                v.memset(krp[:, :, 1, 0:ROPE], 0.0)
                v.tensor_tensor(o1, k1, cosv, ALU.mult)
                v.tensor_tensor(o2, k2, cosv, ALU.mult)
                link(v.tensor_tensor(ktmp, k2, sinv, ALU.mult))
                link(v.tensor_tensor(o1, o1, ktmp, ALU.subtract))
                link(v.tensor_tensor(ktmp, k1, sinv, ALU.mult))
                link(v.tensor_tensor(o2, o2, ktmp, ALU.add))
                v.tensor_copy(krp[:, :, 1, ROPE:P], krp[:, :, 0, 0:ROPE]).then_inc(s["krp_ready"], 1)
                dve.wait_ge(s["tm_done"], l + 1)
                v.tensor_copy(tmT3, ps[:, 4, :].rearrange("p (g t) -> p g t", g=2)).then_inc(s["tm_ready"], 1)
                dve.wait_ge(s["pool_done"], l + 1)
                dve.wait_ge(s["vec_in"], (l + 1) * 48)
                for g in range(2):
                    ins = v.tensor_scalar(xT3[:, g, :], ps[:, 1, g * T:(g + 1) * T], colv[:, 5 + g:6 + g], None, ALU.mult)
                ins.then_inc(s["pool_ready"], 1)
                for j in range(NT):
                    dve.wait_ge(s["jobs_done"], l * 12 + j + 1)
                    b = ps[:, 2 + j, 0:H * ROPE].rearrange("p (h r) -> p h r", h=H)
                    q1, q2 = b[:, :, 0:HALF], b[:, :, HALF:ROPE]
                    o1, o2 = qr4[:, j, :, 0:HALF], qr4[:, j, :, HALF:ROPE]
                    co = cosv[:, j, :].unsqueeze(1).to_broadcast([P, H, HALF])
                    si = sinv[:, j, :].unsqueeze(1).to_broadcast([P, H, HALF])
                    v.tensor_tensor(o1, q1, co, ALU.mult)
                    v.tensor_tensor(o2, q2, co, ALU.mult)
                    link(v.tensor_tensor(rtmp[:, j], q2, si, ALU.mult))
                    link(v.tensor_tensor(o1, o1, rtmp[:, j], ALU.subtract))
                    v.tensor_tensor(rtmp[:, j], q1, si, ALU.mult).then_inc(s["jobsD_ready"], 1)
                    dve.wait_ge(s["jobsD_ready"], l * NT + j + 1)
                    v.tensor_tensor(o2, o2, rtmp[:, j], ALU.add).then_inc(s["qr_ready"], 1)
                dve.wait_ge(s["qrT_done"], l + 1)

                def scores(h):
                    dve.wait_ge(s["scores_done"], l * H + h + 1)
                    if h >= 2:
                        dve.wait_ge(s["pT_done"], l * H + h - 1)
                    link(v.tensor_tensor(sP[:, h % 2, :], ps[:, h, 0:3 * P], mask, ALU.add))
                    v.reduce_max(mx[:, h, 0:1], sP[:, h % 2, 0:P], AX_X)
                    link(v.reduce_max(mx[:, h, 1:2], sP[:, h % 2, P:3 * P], AX_X))
                    v.tensor_scalar(nmx[:, h, :], mx[:, h, :], -SCALE, None, ALU.mult).then_inc(s["s_ready"], 1)

                scores(0)
                for h in range(H):
                    if h + 1 < H:
                        scores(h + 1)
                    dve.wait_ge(s["exp_ready"], l * H + h + 1)
                    link(v.reciprocal(rsm[:, h, :], sm[:, h, :]))
                    v.tensor_scalar(sP[:, h % 2, 0:P], sP[:, h % 2, 0:P], rsm[:, h, 0:1], None, ALU.mult)
                    v.tensor_scalar(sP[:, h % 2, P:3 * P], sP[:, h % 2, P:3 * P], rsm[:, h, 1:2], None, ALU.mult).then_inc(s["probs_ready"], 1)

                def norm(which):
                    for j in range(NT):
                        link(v.tensor_tensor(t3[:, j, :], acc3[:, j].rearrange("p h n -> p (h n)"), g_row, ALU.mult))
                        link(v.scalar_tensor_tensor(t3[:, j, :], x3[:, j, :], ALPHA, t3[:, j, :], ALU.mult, ALU.add))
                        v.bn_stats(bn[:, j, 0:6], t3[:, j, 0:512])
                        link(v.bn_stats(bn[:, j, 6:12], t3[:, j, 512:D]), own=True)
                        ins = v.bn_aggr(mv[:, j, :], bn[:, j, :])
                    ins.then_inc(s["ln_stats"], 1)
                    dve.wait_ge(s["ln_std"], 2 * l + which + 1)
                    link(v.reciprocal(rstd, std))
                    v.scalar_tensor_tensor(nmr, mv[:, :, 0], -1.0, rstd, ALU.mult, ALU.mult).then_inc(s["ln_coef"], 1)
                    for j in range(NT):
                        dve.wait_ge(s["ln_norm"], (2 * l + which) * NT + j + 1)
                        link(v.tensor_tensor(x3[:, j, :], t3[:, j, :], lng_row, ALU.mult))
                        link(v.tensor_tensor(x3[:, j, :], x3[:, j, :], lnb_row, ALU.add))
                        if which == 0:
                            hv = h2p[:, j, :].rearrange("p (k q) -> p q k", k=KT)
                            xv = x3[:, j, :].rearrange("p (q k) -> p q k", k=KT)
                            link(v.tensor_tensor(hv, xv, sc_row.rearrange("p (q k) -> p q k", k=KT), ALU.mult))
                            v.tensor_tensor(hv, hv, sh_row.rearrange("p (q k) -> p q k", k=KT), ALU.add).then_inc(s["h2_ready"], 1)

                dve.wait_ge(s["mix_done"], l + 2)
                dve.wait_ge(s["rows1_in"], (l + 1) * 80)
                norm(0)

                dve.wait_ge(s["esc_ready"], l + 1)
                dve.wait_ge(s["rbias_in"], (l + 1) * 16)
                link(v.tensor_scalar(score, score, 1.0, None, ALU.add))
                link(v.reciprocal(score, score))
                link(v.tensor_tensor(choice, score, rbias.unsqueeze(1).to_broadcast([P, NT, E]), ALU.add), own=True)
                ch = choice.rearrange("p j (g n) -> p (j g) n", g=NG)
                t2 = top2.rearrange("p (g n) -> p g n", n=8)
                for k in range(NT * NG):
                    ins = v.max(t2[:, k, :], ch[:, k, :])
                link(ins)
                link(v.tensor_tensor(gs.rearrange("p j g -> p (j g)"), t2[:, :, 0], t2[:, :, 1], ALU.add))
                other = gs.unsqueeze(2).to_broadcast([P, NT, NG, NG])
                own = gs.unsqueeze(3).to_broadcast([P, NT, NG, NG])
                lower = const[:, C_LT:C_LT + NG * NG].rearrange("p (a b) -> p a b", a=NG)
                v.tensor_tensor(cmp1, other, own, ALU.is_gt)
                link(v.tensor_tensor(cmp2, other, own, ALU.is_equal))
                for j in range(NT):
                    ins = v.tensor_tensor(cmp2[:, j], cmp2[:, j], lower, ALU.mult)
                link(ins)
                link(v.tensor_tensor(cmp1, cmp1, cmp2, ALU.add))
                link(v.tensor_reduce(grank, cmp1, AX_X, ALU.add))
                link(v.tensor_scalar(grank, grank, TOPG - 0.5, None, ALU.is_lt))
                link(v.tensor_scalar(gs, grank, -NEG, NEG, ALU.mult, ALU.add))
                m4 = masked.rearrange("p j (g n) -> p (j g) n", g=NG)
                keep = grank.rearrange("p j g -> p (j g)").unsqueeze(2).to_broadcast([P, NT * NG, 8])
                drop = gs.rearrange("p j g -> p (j g)").unsqueeze(2).to_broadcast([P, NT * NG, 8])
                link(v.tensor_tensor(m4, ch, keep, ALU.mult))
                link(v.tensor_tensor(m4, m4, drop, ALU.add), own=True)
                for j in range(NT):
                    ins = v.max(top8[:, j, :], masked[:, j, :])
                link(ins, own=True)
                for j in range(NT):
                    ins = v.match_replace(sel[:, j, :], top8[:, j, :], masked[:, j, :], -3e38)
                link(ins)
                v.tensor_tensor(sel, sel, masked, ALU.not_equal).then_inc(s["sel_ready"], 1)
                dve.wait_ge(s["sel_ready"], l + 1)
                link(v.tensor_tensor(G, sel, score, ALU.mult))
                link(v.tensor_reduce(gsum, G, AX_X, ALU.add))
                link(v.reciprocal(grec, gsum))
                for j in range(NT):
                    v.tensor_scalar(G[:, j, :], G[:, j, :], grec[:, j:j + 1], ROUTED, ALU.mult, ALU.mult)
                dve.wait_ge(s["shsil_ready"], l + 1)
                v.tensor_tensor(shmid.rearrange("p k t -> p (k t)"), shsil, ps[:, B_Y, :], ALU.mult).then_inc(s["shmid_ready"], 1)
                dve.wait_ge(s["rank_done"], l + 1)
                rk = ps[:, B_T, 0:NT * E].rearrange("p (j e) -> p j e", j=NT)
                cnt = ps[0:1, B_T, NT * E:NT * E + E]
                link(v.scalar_tensor_tensor(R, rk, 1024.0, sel, ALU.add, ALU.mult))
                v.tensor_scalar(R, R, -1024.0, None, ALU.add)
                link(v.tensor_scalar(kcnt, cnt, UNIT + 0.5, 1.0, ALU.is_gt, ALU.add))
                for k in range(2, T // UNIT):
                    link(v.tensor_scalar(kcnt2, cnt, k * UNIT + 0.5, None, ALU.is_gt))
                    link(v.tensor_tensor(kcnt, kcnt, kcnt2, ALU.add))
                link(v.tensor_tensor_scan(kcum, ones[0:1, 0:E], kcnt, ubase, ALU.mult, ALU.add))
                v.tensor_copy(utab[0:1, 0:1], ubase)
                link(v.tensor_copy(utab[0:1, 1:E + 1], kcum))
                link(v.tensor_scalar(kodd, utab[0:1, E:E + 1], 1, None, ALU.bitwise_and))
                link(v.tensor_copy(kcnt[:, 0:1], kodd))
                link(v.tensor_tensor(kcum[:, E - 1:E], kcum[:, E - 1:E], kcnt[:, 0:1], ALU.add))
                link(v.tensor_copy(utab[0:1, E:E + 1], kcum[:, E - 1:E]))
                v.tensor_copy(ubase, utab[0:1, E:E + 1]).then_inc(s["table_ready"], 1)
                dve.wait_ge(s["table_ready"], l + 1)
                passed(dve)

                with dve.Fori(0, E) as e:
                    begin, end = units(dve, e)
                    with dve.Fori(begin, end) as u:
                        dve.wait_ge(s["sil_ready"], u + 1)
                        dve.wait_ge(s["down_done"], u)
                        v.tensor_tensor(mid.rearrange("p k n -> p (k n)"), sil, ps[:, B_F, FT * UNIT:2 * FT * UNIT],
                                        ALU.mult).then_inc(s["mid_ready"], 1)
                        with dve.If((u & 1) == 1):
                            dve.wait_ge(s["SGT_done"], (u >> 1) + 1)
                            dve.wait_ge(s["scat_done"], u >> 1)
                            v.tensor_copy(SGT, ps[:, B_T, 0:T]).then_inc(s["SGT_ready"], 1)
                            dve.wait_ge(s["T_done"], u)
                            v.tensor_copy(ysb[:, 0:512], ps[:, B_T, :]).then_inc(s["y0_ready"], 1)
                total = dve.value_load(utab[0:1, E:E + 1], min_val=1, max_val=MAXU)
                dve.wait_ge(s["scat_done"], total >> 1)
                dve.wait_ge(s["hT_ready"], total + l + 1)
                dve.wait_ge(s["rows2_in"], (l + 1) * 48)
                norm(1)
                link(v.tensor_copy(std, rstd))
            assert links[1] == DVE_LINKS, links
            dve.sem_inc(s["layer_ready"], 1)


_INS = ["x", "c", "positions", "w_ada", "b_ada", "w_in", "q_norm_g", "kv_norm_g", "w_uq", "w_ukv", "w_pool",
        "pool_scale", "w_out", "ln1_g", "ln1_b", "w_router", "router_bias", "w_exp_gate", "w_exp_up",
        "w_exp_down", "w_sh_gate", "w_sh_up", "w_sh_down", "ln2_g", "ln2_b"]


def kernel(**inputs):
    import concourse.bacc as _bacc
    from concourse.bass_utils import run_bass_kernel_spmd as _run

    nc = _bacc.Bacc("TRN2", target_bir_lowering=False, num_devices=1)
    arrays, args = {}, []
    consts, band = shape_constants()
    for name in _INS + ["consts", "band"]:
        a = np.ascontiguousarray({"consts": consts, "band": band}[name] if name in ("consts", "band") else inputs[name])
        arrays[f"in_{name}"] = a
        args.append(nc.dram_tensor(f"in_{name}", a.shape, mybir.dt.from_np(a.dtype), kind="ExternalInput").ap())
    out = nc.dram_tensor("out_x", (1, T, D), F32, kind="ExternalOutput").ap()
    decoder_trunk(nc, *args, out)
    r = _run(nc, [arrays], core_ids=[0])
    return r.results[0]["out_x"]
```

```python
from contextlib import ExitStack

import numpy as np

import concourse.bass as bass
from concourse import mybir

P = 128
F32 = mybir.dt.float32
I32 = mybir.dt.int32
ALU = mybir.AluOpType
ACT = mybir.ActivationFunctionType
AX_X = mybir.AxisListType.X

NT = 2
T = NT * P
D = 1024
KT = D // P
L = 2
WINDOWS = (2, 4, 8, 16)
POOL = 256
QL, KVL, ROPE, NOPE, VH = 384, 256, 64, 128, 128
HALF = ROPE // 2
H = 6
INW = POOL + QL + KVL + ROPE
HW = INW // 2
QW = NOPE + ROPE
E, NG, TOPG, TOPK = 64, 8, 4, 8
F = 256
FT = F // P
UNIT = 64
RING = 4
ALPHA = (2.0 * L) ** 0.25
LN_EPS, RMS_EPS = 1e-5, 1e-6
ROUTED = 2.5
SCALE = float(QW) ** -0.5
NEG = -1e30
ADA_W = 2048
ADA_PARTS = 6 * D // ADA_W
ADA_BUFS = 6
ADA_USES = ADA_PARTS * KT // ADA_BUFS
TWO_PI_PARTS = (6.28125, 0.0019350051879882812, 3.0199159819567396e-07)
MAGIC = 12582912.0
SLOT_W = 3 * KT * F
DVE_LINKS = 81
B0 = 1
MAXB = B0 + L * (E // 2) * (T // UNIT)

C_ID = 0
C_MASK = C_ID + P
C_UP = C_MASK + 3 * P
C_ONE = C_UP + P
C_IOTA = C_ONE + P
C_FREQ = C_IOTA + UNIT
C_LT = C_FREQ + HALF
C_N = C_LT + NG * NG


def shape_constants():
    c = np.zeros((P, C_N), np.float32)
    i = np.arange(P)
    c[:, C_ID:C_ID + P] = np.eye(P)
    causal = np.where(i[:, None] >= i[None, :], 0.0, NEG)
    c[:, C_MASK:C_MASK + P] = causal
    c[:, C_MASK + 2 * P:C_MASK + 3 * P] = causal
    c[:, C_UP:C_UP + P] = i[:, None] < i[None, :]
    c[:, C_ONE:C_ONE + P] = 1.0
    c[:, C_IOTA:C_IOTA + UNIT] = np.arange(UNIT)[None, :]
    c[:, C_FREQ:C_FREQ + HALF] = (10000.0 ** (-np.arange(HALF) / HALF)).astype(np.float32)[None, :]
    g = np.arange(NG)
    c[:, C_LT:] = (g[None, :] < g[:, None]).astype(np.float32).reshape(1, -1)
    t = np.arange(T)
    band = np.zeros((len(WINDOWS), T, T), np.float32)
    for k, w in enumerate(WINDOWS):
        inside = (t[:, None] <= t[None, :]) & (t[:, None] > t[None, :] - w)
        band[k] = inside / np.minimum(t + 1, w)[None, :] - np.eye(T)
    first = band[:, :P, :].transpose(1, 0, 2).reshape(P, -1)
    second = band[:, P:, P:].transpose(1, 0, 2).reshape(P, -1)
    return c, np.ascontiguousarray(np.concatenate([first, second], axis=1).astype(np.float32))


def decoder_trunk(nc, x, c, positions, w_ada, b_ada, w_in, q_norm_g, kv_norm_g, w_uq, w_ukv, w_pool,
                  pool_scale, w_out, ln1_g, ln1_b, w_router, router_bias, w_exp_gate, w_exp_up,
                  w_exp_down, w_sh_gate, w_sh_up, w_sh_down, ln2_g, ln2_b, consts_dram, band_dram, out):
    mod_dram = nc.dram_tensor("mod_rows", (L, 6 * D), F32, kind="Internal").ap()
    ds = bass.ds

    with ExitStack() as ctx:
        ctx.enter_context(nc.allow_non_contiguous_dma(reason="short vectors laid on partitions"))

        def sb(name, cols, dt=F32, rows=P):
            return ctx.enter_context(nc.sbuf_tensor(name, [rows, cols], dt))

        def sem(name):
            return ctx.enter_context(nc.semaphore(name))

        ring = sb("ring", RING * SLOT_W)
        w1 = sb("w1", KT * D)
        w2 = sb("w2", 6912)
        router_sb = sb("router_sb", KT * E)
        x_sb = sb("x_sb", NT * D)
        xT = sb("xT", KT * T)
        rows = sb("rows", 5 * D)
        temp = sb("temp", 2 * D)
        const = sb("const", C_N)
        modl = sb("modl", 2 * KT)
        c32 = sb("c32", KT * 32)
        small = sb("small", 160)
        colv = sb("colv", 8)
        btab = sb("btab", E // 2 + 1, I32, 1)

        x3 = x_sb[:, :].rearrange("p (j d) -> p j d", j=NT)
        xT3 = xT[:, :].rearrange("p (k t) -> p k t", k=KT)
        t3 = temp[:, :].rearrange("p (j d) -> p j d", j=NT)
        g_row, lng_row, lnb_row, sc_row, sh_row = (rows[:, i * D:(i + 1) * D] for i in range(5))
        win3 = w1[:, 0:KT * INW].rearrange("p (k n) -> p k n", k=KT)
        wout3 = w1[:, :].rearrange("p (k n) -> p k n", k=KT)
        uq3 = w2[:, 0:3 * H * QW].rearrange("p (k n) -> p k n", k=3)
        ukv3 = w2[:, 3456:3456 + 2 * H * 256].rearrange("p (k n) -> p k n", k=2)
        router3 = router_sb[:, :].rearrange("p (k e) -> p k e", k=KT)
        ident = const[:, C_ID:C_ID + P]
        mask = const[:, C_MASK:C_MASK + 3 * P]
        upper = const[:, C_UP:C_UP + P]
        ones = const[:, C_ONE:C_ONE + P]
        freq = const[:, C_FREQ:C_FREQ + HALF]

        def gate_w(s):
            return ring[:, s * SLOT_W:s * SLOT_W + KT * F].rearrange("p (k f) -> p k f", k=KT)

        def up_w(s):
            return ring[:, s * SLOT_W + KT * F:s * SLOT_W + 2 * KT * F].rearrange("p (k f) -> p k f", k=KT)

        def down_w(s):
            return ring[:, s * SLOT_W + 2 * KT * F:(s + 1) * SLOT_W].rearrange("p (k d) -> p k d", k=FT)

        def gate_up(s):
            return ring[:, s * SLOT_W:s * SLOT_W + 2 * KT * F].rearrange("p (q k f) -> p q k f", q=2, k=KT)

        ada = [ring[:, s * ADA_W:(s + 1) * ADA_W].rearrange("p (g n) -> p g n", g=4) for s in range(ADA_BUFS)]
        c32v = c32[:, :].rearrange("p (k n) -> p k n", k=KT)
        mod_bias = [xT[:, 0:512], sc_row[:, 0:512], sh_row[:, 0:512]]
        mod_val = [xT[:, 512:1024], sc_row[:, 512:1024], sh_row[:, 512:1024]]

        at = [2 * SLOT_W]

        def carve(n):
            at[0] += n
            return ring[:, at[0] - n:at[0]]

        proj3 = carve(NT * INW).rearrange("p (j n) -> p j n", j=NT)
        qT3 = carve(H * T).rearrange("p (h t) -> p h t", h=H)
        qrT3 = carve(3 * T).rearrange("p (h t) -> p h t", h=3)
        kT3 = carve(H * T).rearrange("p (h t) -> p h t", h=H)
        krT3 = carve(2 * T).rearrange("p (v t) -> p v t", v=2)
        v3 = carve(NT * H * VH).rearrange("p (j n) -> p j n", j=NT)
        latT3 = carve(5 * T).rearrange("p (k t) -> p k t", k=5)
        band_sb = carve(len(WINDOWS) * (T + P))
        band0 = band_sb[:, 0:len(WINDOWS) * T].rearrange("p (g t) -> p g t", t=T)
        band1 = band_sb[:, len(WINDOWS) * T:].rearrange("p (g t) -> p g t", t=P)
        tmT3 = carve(2 * T).rearrange("p (g t) -> p g t", g=2)
        wpool3 = carve(2 * 64).rearrange("p (g d) -> p g d", g=2)
        assert at[0] <= RING * SLOT_W

        qr3 = t3[:, :, 0:H * ROPE]
        qr4 = qr3.rearrange("p j (h r) -> p j h r", h=H)
        krp = t3[:, :, 384:384 + 2 * P].rearrange("p j (v n) -> p j v n", v=2)
        rtmp = t3[:, :, 640:832].rearrange("p j (h r) -> p j h r", h=H)
        ktmp = t3[:, :, 832:864]
        sP = temp[:, 0:768].rearrange("p (b n) -> p b n", b=2)
        PT = temp[:, 768:1536].rearrange("p (b n) -> p b n", b=2)
        junk = temp[:, 1536:1536 + QL]

        mt = [0]

        def moe(n):
            mt[0] += n
            return w2[:, mt[0] - n:mt[0]]

        h2p = moe(NT * D).rearrange("p (j d) -> p j d", j=NT)
        hTb = moe(KT * P).rearrange("p (k n) -> p k n", k=KT)
        ysb = moe(D)
        ST = moe(T)
        S = moe(NT * P).rearrange("p (j g n) -> p j g n", j=NT, g=2)
        SG = moe(NT * P).rearrange("p (j g n) -> p j g n", j=NT, g=2)
        sil = moe(F)
        mid = moe(F)
        midT = moe(FT * P).rearrange("p (k n) -> p k n", k=FT)
        R = moe(NT * E).rearrange("p (j e) -> p j e", j=NT)
        G = moe(NT * E).rearrange("p (j e) -> p j e", j=NT)
        Rc = moe(NT * 2).rearrange("p (j g) -> p j g", j=NT)
        Gc = moe(NT * 2).rearrange("p (j g) -> p j g", j=NT)
        sel = moe(NT * E).rearrange("p (j e) -> p j e", j=NT)
        shmid = moe(FT * T).rearrange("p (k t) -> p k t", k=FT)
        rbias = moe(E)
        assert mt[0] <= 6912
        shsil = temp[:, 1536:2048]

        def rt(i, n=NT * E):
            return temp[:, i:i + n]

        score = rt(0).rearrange("p (j e) -> p j e", j=NT)
        choice = rt(128).rearrange("p (j e) -> p j e", j=NT)
        top2 = rt(256)
        gs = rt(384, NT * NG).rearrange("p (j g) -> p j g", j=NT)
        grank = rt(400, NT * NG).rearrange("p (j g) -> p j g", j=NT)
        cmp1 = rt(512).rearrange("p (j a b) -> p j a b", j=NT, a=NG)
        cmp2 = rt(640).rearrange("p (j a b) -> p j a b", j=NT, a=NG)
        masked = rt(768).rearrange("p (j e) -> p j e", j=NT)
        top8 = rt(896, NT * 8).rearrange("p (j e) -> p j e", j=NT)
        gsum = rt(912, NT)
        grec = rt(914, NT)
        kcnt = temp[0:1, 1024:1024 + E]
        kcum = temp[0:1, 1088:1088 + E]
        kcnt2 = temp[0:1, 1160:1160 + E]
        kmax = temp[0:1, 1224:1224 + E // 2]

        posi = small[:, 0:2].bitcast(I32)
        posf = small[:, 2:4]
        eps_ln = small[:, 4:5]
        eps_rms = small[:, 5:6]
        bn = small[:, 16:40].rearrange("p (j s) -> p j s", j=NT)
        mv = small[:, 40:44].rearrange("p (j s) -> p j s", j=NT)
        std = small[:, 44:46]
        rstd = small[:, 46:48]
        nmr = small[:, 48:50]
        ssq = small[:, 50:54].rearrange("p (j s) -> p j s", j=NT)
        rms = small[:, 54:58].rearrange("p (j s) -> p j s", j=NT)
        mx = small[:, 60:72].rearrange("p (h s) -> p h s", h=H)
        nmx = small[:, 72:84].rearrange("p (h s) -> p h s", h=H)
        sm = small[:, 84:96].rearrange("p (h s) -> p h s", h=H)
        rsm = small[:, 96:108].rearrange("p (h s) -> p h s", h=H)
        ubase = small[0:1, 108:109]
        cs = sb("cs", NT * ROPE)
        cosv = cs[:, 0:NT * HALF].rearrange("p (j r) -> p j r", j=NT)
        sinv = cs[:, NT * HALF:].rearrange("p (j r) -> p j r", j=NT)
        c8 = temp[0:KT, 0:P]
        ang = temp[:, 512:512 + NT * HALF].rearrange("p (j r) -> p j r", j=NT)
        turns = temp[:, 576:576 + NT * HALF].rearrange("p (j r) -> p j r", j=NT)
        red = temp[:, 640:640 + NT * HALF].rearrange("p (j r) -> p j r", j=NT)

        ps = ctx.enter_context(nc.psum_tensor("ps", [P, 8, 512], F32))
        acc3 = ps[:, 0:4, :].rearrange("p (j h) n -> p j h n", j=NT)
        B_F, B_T, B_0, B_1 = 4, 5, 6, 7

        names = """consts_in x_in c_in pos_in eps_set cT_done c32_ready bias_in ada_done mod_val_ready
        modT_done modl_ready mod_written
        rope_ready layer_ready xT_done xT_ready win_in proj_done projA_ready projD_ready ssq_ready std_ready
        lat_ready krp_ready band_in tm_done tm_ready lat_done latT_ready krT_done krT_ready vec_in wpool_in pool_done
        pool_ready w2_in jobs_done jobsA_ready jobsD_ready qr_ready qrT_done qrT_ready scores_done s_ready
        exp_ready probs_ready pT_done PT_ready pv_done pv_ready wout_in mix_done rows1_in rows2_in ln_stats
        ln_std ln_coef ln_norm h2_ready h2T_done h2T_ready router_in rbias_in logits_done esc_ready sh_up_done
        shsil_ready shmid_ready sel_ready rank_done table_ready rg_ready
        sh_landed S_ready gath_done hT_ready gu_done sil_ready mid_ready SG_ready midT_done midT_ready down_done
        ST_done ST_ready y0_ready y1_ready scat_done sh_free out_done ang_ready gc_ready rc_ready pro_link
        dve_link waits_passed dist_ready""".split()
        s = {n: sem(n) for n in names}
        ada_landed = [sem(f"ada_landed{i}") for i in range(ADA_BUFS)]
        ada_used = [sem(f"ada_used{i}") for i in range(ADA_BUFS)]
        w_landed = [sem(f"w_landed{i}") for i in range(RING)]
        w_free = [sem(f"w_free{i}") for i in range(RING)]

        def passed(eng):
            eng.sem_inc(s["waits_passed"], 1)

        def blocks(eng, r):
            begin = eng.value_load(btab[0:1, ds(r, 1)], min_val=B0, max_val=MAXB)
            return begin, eng.value_load(btab[0:1, ds(r + 1, 1)], min_val=B0, max_val=MAXB)

        block = ctx.enter_context(nc.Block())

        def start_counts(eng, counts="", twice="", ones=()):
            for n in counts.split():
                eng.sem_inc(s[n], B0)
            for n in twice.split():
                eng.sem_inc(s[n], 2 * B0)
            for one in ones:
                eng.sem_inc(one, 1)

        @block.sync
        def _(sp):
            sp.dma_start(c8, c.rearrange("b (k p) -> (b k) p", p=P)).then_inc(s["c_in"], 16)
            sp.dma_start(const[:, :], consts_dram).then_inc(s["consts_in"], 16)
            sp.dma_start(posi, positions.rearrange("b (j p) -> p (b j)", p=P)).then_inc(s["pos_in"], 16)
            sp.dma_start(x3, x.rearrange("b (j p) d -> p (b j) d", p=P)).then_inc(s["x_in"], 16)
            def ada_tiles(l, first, end):
                for t in range(first, end):
                    part, kt = divmod(t, KT)
                    sp.wait_ge(ada_used[t % ADA_BUFS], l * ADA_USES + t // ADA_BUFS + 1)
                    src = w_ada[ds(l, 1), kt * P:(kt + 1) * P, part * ADA_W:(part + 1) * ADA_W]
                    sp.dma_start(ada[t % ADA_BUFS], src.rearrange("a p (g n) -> p (a g) n", g=4)).then_inc(ada_landed[t % ADA_BUFS], 16)

            def ada_bias(l, part):
                src = b_ada[ds(l, 1), part * ADA_W:(part + 1) * ADA_W]
                for g in range(4):
                    sp.dma_start(mod_bias[part][32 * g:32 * g + 32, :],
                                 src[:, g * 512:(g + 1) * 512].to_broadcast([32, 512])).then_inc(s["bias_in"], 16)

            def store_mod(l, part):
                sp.wait_ge(s["mod_val_ready"], l * 3 + part + 1)
                dst = mod_dram[ds(l, 1), part * ADA_W:(part + 1) * ADA_W].rearrange("a (g n) -> (a g) n", g=4)
                sp.dma_start(dst, mod_val[part][0:P:32, :]).then_inc(s["mod_written"], 16)
                sp.wait_ge(s["mod_written"], (l * 2 + part) * 16)

            def lay(w, l):
                return w[ds(l, 1)]

            def expert(slot, l, e):
                sp.dma_start(gate_w(slot), w_exp_gate[ds(l, 1), ds(e, 1)].rearrange("a b (p k) f -> p (a b k) f", k=KT)).then_inc(w_landed[slot], 16)
                sp.dma_start(up_w(slot), w_exp_up[ds(l, 1), ds(e, 1)].rearrange("a b (p k) f -> p (a b k) f", k=KT)).then_inc(w_landed[slot], 16)
                sp.dma_start(down_w(slot), w_exp_down[ds(l, 1), ds(e, 1)].rearrange("a b (k p) d -> p (a b k) d", p=P)).then_inc(w_landed[slot], 16)

            def row(dst, src, sm_):
                sp.dma_start(dst, src.to_broadcast([P, D])).then_inc(sm_, 16)

            with sp.Fori(0, L) as l:
                def mod_row(dst, m, sm_):
                    row(dst, mod_dram[ds(l, 1), m * D:(m + 1) * D], sm_)

                sp.wait_ge(s["sh_free"], l + 1)
                ada_bias(l, 0)
                for k in range(2):
                    sp.wait_ge(w_free[k], l * (E // RING) + 1)
                ada_tiles(l, 0, 4)
                sp.wait_ge(s["mix_done"], l + 1)
                sp.dma_start(win3, lay(w_in, l).rearrange("a (k p) n -> p (a k) n", p=P)).then_inc(s["win_in"], 16)
                ada_tiles(l, 4, 8)
                sp.wait_ge(s["layer_ready"], l + 1)
                ada_bias(l, 1)
                ada_bias(l, 2)
                sp.dma_start(colv[:, 0:3], lay(q_norm_g, l).rearrange("a (k p) -> p (a k)", p=P)).then_inc(s["vec_in"], 16)
                sp.dma_start(colv[:, 3:5], lay(kv_norm_g, l).rearrange("a (k p) -> p (a k)", p=P)).then_inc(s["vec_in"], 16)
                sp.dma_start(colv[:, 5:7], lay(pool_scale, l).rearrange("a (k p) -> p (a k)", p=P)).then_inc(s["vec_in"], 16)
                ada_tiles(l, 8, 12)
                sp.dma_start(band_sb, band_dram).then_inc(s["band_in"], 16)
                for g in range(2):
                    sp.dma_start(wpool3[:, g, :], w_pool[ds(l, 1), 2 * g:2 * g + 2].rearrange("a g c d -> (a g c) d")).then_inc(s["wpool_in"], 16)
                sp.dma_start(uq3, lay(w_uq, l).rearrange("a (k p) n -> p (a k) n", p=P)).then_inc(s["w2_in"], 16)
                sp.dma_start(ukv3, lay(w_ukv, l).rearrange("a (k p) n -> p (a k) n", p=P)).then_inc(s["w2_in"], 16)
                ada_tiles(l, 12, 16)
                sp.wait_ge(s["proj_done"], l + 1)
                sp.dma_start(wout3, lay(w_out, l).rearrange("a (k p) n -> p (a k) n", p=P)).then_inc(s["wout_in"], 16)
                sp.dma_start(router3, lay(w_router, l).rearrange("a (p k) e -> p (a k) e", k=KT)).then_inc(s["router_in"], 16)
                row(lng_row, lay(ln1_g, l), s["rows1_in"])
                row(lnb_row, lay(ln1_b, l), s["rows1_in"])
                ada_tiles(l, 16, 20)
                store_mod(l, 1)
                mod_row(g_row, 2, s["rows1_in"])
                ada_tiles(l, 20, 24)
                store_mod(l, 2)
                mod_row(sc_row, 4, s["rows1_in"])
                mod_row(sh_row, 3, s["rows1_in"])
                for k in range(2):
                    expert(k, l, k)
                sp.wait_ge(s["pv_ready"], (l + 1) * H)
                sp.dma_start(gate_w(3), lay(w_sh_gate, l).rearrange("a (p k) f -> p (a k) f", k=KT)).then_inc(s["sh_landed"], 16)
                sp.dma_start(up_w(3), lay(w_sh_up, l).rearrange("a (p k) f -> p (a k) f", k=KT)).then_inc(s["sh_landed"], 16)
                sp.dma_start(down_w(3), lay(w_sh_down, l).rearrange("a (k p) d -> p (a k) d", p=P)).then_inc(s["sh_landed"], 16)
                expert(2, l, 2)
                sp.wait_ge(s["h2_ready"], (l + 1) * NT)
                sp.dma_start(rbias, lay(router_bias, l).to_broadcast([P, E])).then_inc(s["rbias_in"], 16)
                mod_row(g_row, 5, s["rows2_in"])
                row(lng_row, lay(ln2_g, l), s["rows2_in"])
                row(lnb_row, lay(ln2_b, l), s["rows2_in"])
                sp.wait_ge(s["sh_free"], l + 2)
                expert(3, l, 3)
                with sp.Fori(1, E // RING) as i:
                    for k in range(RING):
                        sp.wait_ge(w_free[k], l * (E // RING) + i + 1)
                        expert(k, l, i * RING + k)
            sp.wait_ge(s["layer_ready"], L + 1)
            sp.dma_start(out.rearrange("b (j p) d -> p (b j) d", p=P), x3).then_inc(s["out_done"], 16)
            sp.wait_ge(s["out_done"], 16)

        @block.tensor
        def _(pe):
            mm = nc.tensor.matmul
            tr = nc.tensor.transpose
            start_counts(pe, "gu_done midT_done ST_done scat_done", "gath_done down_done",
                         [s["mix_done"], s["sh_free"], *ada_used])

            pe.wait_ge(s["consts_in"], 16)
            pe.wait_ge(s["c_in"], 16)
            tr(ps[:, 4, 0:KT], c8, ident[0:KT, 0:KT]).then_inc(s["cT_done"], 1)
            pe.wait_ge(s["c32_ready"], 1)

            def modulation(l, part):
                for kt in range(KT):
                    t = part * KT + kt
                    pe.wait_ge(ada_landed[t % ADA_BUFS], (l * ADA_USES + t // ADA_BUFS + 1) * 16)
                    passed(pe)
                    for g in range(4):
                        last = mm(ps[32 * g:32 * g + 32, 7, :], c32v[:, kt, :], ada[t % ADA_BUFS][:, g, :],
                                  start=kt == 0, stop=kt == KT - 1)
                    last.then_inc(ada_used[t % ADA_BUFS], 1)

            with pe.Fori(0, L) as l:
                modulation(l, 0)
                pe.wait_ge(s["mod_val_ready"], l * 3 + 1)
                for k in range(4):
                    last = tr(ps[:, 6, k * P:(k + 1) * P], mod_val[0][:, k * P:(k + 1) * P], ident)
                last.then_inc(s["modT_done"], 1)
                pe.wait_ge(s["layer_ready"], l + 1)
                for kt in range(KT):
                    if kt == 4:
                        pe.wait_ge(s["modl_ready"], l + 1)
                    for j in range(NT):
                        last = tr(ps[:, 4 + kt // 2, (kt % 2) * T + j * P:(kt % 2) * T + (j + 1) * P],
                                  x3[:, j, kt * P:(kt + 1) * P], ident)
                    if kt % 2:
                        last.then_inc(s["xT_done"], 1)
                pe.wait_ge(s["win_in"], (l + 1) * 16)
                for kt in range(KT):
                    pe.wait_ge(s["xT_ready"], l * KT + kt + 1)
                    for j in range(NT):
                        for half in range(2):
                            last = mm(ps[:, 2 * j + half, 0:HW], xT3[:, kt, j * P:(j + 1) * P],
                                      win3[:, kt, half * HW:(half + 1) * HW], start=kt == 0, stop=kt == KT - 1)
                last.then_inc(s["proj_done"], 1)
                modulation(l, 1)
                pe.wait_ge(s["projA_ready"], l + 1)
                pe.wait_ge(s["projD_ready"], l + 1)
                pe.wait_ge(s["band_in"], (l + 1) * 16)
                for g in range(2):
                    for i in range(2):
                        o = ps[i * 64:(i + 1) * 64, 1, :]
                        u = 2 * g + i
                        mm(o[:, g * T:(g + 1) * T], proj3[:, 0, u * 64:(u + 1) * 64], band0[:, u, :], start=True, stop=False)
                        last = mm(o[:, g * T + P:(g + 1) * T], proj3[:, 1, u * 64:(u + 1) * 64], band1[:, u, :], start=False, stop=True)
                last.then_inc(s["tm_done"], 1)
                pe.wait_ge(s["lat_ready"], l + 1)
                for i in range(5):
                    for j in range(NT):
                        last = tr(ps[:, 4 + i // 2, (i % 2) * T + j * P:(i % 2) * T + (j + 1) * P],
                                  proj3[:, j, POOL + i * P:POOL + (i + 1) * P], ident)
                last.then_inc(s["lat_done"], 1)
                pe.wait_ge(s["krp_ready"], l + 1)
                for v in range(2):
                    for j in range(NT):
                        last = tr(ps[:, 0, v * T + j * P:v * T + (j + 1) * P], krp[:, j, v, :], ident)
                last.then_inc(s["krT_done"], 1)
                pe.wait_ge(s["tm_ready"], l + 1)
                pe.wait_ge(s["wpool_in"], (l + 1) * 32)
                passed(pe)
                for g in range(2):
                    for i in range(2):
                        q = slice(i * 64, (i + 1) * 64)
                        last = mm(ps[q, 1, g * T:(g + 1) * T], wpool3[q, g, :], tmT3[q, g, :], start=True, stop=True)
                last.then_inc(s["pool_done"], 1)
                pe.wait_ge(s["mod_val_ready"], l * 3 + 2)
                pe.wait_ge(s["w2_in"], (l + 1) * 32)
                pe.wait_ge(s["latT_ready"], (l + 1) * 5)

                def job_bank(n):
                    if n in (6, 7):
                        pe.wait_ge(s["jobsD_ready"], l * 2 + n - 5)
                    elif n >= 8:
                        pe.wait_ge(s["jobsA_ready"], l * 10 + n - 7)
                    return ps[:, 2 + n % 6, :]

                for j in range(NT):
                    o = job_bank(j)[:, 0:H * ROPE].rearrange("p (h r) -> p h r", h=H)
                    for kt in range(3):
                        w = uq3[:, kt, :].rearrange("p (h n) -> p h n", h=H)[:, :, NOPE:QW]
                        last = mm(o, latT3[:, kt, j * P:(j + 1) * P], w, start=kt == 0, stop=kt == 2)
                    last.then_inc(s["jobs_done"], 1)
                n = 2
                for hp in range(H // 2):
                    o = job_bank(n)
                    for i in range(2):
                        h = 2 * hp + i
                        for kt in range(3):
                            last = mm(o[:, i * T:(i + 1) * T], uq3[:, kt, h * QW:h * QW + NOPE], latT3[:, kt, :],
                                      start=kt == 0, stop=kt == 2)
                    last.then_inc(s["jobs_done"], 1)
                    n += 1
                for hp in range(H // 2):
                    o = job_bank(n)
                    for i in range(2):
                        h = 2 * hp + i
                        for kt in range(2):
                            last = mm(o[:, i * T:(i + 1) * T], ukv3[:, kt, h * 256:h * 256 + NOPE], latT3[:, 3 + kt, :],
                                      start=kt == 0, stop=kt == 1)
                    last.then_inc(s["jobs_done"], 1)
                    n += 1
                for j in range(NT):
                    for hh in range(2):
                        o = job_bank(n)[:, 0:3 * VH].rearrange("p (h n) -> p h n", h=3)
                        for kt in range(2):
                            w = ukv3[:, kt, :].rearrange("p (h n) -> p h n", h=H)[:, 3 * hh:3 * hh + 3, NOPE:256]
                            last = mm(o, latT3[:, 3 + kt, j * P:(j + 1) * P], w, start=kt == 0, stop=kt == 1)
                        last.then_inc(s["jobs_done"], 1)
                        n += 1
                pe.wait_ge(s["qr_ready"], (l + 1) * NT)
                pe.wait_ge(s["krT_ready"], l + 1)
                pe.wait_ge(s["pool_ready"], l + 1)
                for i in range(3):
                    for j in range(NT):
                        last = tr(ps[:, i // 2, (i % 2) * T + j * P:(i % 2) * T + (j + 1) * P],
                                  qr3[:, j, i * P:(i + 1) * P], ident)
                last.then_inc(s["qrT_done"], 1)
                pe.wait_ge(s["jobsA_ready"], (l + 1) * 10)
                pe.wait_ge(s["qrT_ready"], l + 1)
                for h in range(H):
                    for j in range(NT):
                        o = ps[:, h, j * P:j * P + (j + 1) * P]
                        mm(o, qT3[:, h, j * P:(j + 1) * P], kT3[:, h, 0:(j + 1) * P], start=True, stop=False)
                        last = mm(o, qrT3[:, h // 2, j * P:(j + 1) * P], krT3[:, h % 2, 0:(j + 1) * P], start=False, stop=True)
                    last.then_inc(s["scores_done"], 1)

                def turn_probs(h):
                    pe.wait_ge(s["probs_ready"], l * H + h + 1)
                    if h >= 2:
                        pe.wait_ge(s["PT_ready"], l * H + h - 1)
                    for i in range(3):
                        last = tr(ps[:, 6 + h % 2, i * P:(i + 1) * P], sP[:, h % 2, i * P:(i + 1) * P], ident)
                    last.then_inc(s["pT_done"], 1)

                turn_probs(0)
                for h in range(H):
                    if h + 1 < H:
                        turn_probs(h + 1)
                    pe.wait_ge(s["PT_ready"], l * H + h + 1)
                    v = [v3[:, j, h * VH:(h + 1) * VH] for j in range(NT)]
                    mm(ps[:, h, 0:P], v[0], PT[:, h % 2, 0:P], start=True, stop=True)
                    mm(ps[:, h, P:2 * P], v[0], PT[:, h % 2, P:2 * P], start=True, stop=False)
                    mm(ps[:, h, P:2 * P], v[1], PT[:, h % 2, 2 * P:3 * P], start=False, stop=True).then_inc(s["pv_done"], 1)
                modulation(l, 2)
                pe.wait_ge(s["wout_in"], (l + 1) * 16)
                pe.wait_ge(s["pv_ready"], (l + 1) * H)
                for kt in range(KT):
                    for j in range(NT):
                        for half in range(2):
                            last = mm(acc3[:, j, half, :], xT3[:, kt, j * P:(j + 1) * P],
                                      wout3[:, kt, half * 512:(half + 1) * 512], start=kt == 0, stop=kt == KT - 1)
                last.then_inc(s["mix_done"], 1)
                pe.wait_ge(s["mod_val_ready"], l * 3 + 3)
                pe.wait_ge(s["h2_ready"], (l + 1) * NT)
                for kt in range(KT):
                    for j in range(NT):
                        last = tr(ps[:, 4 + kt // 2, (kt % 2) * T + j * P:(kt % 2) * T + (j + 1) * P],
                                  h2p[:, j, kt * P:(kt + 1) * P], ident)
                    if kt % 2:
                        last.then_inc(s["h2T_done"], 1)
                pe.wait_ge(s["h2T_ready"], (l + 1) * 4)
                pe.wait_ge(s["router_in"], (l + 1) * 16)
                for j in range(NT):
                    for kt in range(KT):
                        last = mm(ps[:, 4, j * E:(j + 1) * E], xT3[:, kt, j * P:(j + 1) * P], router3[:, kt, :],
                                  start=kt == 0, stop=kt == KT - 1)
                last.then_inc(s["logits_done"], 1)
                pe.wait_ge(s["sh_landed"], (l + 1) * 48)
                for w, b in ((gate_w(3), 5), (up_w(3), 6)):
                    for f in range(FT):
                        for kt in range(KT):
                            last = mm(ps[:, b, f * T:(f + 1) * T], w[:, kt, f * P:(f + 1) * P], xT3[:, kt, :],
                                      start=kt == 0, stop=kt == KT - 1)
                last.then_inc(s["sh_up_done"], 1)
                pe.wait_ge(s["sel_ready"], l + 1)
                mm(ps[:, 7, 0:E], upper, sel[:, 0, :], start=True, stop=True)
                mm(ps[:, 7, E:2 * E], ones, sel[:, 0, :], start=True, stop=False)
                mm(ps[:, 7, E:2 * E], upper, sel[:, 1, :], start=False, stop=True)
                mm(ps[0:1, 7, 2 * E:3 * E], ones[:, 0:1], sel[:, 0, :], start=True, stop=False)
                mm(ps[0:1, 7, 2 * E:3 * E], ones[:, 0:1], sel[:, 1, :], start=False, stop=True).then_inc(s["rank_done"], 1)
                pe.wait_ge(s["shmid_ready"], l + 1)
                for f in range(FT):
                    for j in range(NT):
                        for half in range(2):
                            last = mm(acc3[:, j, half, :], shmid[:, f, j * P:(j + 1) * P],
                                      down_w(3)[:, f, half * 512:(half + 1) * 512], start=f == 0, stop=f == FT - 1)
                last.then_inc(s["sh_free"], 1)

                def gather(b, half):
                    for kt in range(4 * half, 4 * half + 4):
                        for j in range(NT):
                            last = mm(ps[:, B_0 + half, (kt % 4) * P:(kt % 4 + 1) * P], h2p[:, j, kt * P:(kt + 1) * P],
                                      S[:, j].rearrange("p g n -> p (g n)"), start=j == 0, stop=j == NT - 1)
                    last.then_inc(s["gath_done"], 1)

                pe.wait_ge(s["table_ready"], l + 1)
                pe.wait_ge(s["shmid_ready"], l + 1)
                passed(pe)
                b0 = pe.value_load(btab[0:1, 0:1], min_val=B0, max_val=MAXB)
                pe.wait_ge(s["S_ready"], b0 + l + 1)
                gather(b0, 0)
                gather(b0, 1)
                with pe.Fori(0, E // RING) as i:
                    for q in range(2):
                        begin, end = blocks(pe, i * 2 + q)
                        slots = (2 * q, 2 * q + 1)
                        for k in slots:
                            pe.wait_ge(w_landed[k], (l * (E // RING) + i + 1) * 48)
                        passed(pe)
                        with pe.Fori(begin, end) as b:
                            pe.wait_ge(s["hT_ready"], (b + l + 1) * 2)
                            pe.wait_ge(s["y1_ready"], b)
                            passed(pe)
                            for kt in range(KT):
                                for g, k in enumerate(slots):
                                    last = mm(ps[64 * g:64 * g + 64, B_F, :].rearrange("p (q f) -> p q f", q=2),
                                              hTb[:, kt, 64 * g:64 * g + 64], gate_up(k)[:, :, kt, :],
                                              start=kt == 0, stop=kt == KT - 1)
                            last.then_inc(s["gu_done"], 1)
                            pe.wait_ge(s["S_ready"], b + l + 2)
                            pe.wait_ge(s["y0_ready"], b)
                            gather(b + 1, 0)
                            pe.wait_ge(s["mid_ready"], b + 1)
                            pe.wait_ge(s["ST_ready"], b)
                            for f in range(FT):
                                last = tr(ps[:, B_T, f * P:(f + 1) * P], mid[:, f * P:(f + 1) * P], ident)
                            last.then_inc(s["midT_done"], 1)
                            gather(b + 1, 1)

                            def down(half, bank):
                                for f in range(FT):
                                    for g, k in enumerate(slots):
                                        last = mm(ps[64 * g:64 * g + 64, bank, :], midT[:, f, 64 * g:64 * g + 64],
                                                  down_w(k)[:, f, half * 512:(half + 1) * 512], start=f == 0, stop=f == FT - 1)
                                last.then_inc(s["down_done"], 1)

                            pe.wait_ge(s["midT_ready"], b + 1)
                            pe.wait_ge(s["hT_ready"], (b + l + 1) * 2 + 1)
                            passed(pe)
                            down(0, B_0)
                            pe.wait_ge(s["SG_ready"], b + 1)
                            for j in range(NT):
                                last = tr(ps[:, B_T, j * P:(j + 1) * P], SG[:, j].rearrange("p g n -> p (g n)"), ident)
                            last.then_inc(s["ST_done"], 1)
                            down(1, B_F)
                            pe.wait_ge(s["ST_ready"], b + 1)
                            for half in range(2):
                                pe.wait_ge(s[f"y{half}_ready"], b + 1)
                                for j in range(NT):
                                    last = mm(acc3[:, j, half, :], ST[:, j * P:(j + 1) * P],
                                              ysb[:, half * 512:(half + 1) * 512], start=False, stop=True,
                                              skip_group_check=True)
                            last.then_inc(s["scat_done"], 1)
                last = pe.value_load(btab[0:1, E // 2:E // 2 + 1], min_val=B0, max_val=MAXB)
                pe.wait_ge(s["hT_ready"], (last + l + 1) * 2)

        @block.scalar
        def _(act):
            fn = nc.scalar.activation
            start_counts(act, "sil_ready y0_ready", "hT_ready")
            act.wait_ge(s["cT_done"], 1)
            fn(c32v, ps[:, 4, 0:KT].unsqueeze(2).to_broadcast([P, KT, 32]), ACT.Silu).then_inc(s["c32_ready"], 1)
            act.wait_ge(s["ang_ready"], 1)
            fn(sinv, ang, ACT.Sin)
            fn(cosv, red, ACT.Sin).then_inc(s["rope_ready"], 1)

            with act.Fori(0, L) as l:
                act.wait_ge(s["modl_ready"], l + 1)
                for kt in range(KT):
                    act.wait_ge(s["xT_done"], l * (KT // 2) + kt // 2 + 1)
                    fn(xT3[:, kt, :], ps[:, 4 + kt // 2, (kt % 2) * T:(kt % 2 + 1) * T], ACT.Identity,
                       scale=modl[:, KT + kt:KT + kt + 1], bias=modl[:, kt:kt + 1]).then_inc(s["xT_ready"], 1)
                act.wait_ge(s["proj_done"], l + 1)
                fn(proj3[:, 0, :].rearrange("p (b n) -> p b n", b=2), ps[:, 0:2, 0:HW], ACT.Copy).then_inc(s["projA_ready"], 1)
                act.wait_ge(s["projA_ready"], l + 1)
                act.wait_ge(s["projD_ready"], l + 1)
                for j in range(NT):
                    fn(junk, proj3[:, j, POOL:POOL + QL], ACT.Square, accum_out=ssq[:, j, 0:1]).then_inc(s["ssq_ready"], 1)
                    act.wait_ge(s["ssq_ready"], l * 4 + 2 * j + 1)
                    fn(junk[:, 0:KVL], proj3[:, j, POOL + QL:POOL + QL + KVL], ACT.Square, accum_out=ssq[:, j, 1:2]).then_inc(s["ssq_ready"], 1)
                    act.wait_ge(s["ssq_ready"], l * 4 + 2 * j + 2)
                fn(rms[:, :, 0], ssq[:, :, 0], ACT.Sqrt, scale=1.0 / QL, bias=eps_rms)
                fn(rms[:, :, 1], ssq[:, :, 1], ACT.Sqrt, scale=1.0 / KVL, bias=eps_rms).then_inc(s["std_ready"], 1)
                act.wait_ge(s["lat_done"], l + 1)
                act.wait_ge(s["vec_in"], (l + 1) * 48)
                for k in range(5):
                    fn(latT3[:, k, :], ps[:, 4 + k // 2, (k % 2) * T:(k % 2 + 1) * T], ACT.Copy,
                       scale=colv[:, k:k + 1]).then_inc(s["latT_ready"], 1)
                act.wait_ge(s["krT_done"], l + 1)
                fn(krT3, ps[:, 0, :].rearrange("p (v t) -> p v t", v=2), ACT.Copy).then_inc(s["krT_ready"], 1)
                for n in range(2, 12):
                    act.wait_ge(s["jobs_done"], l * 12 + n + 1)
                    b = ps[:, 2 + n % 6, :]
                    if n < 5:
                        dst, src = qT3[:, 2 * (n - 2):2 * (n - 2) + 2, :], b.rearrange("p (h t) -> p h t", h=2)
                    elif n < 8:
                        dst, src = kT3[:, 2 * (n - 5):2 * (n - 5) + 2, :], b.rearrange("p (h t) -> p h t", h=2)
                    else:
                        j, hh = divmod(n - 8, 2)
                        dst, src = v3[:, j, hh * 3 * VH:(hh + 1) * 3 * VH], b[:, 0:3 * VH]
                    fn(dst, src, ACT.Copy).then_inc(s["jobsA_ready"], 1)
                act.wait_ge(s["qrT_done"], l + 1)
                fn(qrT3.rearrange("p h t -> p (h t)"), ps[:, 0:2, :].rearrange("p b n -> p (b n)")[:, 0:3 * T], ACT.Copy).then_inc(s["qrT_ready"], 1)

                def exps(h):
                    act.wait_ge(s["s_ready"], l * H + h + 1)
                    fn(sP[:, h % 2, 0:P], sP[:, h % 2, 0:P], ACT.Exp, scale=SCALE, bias=nmx[:, h, 0:1], accum_out=sm[:, h, 0:1])
                    fn(sP[:, h % 2, P:3 * P], sP[:, h % 2, P:3 * P], ACT.Exp, scale=SCALE, bias=nmx[:, h, 1:2],
                       accum_out=sm[:, h, 1:2]).then_inc(s["exp_ready"], 1)

                def mixed(h):
                    act.wait_ge(s["pv_done"], l * H + h + 1)
                    fn(xT3[:, 2 + h, :], ps[:, h, 0:T], ACT.Copy).then_inc(s["pv_ready"], 1)

                exps(0)
                for h in range(H):
                    if h + 1 < H:
                        exps(h + 1)
                    act.wait_ge(s["pT_done"], l * H + h + 1)
                    if h >= 2:
                        act.wait_ge(s["pv_done"], l * H + h - 1)
                    fn(PT[:, h % 2, :], ps[:, 6 + h % 2, 0:3 * P], ACT.Copy).then_inc(s["PT_ready"], 1)
                    if h >= 1:
                        mixed(h - 1)
                mixed(H - 1)

                def norm(which):
                    act.wait_ge(s["ln_stats"], 2 * l + which + 1)
                    fn(std, mv[:, :, 1], ACT.Sqrt, bias=eps_ln).then_inc(s["ln_std"], 1)
                    act.wait_ge(s["ln_coef"], 2 * l + which + 1)
                    for j in range(NT):
                        fn(t3[:, j, :], t3[:, j, :], ACT.Identity, scale=rstd[:, j:j + 1], bias=nmr[:, j:j + 1]).then_inc(s["ln_norm"], 1)

                norm(0)
                for b in range(4):
                    act.wait_ge(s["h2T_done"], l * 4 + b + 1)
                    fn(xT3[:, 2 * b:2 * b + 2, :], ps[:, 4 + b, :].rearrange("p (k t) -> p k t", k=2), ACT.Copy).then_inc(s["h2T_ready"], 1)
                act.wait_ge(s["logits_done"], l + 1)
                fn(score.rearrange("p j e -> p (j e)"), ps[:, 4, 0:NT * E], ACT.Exp, scale=-1.0).then_inc(s["esc_ready"], 1)
                act.wait_ge(s["sh_up_done"], l + 1)
                fn(shsil, ps[:, 5, :], ACT.Silu).then_inc(s["shsil_ready"], 1)

                def gathered(b, half):
                    act.wait_ge(s["gath_done"], (b + l) * 2 + half + 1)
                    fn(hTb[:, 4 * half:4 * half + 4, :], ps[:, B_0 + half, :].rearrange("p (k n) -> p k n", k=4), ACT.Copy).then_inc(s["hT_ready"], 1)

                act.wait_ge(s["table_ready"], l + 1)
                passed(act)
                b0 = act.value_load(btab[0:1, 0:1], min_val=B0, max_val=MAXB)
                gathered(b0, 0)
                gathered(b0, 1)
                with act.Fori(0, E // 2) as r:
                    begin, end = blocks(act, r)
                    with act.Fori(begin, end) as b:
                        act.wait_ge(s["gu_done"], b + 1)
                        act.wait_ge(s["mid_ready"], b)
                        fn(sil, ps[:, B_F, 0:F], ACT.Silu).then_inc(s["sil_ready"], 1)
                        gathered(b + 1, 0)
                        gathered(b + 1, 1)
                        act.wait_ge(s["down_done"], b * 2 + 1)
                        act.wait_ge(s["scat_done"], b)
                        fn(ysb[:, 0:512], ps[:, B_0, :], ACT.Copy).then_inc(s["y0_ready"], 1)
                norm(1)

        @block.gpsimd
        def _(pool):
            eng = nc.gpsimd
            start_counts(pool, "S_ready SG_ready rc_ready dist_ready")
            eng.memset(eps_ln, LN_EPS)
            eng.memset(eps_rms, RMS_EPS).then_inc(s["eps_set"], 1)
            iota = const[:, C_IOTA:C_IOTA + UNIT].unsqueeze(1).unsqueeze(1).to_broadcast([P, NT, 2, UNIT])
            pool.wait_ge(s["consts_in"], 16)
            with pool.Fori(0, L) as l:
                def one_hot(count):
                    eng.tensor_tensor(S, iota, Rc.unsqueeze(3).to_broadcast([P, NT, 2, UNIT]), ALU.subtract).then_inc(s["dist_ready"], 1)
                    pool.wait_ge(s["dist_ready"], count)
                    passed(pool)
                    return eng.tensor_scalar(S, S, 0.0, None, ALU.is_equal)

                pool.wait_ge(s["table_ready"], l + 1)
                passed(pool)
                with pool.Fori(0, E // 2) as r:
                    begin, end = blocks(pool, r)
                    pool.wait_ge(s["SG_ready"], begin)
                    pool.wait_ge(s["rc_ready"], l * (E // 2) + r + begin)
                    passed(pool)
                    eng.tensor_copy(Gc, G[:, :, ds(r * 2, 2)]).then_inc(s["gc_ready"], 1)
                    eng.tensor_copy(Rc, R[:, :, ds(r * 2, 2)]).then_inc(s["rc_ready"], 1)
                    pool.wait_ge(s["gc_ready"], l * (E // 2) + r + 1)
                    passed(pool)
                    with pool.Fori(begin, end) as b:
                        pool.wait_ge(s["rc_ready"], l * (E // 2) + r + 1 + b)
                        pool.wait_ge(s["gath_done"], (b + l) * 2)
                        one_hot(b + l + 1).then_inc(s["S_ready"], 1)
                        pool.wait_ge(s["S_ready"], b + l + 1)
                        pool.wait_ge(s["ST_done"], b)
                        eng.tensor_tensor(SG, S, Gc.unsqueeze(3).to_broadcast([P, NT, 2, UNIT]), ALU.mult).then_inc(s["SG_ready"], 1)
                        eng.tensor_scalar(Rc, Rc, -float(UNIT), None, ALU.add).then_inc(s["rc_ready"], 1)
                last = pool.value_load(btab[0:1, E // 2:E // 2 + 1], min_val=B0, max_val=MAXB)
                pool.wait_ge(s["rc_ready"], (l + 1) * (E // 2) + last)
                pool.wait_ge(s["gath_done"], (last + l) * 2)
                one_hot(last + l + 1).then_inc(s["S_ready"], 1)

        @block.vector
        def _(dve):
            v = nc.vector
            links = [0, 0]
            start_counts(dve, "mid_ready midT_ready ST_ready y1_ready", ones=w_free)

            def plink(ins):
                links[0] += 1
                ins.then_inc(s["pro_link"], 1)
                dve.wait_ge(s["pro_link"], links[0])

            plink(v.memset(ubase, float(B0)))
            dve.wait_ge(s["pos_in"], 16)
            dve.wait_ge(s["consts_in"], 16)
            plink(v.tensor_copy(posf, posi))
            for j in range(NT):
                ins = v.tensor_scalar(ang[:, j, :], freq, posf[:, j:j + 1], None, ALU.mult)
            plink(ins)

            def reduce_angle(dst, quarter):
                plink(v.tensor_scalar(turns, ang, 0.15915494309189535, 0.25 * quarter, ALU.mult, ALU.add))
                plink(v.tensor_scalar(turns, turns, MAGIC, None, ALU.add))
                plink(v.tensor_scalar(turns, turns, -MAGIC, None, ALU.add))
                src = ang
                for part in TWO_PI_PARTS:
                    plink(v.scalar_tensor_tensor(dst, turns, -part, src, ALU.mult, ALU.add))
                    src = dst
                if quarter:
                    plink(v.tensor_scalar(dst, dst, 1.5707963267948966, None, ALU.add))
                return v.tensor_scalar(dst, dst, 3.1415925, -3.1415925, ALU.min, ALU.max)

            plink(reduce_angle(red, 1))
            reduce_angle(ang, 0).then_inc(s["ang_ready"], 1)
            dve.wait_ge(s["rope_ready"], 1)
            dve.wait_ge(s["eps_set"], 1)
            dve.wait_ge(s["c32_ready"], 1)
            dve.wait_ge(s["x_in"], 16)

            with dve.Fori(0, L) as l:
                def link(ins, own=False):
                    links[1] += 1
                    ins.then_inc(s["dve_link"], 1)
                    dve.wait_ge(s["dve_link"], l * DVE_LINKS + links[1])
                    if own:
                        passed(dve)

                def mod_value(part, plus_one):
                    dve.wait_ge(ada_used[(part * KT + KT - 1) % ADA_BUFS], l * ADA_USES + (part * KT + KT - 1) // ADA_BUFS + 2)
                    dve.wait_ge(s["bias_in"], (l * 3 + part + 1) * 64)
                    first = v.tensor_tensor(mod_val[part], ps[:, 7, :], mod_bias[part], ALU.add)
                    if plus_one is None:
                        return first
                    link(first)
                    return v.tensor_scalar(mod_val[part][plus_one, :], mod_val[part][plus_one, :], 1.0, None, ALU.add)

                dve.sem_inc(s["layer_ready"], 1)
                mod_value(0, slice(64, 128)).then_inc(s["mod_val_ready"], 1)
                dve.wait_ge(s["modT_done"], l + 1)
                v.tensor_copy(modl[:, :].rearrange("p (g k) -> p g k", g=4),
                              ps[:, 6, :].rearrange("p (k g n) -> p g k n", k=4, g=4)[:, :, :, 0]).then_inc(s["modl_ready"], 1)
                dve.wait_ge(s["proj_done"], l + 1)
                v.tensor_copy(proj3[:, 1, :].rearrange("p (b n) -> p b n", b=2), ps[:, 2:4, 0:HW]).then_inc(s["projD_ready"], 1)
                mod_value(1, None).then_inc(s["mod_val_ready"], 1)
                dve.wait_ge(s["std_ready"], l + 1)
                link(v.reciprocal(ssq, rms))
                for j in range(NT):
                    for a, n, k in ((POOL, QL, 0), (POOL + QL, KVL, 1)):
                        ins = v.tensor_scalar(proj3[:, j, a:a + n], proj3[:, j, a:a + n], ssq[:, j, k:k + 1], None, ALU.mult)
                ins.then_inc(s["lat_ready"], 1)
                k1, k2 = proj3[:, :, INW - ROPE:INW - HALF], proj3[:, :, INW - HALF:INW]
                o1, o2 = krp[:, :, 0, 0:HALF], krp[:, :, 0, HALF:ROPE]
                v.memset(krp[:, :, 0, ROPE:P], 0.0)
                v.memset(krp[:, :, 1, 0:ROPE], 0.0)
                v.tensor_tensor(o1, k1, cosv, ALU.mult)
                v.tensor_tensor(o2, k2, cosv, ALU.mult)
                link(v.tensor_tensor(ktmp, k2, sinv, ALU.mult))
                link(v.tensor_tensor(o1, o1, ktmp, ALU.subtract))
                link(v.tensor_tensor(ktmp, k1, sinv, ALU.mult))
                link(v.tensor_tensor(o2, o2, ktmp, ALU.add))
                v.tensor_copy(krp[:, :, 1, ROPE:P], krp[:, :, 0, 0:ROPE]).then_inc(s["krp_ready"], 1)
                dve.wait_ge(s["tm_done"], l + 1)
                v.tensor_copy(tmT3, ps[:, 1, :].rearrange("p (g t) -> p g t", g=2)).then_inc(s["tm_ready"], 1)
                dve.wait_ge(s["pool_done"], l + 1)
                dve.wait_ge(s["vec_in"], (l + 1) * 48)
                for g in range(2):
                    ins = v.tensor_scalar(xT3[:, g, :], ps[:, 1, g * T:(g + 1) * T], colv[:, 5 + g:6 + g], None, ALU.mult)
                ins.then_inc(s["pool_ready"], 1)
                for j in range(NT):
                    dve.wait_ge(s["jobs_done"], l * 12 + j + 1)
                    b = ps[:, 2 + j, 0:H * ROPE].rearrange("p (h r) -> p h r", h=H)
                    q1, q2 = b[:, :, 0:HALF], b[:, :, HALF:ROPE]
                    o1, o2 = qr4[:, j, :, 0:HALF], qr4[:, j, :, HALF:ROPE]
                    co = cosv[:, j, :].unsqueeze(1).to_broadcast([P, H, HALF])
                    si = sinv[:, j, :].unsqueeze(1).to_broadcast([P, H, HALF])
                    v.tensor_tensor(o1, q1, co, ALU.mult)
                    v.tensor_tensor(o2, q2, co, ALU.mult)
                    link(v.tensor_tensor(rtmp[:, j], q2, si, ALU.mult))
                    link(v.tensor_tensor(o1, o1, rtmp[:, j], ALU.subtract))
                    v.tensor_tensor(rtmp[:, j], q1, si, ALU.mult).then_inc(s["jobsD_ready"], 1)
                    dve.wait_ge(s["jobsD_ready"], l * NT + j + 1)
                    v.tensor_tensor(o2, o2, rtmp[:, j], ALU.add).then_inc(s["qr_ready"], 1)
                dve.wait_ge(s["qrT_done"], l + 1)

                def scores(h):
                    dve.wait_ge(s["scores_done"], l * H + h + 1)
                    if h >= 2:
                        dve.wait_ge(s["pT_done"], l * H + h - 1)
                    link(v.tensor_tensor(sP[:, h % 2, :], ps[:, h, 0:3 * P], mask, ALU.add))
                    v.reduce_max(mx[:, h, 0:1], sP[:, h % 2, 0:P], AX_X)
                    link(v.reduce_max(mx[:, h, 1:2], sP[:, h % 2, P:3 * P], AX_X))
                    v.tensor_scalar(nmx[:, h, :], mx[:, h, :], -SCALE, None, ALU.mult).then_inc(s["s_ready"], 1)

                scores(0)
                for h in range(H):
                    if h + 1 < H:
                        scores(h + 1)
                    dve.wait_ge(s["exp_ready"], l * H + h + 1)
                    link(v.reciprocal(rsm[:, h, :], sm[:, h, :]))
                    v.tensor_scalar(sP[:, h % 2, 0:P], sP[:, h % 2, 0:P], rsm[:, h, 0:1], None, ALU.mult)
                    v.tensor_scalar(sP[:, h % 2, P:3 * P], sP[:, h % 2, P:3 * P], rsm[:, h, 1:2], None, ALU.mult).then_inc(s["probs_ready"], 1)

                def norm(which):
                    for j in range(NT):
                        link(v.tensor_tensor(t3[:, j, :], acc3[:, j].rearrange("p h n -> p (h n)"), g_row, ALU.mult))
                        link(v.scalar_tensor_tensor(t3[:, j, :], x3[:, j, :], ALPHA, t3[:, j, :], ALU.mult, ALU.add))
                        v.bn_stats(bn[:, j, 0:6], t3[:, j, 0:512])
                        link(v.bn_stats(bn[:, j, 6:12], t3[:, j, 512:D]), own=True)
                        ins = v.bn_aggr(mv[:, j, :], bn[:, j, :])
                    ins.then_inc(s["ln_stats"], 1)
                    dve.wait_ge(s["ln_std"], 2 * l + which + 1)
                    link(v.reciprocal(rstd, std))
                    v.scalar_tensor_tensor(nmr, mv[:, :, 0], -1.0, rstd, ALU.mult, ALU.mult).then_inc(s["ln_coef"], 1)
                    for j in range(NT):
                        dve.wait_ge(s["ln_norm"], (2 * l + which) * NT + j + 1)
                        link(v.tensor_tensor(x3[:, j, :], t3[:, j, :], lng_row, ALU.mult))
                        link(v.tensor_tensor(x3[:, j, :], x3[:, j, :], lnb_row, ALU.add))
                        if which == 0:
                            hv = h2p[:, j, :].rearrange("p (k q) -> p q k", k=KT)
                            xv = x3[:, j, :].rearrange("p (q k) -> p q k", k=KT)
                            link(v.tensor_tensor(hv, xv, sc_row.rearrange("p (q k) -> p q k", k=KT), ALU.mult))
                            v.tensor_tensor(hv, hv, sh_row.rearrange("p (q k) -> p q k", k=KT), ALU.add).then_inc(s["h2_ready"], 1)

                mod_value(2, slice(0, 64)).then_inc(s["mod_val_ready"], 1)
                dve.wait_ge(s["mix_done"], l + 2)
                dve.wait_ge(s["rows1_in"], (l + 1) * 80)
                norm(0)

                dve.wait_ge(s["esc_ready"], l + 1)
                dve.wait_ge(s["rbias_in"], (l + 1) * 16)
                link(v.tensor_scalar(score, score, 1.0, None, ALU.add))
                link(v.reciprocal(score, score))
                link(v.tensor_tensor(choice, score, rbias.unsqueeze(1).to_broadcast([P, NT, E]), ALU.add), own=True)
                ch = choice.rearrange("p j (g n) -> p (j g) n", g=NG)
                t2 = top2.rearrange("p (g n) -> p g n", n=8)
                for k in range(NT * NG):
                    ins = v.max(t2[:, k, :], ch[:, k, :])
                link(ins)
                link(v.tensor_tensor(gs.rearrange("p j g -> p (j g)"), t2[:, :, 0], t2[:, :, 1], ALU.add))
                other = gs.unsqueeze(2).to_broadcast([P, NT, NG, NG])
                own = gs.unsqueeze(3).to_broadcast([P, NT, NG, NG])
                lower = const[:, C_LT:C_LT + NG * NG].rearrange("p (a b) -> p a b", a=NG)
                v.tensor_tensor(cmp1, other, own, ALU.is_gt)
                link(v.tensor_tensor(cmp2, other, own, ALU.is_equal))
                for j in range(NT):
                    ins = v.tensor_tensor(cmp2[:, j], cmp2[:, j], lower, ALU.mult)
                link(ins)
                link(v.tensor_tensor(cmp1, cmp1, cmp2, ALU.add))
                link(v.tensor_reduce(grank, cmp1, AX_X, ALU.add))
                link(v.tensor_scalar(grank, grank, TOPG - 0.5, None, ALU.is_lt))
                link(v.tensor_scalar(gs, grank, -NEG, NEG, ALU.mult, ALU.add))
                m4 = masked.rearrange("p j (g n) -> p (j g) n", g=NG)
                keep = grank.rearrange("p j g -> p (j g)").unsqueeze(2).to_broadcast([P, NT * NG, 8])
                drop = gs.rearrange("p j g -> p (j g)").unsqueeze(2).to_broadcast([P, NT * NG, 8])
                link(v.tensor_tensor(m4, ch, keep, ALU.mult))
                link(v.tensor_tensor(m4, m4, drop, ALU.add), own=True)
                for j in range(NT):
                    ins = v.max(top8[:, j, :], masked[:, j, :])
                link(ins, own=True)
                for j in range(NT):
                    ins = v.match_replace(sel[:, j, :], top8[:, j, :], masked[:, j, :], -3e38)
                link(ins)
                v.tensor_tensor(sel, sel, masked, ALU.not_equal).then_inc(s["sel_ready"], 1)
                dve.wait_ge(s["sel_ready"], l + 1)
                link(v.tensor_tensor(G, sel, score, ALU.mult))
                link(v.tensor_reduce(gsum, G, AX_X, ALU.add))
                link(v.reciprocal(grec, gsum))
                for j in range(NT):
                    v.tensor_scalar(G[:, j, :], G[:, j, :], grec[:, j:j + 1], ROUTED, ALU.mult, ALU.mult)
                dve.wait_ge(s["shsil_ready"], l + 1)
                v.tensor_tensor(shmid.rearrange("p k t -> p (k t)"), shsil, ps[:, 6, :], ALU.mult).then_inc(s["shmid_ready"], 1)
                dve.wait_ge(s["rank_done"], l + 1)
                rk = ps[:, 7, 0:NT * E].rearrange("p (j e) -> p j e", j=NT)
                cnt = ps[0:1, 7, NT * E:NT * E + E]
                link(v.scalar_tensor_tensor(R, rk, 1024.0, sel, ALU.add, ALU.mult))
                v.tensor_scalar(R, R, -1024.0, None, ALU.add)
                link(v.tensor_scalar(kcnt, cnt, UNIT + 0.5, 1.0, ALU.is_gt, ALU.add))
                for k in range(2, T // UNIT):
                    link(v.tensor_scalar(kcnt2, cnt, k * UNIT + 0.5, None, ALU.is_gt))
                    link(v.tensor_tensor(kcnt, kcnt, kcnt2, ALU.add))
                link(v.tensor_reduce(kmax, kcnt.rearrange("p (r g) -> p r g", g=2), AX_X, ALU.max))
                link(v.tensor_tensor_scan(kcum[:, 0:E // 2], ones[0:1, 0:E // 2], kmax, ubase, ALU.mult, ALU.add))
                v.tensor_copy(btab[0:1, 1:E // 2 + 1], kcum[:, 0:E // 2])
                link(v.tensor_copy(btab[0:1, 0:1], ubase))
                v.tensor_copy(ubase, kcum[:, E // 2 - 1:E // 2]).then_inc(s["table_ready"], 1)
                dve.wait_ge(s["table_ready"], l + 1)
                passed(dve)

                with dve.Fori(0, E // RING) as i:
                    for q in range(2):
                        begin, end = blocks(dve, i * 2 + q)
                        with dve.Fori(begin, end) as b:
                            dve.wait_ge(s["sil_ready"], b + 1)
                            dve.wait_ge(s["midT_done"], b)
                            v.tensor_tensor(mid, sil, ps[:, B_F, F:2 * F], ALU.mult).then_inc(s["mid_ready"], 1)
                            dve.wait_ge(s["midT_done"], b + 1)
                            dve.wait_ge(s["down_done"], b * 2)
                            v.tensor_copy(midT.rearrange("p k n -> p (k n)"), ps[:, B_T, 0:FT * P]).then_inc(s["midT_ready"], 1)
                            dve.wait_ge(s["ST_done"], b + 1)
                            dve.wait_ge(s["scat_done"], b)
                            v.tensor_copy(ST, ps[:, B_T, 0:T]).then_inc(s["ST_ready"], 1)
                            dve.wait_ge(s["down_done"], b * 2 + 2)
                            v.tensor_copy(ysb[:, 512:D], ps[:, B_F, :]).then_inc(s["y1_ready"], 1)
                        for k in (2 * q, 2 * q + 1):
                            dve.sem_inc(w_free[k], 1)
                total = dve.value_load(btab[0:1, E // 2:E // 2 + 1], min_val=B0, max_val=MAXB)
                dve.wait_ge(s["scat_done"], total)
                dve.wait_ge(s["hT_ready"], (total + l + 1) * 2)
                dve.wait_ge(s["rows2_in"], (l + 1) * 48)
                norm(1)
                link(v.tensor_copy(std, rstd))
            assert links[1] == DVE_LINKS, links
            dve.sem_inc(s["layer_ready"], 1)


_INS = ["x", "c", "positions", "w_ada", "b_ada", "w_in", "q_norm_g", "kv_norm_g", "w_uq", "w_ukv", "w_pool",
        "pool_scale", "w_out", "ln1_g", "ln1_b", "w_router", "router_bias", "w_exp_gate", "w_exp_up",
        "w_exp_down", "w_sh_gate", "w_sh_up", "w_sh_down", "ln2_g", "ln2_b"]


def kernel(**inputs):
    import concourse.bacc as _bacc
    from concourse.bass_utils import run_bass_kernel_spmd as _run

    nc = _bacc.Bacc("TRN2", target_bir_lowering=False, num_devices=1)
    arrays, args = {}, []
    consts, band = shape_constants()
    for name in _INS + ["consts", "band"]:
        a = np.ascontiguousarray({"consts": consts, "band": band}[name] if name in ("consts", "band") else inputs[name])
        arrays[f"in_{name}"] = a
        args.append(nc.dram_tensor(f"in_{name}", a.shape, mybir.dt.from_np(a.dtype), kind="ExternalInput").ap())
    out = nc.dram_tensor("out_x", (1, T, D), F32, kind="ExternalOutput").ap()
    decoder_trunk(nc, *args, out)
    r = _run(nc, [arrays], core_ids=[0])
    return r.results[0]["out_x"]
```

```python
from contextlib import ExitStack

import numpy as np

import concourse.bass as bass
from concourse import mybir

P = 128
F32 = mybir.dt.float32
F32R = mybir.dt.float32r
I32 = mybir.dt.int32
ALU = mybir.AluOpType
ACT = mybir.ActivationFunctionType
AX_X = mybir.AxisListType.X

NT = 2
T = NT * P
D = 1024
KT = D // P
L = 2
assert L == 2
WINDOWS = (2, 4, 8, 16)
POOL = 256
QL, KVL, ROPE, NOPE, VH = 384, 256, 64, 128, 128
HALF = ROPE // 2
H = 6
INW = POOL + QL + KVL + ROPE
HW = INW // 2
QW = NOPE + ROPE
E, NG, TOPG, TOPK = 64, 8, 4, 8
F = 256
FT = F // P
PAIR_UNIT = P // 2
QUAD_UNIT = P // 4
CYCLE = 8
CYCLES = E // CYCLE
ROUNDS = 3
RING = 4
ALPHA = (2.0 * L) ** 0.25
LN_EPS, RMS_EPS = 1e-5, 1e-6
ROUTED = 2.5
SCALE = float(QW) ** -0.5
NEG = -1e30
ADA_W = 2048
ADA_PARTS = 6 * D // ADA_W
ADA_BUFS = 4
ADA_USES = ADA_PARTS * KT // ADA_BUFS
TWO_PI_PARTS = (6.28125, 0.0019350051879882812, 3.0199159819567396e-07)
MAGIC = 12582912.0
SLOT_W = 3 * KT * F
DVE_LINKS = 92
B0 = 1
MAXB = B0 + L * CYCLES * (2 * (T // PAIR_UNIT) + T // QUAD_UNIT)

C_ID = 0
C_GATE = C_ID + P
C_MASK = C_GATE + NT * 4
C_UP = C_MASK + 3 * P
C_ONE = C_UP + P
C_IOTA = C_ONE + P
C_FREQ = C_IOTA + PAIR_UNIT
C_LT = C_FREQ + HALF
C_KEY = C_LT + NG * NG
C_KEYC = C_KEY + E
C_NUM = C_KEYC + 1
C_ORDER = C_NUM + 1
C_WEIGHT = C_ORDER + E
C_STEP = C_WEIGHT + E
C_N = C_STEP + T // QUAD_UNIT


def shape_constants():
    c = np.zeros((P, C_N), np.float32)
    i = np.arange(P)
    c[:, C_ID:C_ID + P] = np.eye(P)
    causal = np.where(i[:, None] >= i[None, :], 0.0, NEG)
    c[:, C_MASK:C_MASK + P] = causal
    c[:, C_MASK + 2 * P:C_MASK + 3 * P] = causal
    c[:, C_UP:C_UP + P] = i[:, None] < i[None, :]
    c[:, C_ONE:C_ONE + P] = 1.0
    c[:, C_IOTA:C_IOTA + PAIR_UNIT] = np.arange(PAIR_UNIT)[None, :]
    order = np.zeros((CYCLES, CYCLE), np.int64)
    order[0, :4] = np.arange(4)
    for k in range(1, CYCLES):
        order[k, 0:2] = 2 + 2 * k + np.arange(2)
        order[k, 2:4] = E // 2 - 2 * k + np.arange(2)
    order[:, 4:] = E // 2 + np.arange(E // 2).reshape(CYCLES, 4)
    assert sorted(order.ravel()) == list(range(E))
    c[:, C_ORDER:C_ORDER + E] = order.reshape(1, E)
    c[:, C_WEIGHT:C_WEIGHT + E] = np.tile([1.0] * 4 + [2.0] * 4, CYCLES)[None, :]
    steps = np.arange(T // QUAD_UNIT) * PAIR_UNIT + 0.5
    steps[0] = -1.0
    c[:, C_STEP:C_STEP + T // QUAD_UNIT] = steps[None, :]
    c[:, C_FREQ:C_FREQ + HALF] = (10000.0 ** (-np.arange(HALF) / HALF)).astype(np.float32)[None, :]
    g = np.arange(NG)
    e = np.arange(P)
    key = (E - 1 - e) + np.where(e < RING, (RING - e) * 2.0 ** 20, 0.0)
    c[:, C_KEY:C_KEY + E] = key[None, :E]
    c[:, C_KEYC] = key
    c[:, C_NUM] = e
    c[:, C_LT:C_LT + NG * NG] = (g[None, :] < g[:, None]).astype(np.float32).reshape(1, -1)
    t = np.arange(T)
    band = np.zeros((len(WINDOWS), T, T), np.float32)
    for k, w in enumerate(WINDOWS):
        inside = (t[:, None] <= t[None, :]) & (t[:, None] > t[None, :] - w)
        band[k] = inside / np.minimum(t + 1, w)[None, :] - np.eye(T)
    first = band[:, :P, :].transpose(1, 0, 2).reshape(P, -1)
    second = band[:, P:, P:].transpose(1, 0, 2).reshape(P, -1)
    return c, np.ascontiguousarray(np.concatenate([first, second], axis=1).astype(np.float32))


def decoder_trunk(nc, x, c, positions, w_ada, b_ada, w_in, q_norm_g, kv_norm_g, w_uq, w_ukv, w_pool,
                  pool_scale, w_out, ln1_g, ln1_b, w_router, router_bias, w_exp_gate, w_exp_up,
                  w_exp_down, w_sh_gate, w_sh_up, w_sh_down, ln2_g, ln2_b, consts_dram, band_dram, out):
    mod_dram = nc.dram_tensor("mod_rows", (L, 6 * D), F32, kind="Internal").ap()
    ds = bass.ds

    with ExitStack() as ctx:
        ctx.enter_context(nc.allow_non_contiguous_dma(reason="short vectors laid on partitions"))

        def sb(name, cols, dt=F32, rows=P):
            return ctx.enter_context(nc.sbuf_tensor(name, [rows, cols], dt))

        def sem(name):
            return ctx.enter_context(nc.semaphore(name))

        ring = sb("ring", RING * SLOT_W)
        w1 = sb("w1", KT * D)
        w2 = sb("w2", 4560)
        scat = ctx.enter_context(nc.sbuf_tensor("scat", [P, T + 2 * D], F32R))
        router_sb = sb("router_sb", KT * E)
        x_sb = sb("x_sb", NT * D)
        xT = sb("xT", KT * T)
        rows = sb("rows", 5 * D)
        temp = sb("temp", 2 * D)
        const = sb("const", C_N)
        modl = sb("modl", 2 * KT)
        c32 = sb("c32", KT * 32)
        small = sb("small", 112)
        colv = sb("colv", 8)
        btab = sb("btab", CYCLES * ROUNDS + 1, I32, 1)
        otab = sb("otab", E, I32, 1)

        x3 = x_sb[:, :].rearrange("p (j d) -> p j d", j=NT)
        xT3 = xT[:, :].rearrange("p (k t) -> p k t", k=KT)
        t3 = temp[:, :].rearrange("p (j d) -> p j d", j=NT)
        g_row, lng_row, lnb_row, sc_row, sh_row = (rows[:, i * D:(i + 1) * D] for i in range(5))
        win3 = w1[:, 0:KT * INW].rearrange("p (k n) -> p k n", k=KT)
        wout3 = w1[:, :].rearrange("p (k n) -> p k n", k=KT)
        uq3 = w2[:, 0:3 * H * QW].rearrange("p (k n) -> p k n", k=3)
        ukv3 = ring[:, ADA_BUFS * ADA_W:ADA_BUFS * ADA_W + 2 * H * 256].rearrange("p (k n) -> p k n", k=2)
        router3 = router_sb[:, :].rearrange("p (k e) -> p k e", k=KT)
        ident = const[:, C_ID:C_ID + P]
        mask = const[:, C_MASK:C_MASK + 3 * P]
        upper = const[:, C_UP:C_UP + P]
        ones = const[:, C_ONE:C_ONE + P]
        freq = const[:, C_FREQ:C_FREQ + HALF]

        def gate_w(s):
            return ring[:, s * SLOT_W:s * SLOT_W + KT * F].rearrange("p (k f) -> p k f", k=KT)

        def up_w(s):
            return ring[:, s * SLOT_W + KT * F:s * SLOT_W + 2 * KT * F].rearrange("p (k f) -> p k f", k=KT)

        def down_w(s):
            return ring[:, s * SLOT_W + 2 * KT * F:(s + 1) * SLOT_W].rearrange("p (k d) -> p k d", k=FT)

        def gate_up(s):
            return ring[:, s * SLOT_W:s * SLOT_W + 2 * KT * F].rearrange("p (q k f) -> p q k f", q=2, k=KT)

        ada = [ring[:, s * ADA_W:(s + 1) * ADA_W].rearrange("p (g n) -> p g n", g=4) for s in range(ADA_BUFS)]
        c32v = c32[:, :].rearrange("p (k n) -> p k n", k=KT)
        mod_bias = [xT[:, 0:512], sc_row[:, 0:512], sh_row[:, 0:512]]
        mod_val = [xT[:, 512:1024], sc_row[:, 512:1024], sh_row[:, 512:1024]]

        at = [2 * SLOT_W]

        def carve(n):
            at[0] += n
            return ring[:, at[0] - n:at[0]]

        proj3 = carve(NT * INW).rearrange("p (j n) -> p j n", j=NT)
        qT3 = carve(H * T).rearrange("p (h t) -> p h t", h=H)
        qrT3 = carve(3 * T).rearrange("p (h t) -> p h t", h=3)
        kT3 = carve(H * T).rearrange("p (h t) -> p h t", h=H)
        krT3 = carve(2 * T).rearrange("p (v t) -> p v t", v=2)
        v3 = carve(NT * H * VH).rearrange("p (j n) -> p j n", j=NT)
        latT3 = carve(5 * T).rearrange("p (k t) -> p k t", k=5)
        band_sb = carve(len(WINDOWS) * (T + P))
        band0 = band_sb[:, 0:len(WINDOWS) * T].rearrange("p (g t) -> p g t", t=T)
        band1 = band_sb[:, len(WINDOWS) * T:].rearrange("p (g t) -> p g t", t=P)
        tmT3 = carve(2 * T).rearrange("p (g t) -> p g t", g=2)
        wpool3 = carve(2 * 64).rearrange("p (g d) -> p g d", g=2)
        assert at[0] <= RING * SLOT_W

        qr3 = t3[:, :, 0:H * ROPE]
        qr4 = qr3.rearrange("p j (h r) -> p j h r", h=H)
        krp = t3[:, :, 384:384 + 2 * P].rearrange("p j (v n) -> p j v n", v=2)
        rtmp = t3[:, :, 640:832].rearrange("p j (h r) -> p j h r", h=H)
        ktmp = t3[:, :, 832:864]
        sP = temp[:, 0:768].rearrange("p (b n) -> p b n", b=2)
        PT = temp[:, 768:1536].rearrange("p (b n) -> p b n", b=2)
        junk = temp[:, 1536:1536 + QL]

        mt = [0]

        def moe(n):
            mt[0] += n
            return w2[:, mt[0] - n:mt[0]]

        h2p = moe(NT * D).rearrange("p (j d) -> p j d", j=NT)
        hTb = moe(KT * P).rearrange("p (k n) -> p k n", k=KT)
        ST = scat[:, 0:T]
        y_hi, y_lo = scat[:, T:T + D], scat[:, T + D:]
        S = moe(NT * P).rearrange("p (j n) -> p j n", j=NT)
        sil = moe(F)
        mid = moe(F)
        midT = moe(FT * P).rearrange("p (k n) -> p k n", k=FT)
        R = moe(NT * E).rearrange("p (j e) -> p j e", j=NT)
        G = moe(NT * E).rearrange("p (j e) -> p j e", j=NT)
        Rc = moe(NT * 4).rearrange("p (j g) -> p j g", j=NT)
        Gc = const[:, C_GATE:C_GATE + NT * 4].rearrange("p (j g) -> p j g", j=NT)
        TW = P + NT * 4
        ident_gates = const[:, C_ID:C_ID + TW]
        gslot = moe(1)
        sel = moe(NT * E).rearrange("p (j e) -> p j e", j=NT)
        shmid = hTb[:, 0:4, :].rearrange("p k n -> p (k n)").rearrange("p (k t) -> p k t", k=FT)
        rbias = moe(E)
        assert mt[0] <= 4560
        shsil = temp[:, 1536:2048]

        def rt(i, n=NT * E):
            return temp[:, i:i + n]

        score = rt(0).rearrange("p (j e) -> p j e", j=NT)
        choice = rt(128).rearrange("p (j e) -> p j e", j=NT)
        top2 = rt(256)
        gs = rt(384, NT * NG).rearrange("p (j g) -> p j g", j=NT)
        grank = rt(400, NT * NG).rearrange("p (j g) -> p j g", j=NT)
        cmp1 = rt(512).rearrange("p (j a b) -> p j a b", j=NT, a=NG)
        cmp2 = rt(640).rearrange("p (j a b) -> p j a b", j=NT, a=NG)
        masked = rt(768).rearrange("p (j e) -> p j e", j=NT)
        top8 = rt(896, NT * 8).rearrange("p (j e) -> p j e", j=NT)
        gsum = rt(912, NT)
        grec = rt(914, NT)
        kabove = temp[0:1, 512:512 + E * (T // QUAD_UNIT)].rearrange("p (e k) -> p e k", e=E)
        kweighted = temp[0:1, 1160:1160 + E]
        kcnt = temp[0:1, 1024:1024 + E]
        kmax = temp[0:1, 1088:1088 + CYCLES * ROUNDS]
        kcum = temp[0:1, 1112:1112 + CYCLES * ROUNDS]
        key = rt(1260, E)
        above = rt(1324, E)
        place = rt(1388, E)
        ecol = rt(1452, 3)

        posi = small[:, 0:2].bitcast(I32)
        posf = small[:, 2:4]
        eps_ln = small[:, 4:5]
        eps_rms = small[:, 5:6]
        bn = small[:, 16:40].rearrange("p (j s) -> p j s", j=NT)
        mv = small[:, 40:44].rearrange("p (j s) -> p j s", j=NT)
        std = small[:, 44:46]
        rstd = small[:, 46:48]
        ssq = small[:, 50:54].rearrange("p (j s) -> p j s", j=NT)
        rms = small[:, 54:58].rearrange("p (j s) -> p j s", j=NT)
        mx = small[:, 60:72].rearrange("p (h s) -> p h s", h=H)
        nmx = small[:, 72:84].rearrange("p (h s) -> p h s", h=H)
        sm = small[:, 84:96].rearrange("p (h s) -> p h s", h=H)
        rsm = small[:, 96:108].rearrange("p (h s) -> p h s", h=H)
        ubase = small[0:1, 108:109]
        cs = sb("cs", NT * ROPE)
        cosv = cs[:, 0:NT * HALF].rearrange("p (j r) -> p j r", j=NT)
        sinv = cs[:, NT * HALF:].rearrange("p (j r) -> p j r", j=NT)
        c8 = temp[0:KT, 0:P]
        ang = temp[:, 512:512 + NT * HALF].rearrange("p (j r) -> p j r", j=NT)
        turns = temp[:, 576:576 + NT * HALF].rearrange("p (j r) -> p j r", j=NT)
        red = temp[:, 640:640 + NT * HALF].rearrange("p (j r) -> p j r", j=NT)

        ps = ctx.enter_context(nc.psum_tensor("ps", [P, 8, 512], F32))
        acc3 = ps[:, 0:4, :].rearrange("p (j h) n -> p j h n", j=NT)
        MOD_BANK = (7, 4, 7)
        B_F, B_T, B_0, B_1 = 4, 5, 6, 7

        names = """consts_in x_in c_in pos_in eps_set cT_done c32_ready bias_in mod1_summed mod_val_ready
        modT_done modl_ready mod_written
        rope_ready layer_ready xT_done xT_ready win_in proj_done projA_ready projD_ready ssq_ready std_ready
        lat_ready krp_ready band_in tm_done tm_ready lat_done latT_ready krT_done krT_ready vec_in wpool_in pool_done
        pool_ready w2_in jobs_done jobsA_ready jobsD_ready qr_ready qrT_done qrT_ready scores_done s_ready
        exp_ready probs_ready pT_done PT_ready pv_done pv_ready wout_in mix_done rows1_in rows2_in ln_stats
        ln_std folded fold_link x1_ready x2_ready h2_ready h2T_done h2T_ready router_in rbias_in logits_done esc_ready sh_up_done
        shsil_ready shmid_ready sel_ready sh_gate_done rank_done table_ready 
        sh_landed gu_half_done S_ready gath_done hT_ready gu_done sil_ready mid_ready midT_done midT_ready down_done
        ST_done ST_ready y0_ready y1_ready scat_done sh_free out_done ang_ready hi_ready place_ready order_done rc_ready pro_link
        dve_link waits_passed dist_ready""".split()
        s = {n: sem(n) for n in names}
        ada_landed = [sem(f"ada_landed{i}") for i in range(ADA_BUFS)]
        ada_used = [sem(f"ada_used{i}") for i in range(ADA_BUFS)]
        gu_landed = [[sem(f"gu_landed{half}_{i}") for i in range(RING // 2)] for half in range(2)]
        down_landed = [sem(f"down_landed{i}") for i in range(RING // 2)]

        def passed(eng):
            eng.sem_inc(s["waits_passed"], 1)

        def btab_value(eng, r):
            return eng.value_load(btab[0:1, ds(r, 1)], min_val=B0, max_val=MAXB)

        def blocks(eng, r):
            begin = btab_value(eng, r)
            return begin, btab_value(eng, r + 1)

        def placed(eng, place):
            return eng.value_load(otab[0:1, ds(place, 1)], min_val=0, max_val=E - 1)

        block = ctx.enter_context(nc.Block())

        def start_counts(eng, counts="", twice="", ones=()):
            for n in counts.split():
                eng.sem_inc(s[n], B0)
            for n in twice.split():
                eng.sem_inc(s[n], 2 * B0)
            for one in ones:
                eng.sem_inc(one, 1)

        @block.sync
        def _(sp):
            sp.dma_start(c8, c.rearrange("b (k p) -> (b k) p", p=P)).then_inc(s["c_in"], 16)
            sp.dma_start(const[:, :], consts_dram).then_inc(s["consts_in"], 16)
            sp.dma_start(posi, positions.rearrange("b (j p) -> p (b j)", p=P)).then_inc(s["pos_in"], 16)
            sp.dma_start(x3, x.rearrange("b (j p) d -> p (b j) d", p=P)).then_inc(s["x_in"], 16)
            def ada_tiles(l, first, end):
                for t in range(first, end):
                    part, kt = divmod(t, KT)
                    sp.wait_ge(ada_used[t % ADA_BUFS], l * ADA_USES + t // ADA_BUFS + 1)
                    src = w_ada[ds(l, 1), kt * P:(kt + 1) * P, part * ADA_W:(part + 1) * ADA_W]
                    sp.dma_start(ada[t % ADA_BUFS], src.rearrange("a p (g n) -> p (a g) n", g=4)).then_inc(ada_landed[t % ADA_BUFS], 16)

            def ada_bias(l, part):
                src = b_ada[ds(l, 1), part * ADA_W:(part + 1) * ADA_W]
                for g in range(4):
                    sp.dma_start(mod_bias[part][32 * g:32 * g + 32, :],
                                 src[:, g * 512:(g + 1) * 512].to_broadcast([32, 512])).then_inc(s["bias_in"], 16)

            def store_mod(l, part):
                sp.wait_ge(s["mod_val_ready"], l * 3 + part + 1)
                dst = mod_dram[ds(l, 1), part * ADA_W:(part + 1) * ADA_W].rearrange("a (g n) -> (a g) n", g=4)
                sp.dma_start(dst, mod_val[part][0:P:32, :]).then_inc(s["mod_written"], 16)
                sp.wait_ge(s["mod_written"], (l * 2 + part) * 16)

            def lay(w, l):
                return w[ds(l, 1)]

            def load_gate_up(l, half, slots, experts):
                kts = slice(half * KT // 2, (half + 1) * KT // 2)
                for slot, e in zip(slots, experts):
                    for dst, w in ((gate_w, w_exp_gate), (up_w, w_exp_up)):
                        src = w[ds(l, 1), ds(e, 1)].rearrange("a b (p k) f -> p (a b k) f", k=KT)
                        sp.dma_start(dst(slot)[:, kts, :], src[:, kts, :]).then_inc(gu_landed[half][slot // 2], 16)

            def load_down(l, slots, experts):
                for slot, e in zip(slots, experts):
                    sp.dma_start(down_w(slot), w_exp_down[ds(l, 1), ds(e, 1)].rearrange("a b (k p) d -> p (a b k) d", p=P)).then_inc(down_landed[slot // 2], 16)

            def row(dst, src, sm_):
                sp.dma_start(dst, src.to_broadcast([P, D])).then_inc(sm_, 16)

            def load_w_in(l):
                sp.dma_start(win3, lay(w_in, l).rearrange("a (k p) n -> p (a k) n", p=P)).then_inc(s["win_in"], 16)

            load_w_in(0)
            sp.wait_ge(s["table_ready"], 1)
            with sp.Fori(0, L) as l:
                def mod_row(dst, m, sm_):
                    row(dst, mod_dram[ds(l, 1), m * D:(m + 1) * D], sm_)

                sp.wait_ge(s["sh_free"], l + 1)
                ada_bias(l, 0)
                used = btab_value(sp, CYCLES * ROUNDS)
                sp.wait_ge(s["gu_done"], used)
                passed(sp)
                ada_tiles(l, 0, 2)
                sp.wait_ge(s["down_done"], used * 2)
                passed(sp)
                ada_tiles(l, 2, 4)
                ada_tiles(l, 4, 8)
                sp.wait_ge(s["layer_ready"], l + 1)
                ada_bias(l, 1)
                ada_bias(l, 2)
                sp.dma_start(colv[:, 0:3], lay(q_norm_g, l).rearrange("a (k p) -> p (a k)", p=P)).then_inc(s["vec_in"], 16)
                sp.dma_start(colv[:, 3:5], lay(kv_norm_g, l).rearrange("a (k p) -> p (a k)", p=P)).then_inc(s["vec_in"], 16)
                sp.dma_start(colv[:, 5:7], lay(pool_scale, l).rearrange("a (k p) -> p (a k)", p=P)).then_inc(s["vec_in"], 16)
                ada_tiles(l, 8, 16)
                sp.dma_start(band_sb, band_dram).then_inc(s["band_in"], 16)
                for g in range(2):
                    sp.dma_start(wpool3[:, g, :], w_pool[ds(l, 1), 2 * g:2 * g + 2].rearrange("a g c d -> (a g c) d")).then_inc(s["wpool_in"], 16)
                sp.dma_start(uq3, lay(w_uq, l).rearrange("a (k p) n -> p (a k) n", p=P)).then_inc(s["w2_in"], 16)
                sp.dma_start(ukv3, lay(w_ukv, l).rearrange("a (k p) n -> p (a k) n", p=P)).then_inc(s["w2_in"], 16)
                sp.wait_ge(s["proj_done"], l + 1)
                sp.dma_start(wout3, lay(w_out, l).rearrange("a (k p) n -> p (a k) n", p=P)).then_inc(s["wout_in"], 16)
                sp.dma_start(router3, lay(w_router, l).rearrange("a (p k) e -> p (a k) e", k=KT)).then_inc(s["router_in"], 16)
                row(lng_row, lay(ln1_g, l), s["rows1_in"])
                row(lnb_row, lay(ln1_b, l), s["rows1_in"])
                ada_tiles(l, 16, 20)
                store_mod(l, 1)
                mod_row(g_row, 2, s["rows1_in"])
                ada_tiles(l, 20, 24)
                store_mod(l, 2)
                mod_row(sc_row, 4, s["rows1_in"])
                mod_row(sh_row, 3, s["rows1_in"])
                sp.wait_ge(s["jobs_done"], (l + 1) * 12)
                sp.dma_start(rbias, lay(router_bias, l).to_broadcast([P, E])).then_inc(s["rbias_in"], 16)
                for half in range(2):
                    load_gate_up(l, half, (0, 1), (0, 1))
                load_down(l, (0, 1), (0, 1))
                sp.wait_ge(s["pv_ready"], (l + 1) * H)
                sp.dma_start(gate_w(3), lay(w_sh_gate, l).rearrange("a (p k) f -> p (a k) f", k=KT)).then_inc(s["sh_landed"], 16)
                sp.dma_start(up_w(3), lay(w_sh_up, l).rearrange("a (p k) f -> p (a k) f", k=KT)).then_inc(s["sh_landed"], 16)
                sp.dma_start(down_w(3), lay(w_sh_down, l).rearrange("a (k p) d -> p (a k) d", p=P)).then_inc(s["sh_landed"], 16)
                for half in range(2):
                    load_gate_up(l, half, (2,), (2,))
                load_down(l, (2,), (2,))
                sp.wait_ge(s["mix_done"], (l + 1) * NT * 2)
                passed(sp)
                with sp.If(l < L - 1):
                    load_w_in(L - 1)
                sp.wait_ge(s["x1_ready"], l + 1)
                mod_row(g_row, 5, s["rows2_in"])
                row(lng_row, lay(ln2_g, l), s["rows2_in"])
                row(lnb_row, lay(ln2_b, l), s["rows2_in"])
                sp.wait_ge(s["sh_up_done"], l + 1)
                passed(sp)
                for half in range(2):
                    load_gate_up(l, half, (3,), (3,))
                sp.wait_ge(s["sh_free"], l + 2)
                passed(sp)
                load_down(l, (3,), (3,))
                sp.wait_ge(s["table_ready"], l + 2)
                passed(sp)

                def refill(l, q, used_round, place):
                    used = btab_value(sp, used_round + 1)
                    experts = [placed(sp, place + g) for g in range(2)]
                    slots = (2 * q, 2 * q + 1)
                    sp.wait_ge(s["gu_half_done"], used)
                    passed(sp)
                    load_gate_up(l, 0, slots, experts)
                    sp.wait_ge(s["gu_done"], used)
                    passed(sp)
                    load_gate_up(l, 1, slots, experts)
                    sp.wait_ge(s["down_done"], used * 2)
                    passed(sp)
                    load_down(l, slots, experts)

                with sp.Fori(0, CYCLES - 1) as i:
                    for q in range(2):
                        refill(l, q, i * ROUNDS + q, i * CYCLE + 4 + 2 * q)
                    for q in range(2):
                        refill(l, q, i * ROUNDS + 2, i * CYCLE + CYCLE + 2 * q)
                for q in range(2):
                    refill(l, q, (CYCLES - 1) * ROUNDS + q, (CYCLES - 1) * CYCLE + 4 + 2 * q)
            for j in range(NT):
                sp.wait_ge(s["x2_ready"], (L - 1) * NT + j + 1)
                sp.dma_start(out[0, j * P:(j + 1) * P, :], x3[:, j, :]).then_inc(s["out_done"], 16)
            sp.wait_ge(s["out_done"], NT * 16)

        @block.tensor
        def _(pe):
            mm = nc.tensor.matmul
            tr = nc.tensor.transpose
            start_counts(pe, "gu_half_done gu_done midT_done ST_done scat_done", "gath_done down_done",
                         [s["sh_free"], *ada_used])

            pe.wait_ge(s["consts_in"], 16)
            pe.wait_ge(s["c_in"], 16)
            tr(ps[:, 4, 0:KT], c8, ident[0:KT, 0:KT]).then_inc(s["cT_done"], 1)
            pe.wait_ge(s["c32_ready"], 1)

            def modulation(l, part, kts=range(KT)):
                for kt in kts:
                    t = part * KT + kt
                    pe.wait_ge(ada_landed[t % ADA_BUFS], (l * ADA_USES + t // ADA_BUFS + 1) * 16)
                    passed(pe)
                    for g in range(4):
                        last = mm(ps[32 * g:32 * g + 32, MOD_BANK[part], :], c32v[:, kt, :], ada[t % ADA_BUFS][:, g, :],
                                  start=kt == 0, stop=kt == KT - 1)
                    last.then_inc(ada_used[t % ADA_BUFS], 1)

            with pe.Fori(0, L) as l:
                modulation(l, 0)
                pe.wait_ge(s["mod_val_ready"], l * 3 + 1)
                for k in range(4):
                    last = tr(ps[:, 6, k * P:(k + 1) * P], mod_val[0][:, k * P:(k + 1) * P], ident)
                last.then_inc(s["modT_done"], 1)
                pe.wait_ge(s["layer_ready"], l + 1)
                for kt in range(KT):
                    if kt == 4:
                        pe.wait_ge(s["modl_ready"], l + 1)
                    for j in range(NT):
                        last = tr(ps[:, 4 + kt // 2, (kt % 2) * T + j * P:(kt % 2) * T + (j + 1) * P],
                                  x3[:, j, kt * P:(kt + 1) * P], ident)
                    if kt % 2:
                        last.then_inc(s["xT_done"], 1)
                pe.wait_ge(s["win_in"], (l + 1) * 16)
                for kt in range(KT):
                    pe.wait_ge(s["xT_ready"], l * KT + kt + 1)
                    for j in range(NT):
                        for half in range(2):
                            last = mm(ps[:, 2 * j + half, 0:HW], xT3[:, kt, j * P:(j + 1) * P],
                                      win3[:, kt, half * HW:(half + 1) * HW], start=kt == 0, stop=kt == KT - 1)
                last.then_inc(s["proj_done"], 1)
                pe.wait_ge(ada_used[(2 * KT - 1) % ADA_BUFS], l * ADA_USES + (2 * KT - 1) // ADA_BUFS + 2)
                for g in range(4):
                    last = mm(ps[32 * g:32 * g + 32, MOD_BANK[1], :], ones[:, 0:32], temp[:, g * 512:(g + 1) * 512],
                              start=True, stop=True)
                last.then_inc(s["mod1_summed"], 1)
                pe.wait_ge(s["projA_ready"], l + 1)
                pe.wait_ge(s["projD_ready"], l + 1)
                pe.wait_ge(s["band_in"], (l + 1) * 16)
                for g in range(2):
                    for i in range(2):
                        o = ps[i * 64:(i + 1) * 64, 1, :]
                        u = 2 * g + i
                        mm(o[:, g * T:(g + 1) * T], proj3[:, 0, u * 64:(u + 1) * 64], band0[:, u, :], start=True, stop=False)
                        last = mm(o[:, g * T + P:(g + 1) * T], proj3[:, 1, u * 64:(u + 1) * 64], band1[:, u, :], start=False, stop=True)
                last.then_inc(s["tm_done"], 1)
                pe.wait_ge(s["lat_ready"], l + 1)
                for i in range(5):
                    for j in range(NT):
                        last = tr(ps[:, 5 + i // 2, (i % 2) * T + j * P:(i % 2) * T + (j + 1) * P],
                                  proj3[:, j, POOL + i * P:POOL + (i + 1) * P], ident)
                last.then_inc(s["lat_done"], 1)
                pe.wait_ge(s["krp_ready"], l + 1)
                for v in range(2):
                    for j in range(NT):
                        last = tr(ps[:, 0, v * T + j * P:v * T + (j + 1) * P], krp[:, j, v, :], ident)
                last.then_inc(s["krT_done"], 1)
                pe.wait_ge(s["tm_ready"], l + 1)
                pe.wait_ge(s["wpool_in"], (l + 1) * 32)
                passed(pe)
                for g in range(2):
                    for i in range(2):
                        q = slice(i * 64, (i + 1) * 64)
                        last = mm(ps[q, 1, g * T:(g + 1) * T], wpool3[q, g, :], tmT3[q, g, :], start=True, stop=True)
                last.then_inc(s["pool_done"], 1)
                pe.wait_ge(s["mod_val_ready"], l * 3 + 2)
                pe.wait_ge(s["w2_in"], (l + 1) * 32)
                pe.wait_ge(s["latT_ready"], (l + 1) * 5)

                def job_bank(n):
                    if n in (6, 7):
                        pe.wait_ge(s["jobsD_ready"], l * 2 + n - 5)
                    elif n >= 8:
                        pe.wait_ge(s["jobsA_ready"], l * 10 + n - 7)
                    return ps[:, 2 + n % 6, :]

                for j in range(NT):
                    o = job_bank(j)[:, 0:H * ROPE].rearrange("p (h r) -> p h r", h=H)
                    for kt in range(3):
                        w = uq3[:, kt, :].rearrange("p (h n) -> p h n", h=H)[:, :, NOPE:QW]
                        last = mm(o, latT3[:, kt, j * P:(j + 1) * P], w, start=kt == 0, stop=kt == 2)
                    last.then_inc(s["jobs_done"], 1)
                n = 2
                for hp in range(H // 2):
                    o = job_bank(n)
                    for i in range(2):
                        h = 2 * hp + i
                        for kt in range(3):
                            last = mm(o[:, i * T:(i + 1) * T], uq3[:, kt, h * QW:h * QW + NOPE], latT3[:, kt, :],
                                      start=kt == 0, stop=kt == 2)
                    last.then_inc(s["jobs_done"], 1)
                    n += 1
                for hp in range(H // 2):
                    o = job_bank(n)
                    for i in range(2):
                        h = 2 * hp + i
                        for kt in range(2):
                            last = mm(o[:, i * T:(i + 1) * T], ukv3[:, kt, h * 256:h * 256 + NOPE], latT3[:, 3 + kt, :],
                                      start=kt == 0, stop=kt == 1)
                    last.then_inc(s["jobs_done"], 1)
                    n += 1
                for j in range(NT):
                    for hh in range(2):
                        o = job_bank(n)[:, 0:3 * VH].rearrange("p (h n) -> p h n", h=3)
                        for kt in range(2):
                            w = ukv3[:, kt, :].rearrange("p (h n) -> p h n", h=H)[:, 3 * hh:3 * hh + 3, NOPE:256]
                            last = mm(o, latT3[:, 3 + kt, j * P:(j + 1) * P], w, start=kt == 0, stop=kt == 1)
                        last.then_inc(s["jobs_done"], 1)
                        n += 1
                pe.wait_ge(s["qr_ready"], (l + 1) * NT)
                pe.wait_ge(s["krT_ready"], l + 1)
                pe.wait_ge(s["pool_ready"], l + 1)
                for i in range(3):
                    for j in range(NT):
                        last = tr(ps[:, i // 2, (i % 2) * T + j * P:(i % 2) * T + (j + 1) * P],
                                  qr3[:, j, i * P:(i + 1) * P], ident)
                last.then_inc(s["qrT_done"], 1)
                pe.wait_ge(s["jobsA_ready"], (l + 1) * 10)
                modulation(l, 2, (0, 1))
                pe.wait_ge(s["qrT_ready"], l + 1)
                for h in range(H):
                    for j in range(NT):
                        o = ps[:, h, j * P:j * P + (j + 1) * P]
                        mm(o, qT3[:, h, j * P:(j + 1) * P], kT3[:, h, 0:(j + 1) * P], start=True, stop=False)
                        last = mm(o, qrT3[:, h // 2, j * P:(j + 1) * P], krT3[:, h % 2, 0:(j + 1) * P], start=False, stop=True)
                    last.then_inc(s["scores_done"], 1)

                def turn_probs(h):
                    pe.wait_ge(s["probs_ready"], l * H + h + 1)
                    for i in range(3):
                        last = tr(ps[:, h, i * P:(i + 1) * P], sP[:, h % 2, i * P:(i + 1) * P], ident)
                    last.then_inc(s["pT_done"], 1)

                modulation(l, 2, (2,))
                turn_probs(0)
                modulation(l, 2, (3,))
                for h in range(H):
                    if h + 1 < H:
                        turn_probs(h + 1)
                    if h < 4:
                        modulation(l, 2, (4 + h,))
                    pe.wait_ge(s["PT_ready"], l * H + h + 1)
                    v = [v3[:, j, h * VH:(h + 1) * VH] for j in range(NT)]
                    mm(ps[:, h, 0:P], v[0], PT[:, h % 2, 0:P], start=True, stop=True)
                    mm(ps[:, h, P:2 * P], v[0], PT[:, h % 2, P:2 * P], start=True, stop=False)
                    mm(ps[:, h, P:2 * P], v[1], PT[:, h % 2, 2 * P:3 * P], start=False, stop=True).then_inc(s["pv_done"], 1)
                pe.wait_ge(s["wout_in"], (l + 1) * 16)
                pe.wait_ge(s["pv_ready"], (l + 1) * H)
                for j in range(NT):
                    for half in range(2):
                        for kt in range(KT):
                            last = mm(acc3[:, j, half, :], xT3[:, kt, j * P:(j + 1) * P],
                                      wout3[:, kt, half * 512:(half + 1) * 512], start=kt == 0, stop=kt == KT - 1)
                        last.then_inc(s["mix_done"], 1)
                pe.wait_ge(s["mod_val_ready"], l * 3 + 3)
                for j in range(NT):
                    for kt in range(KT):
                        if kt % 4 == 0:
                            pe.wait_ge(s["h2_ready"], (l * NT + j) * 2 + kt // 4 + 1)
                        last = tr(ps[:, 4 + kt // 2, (kt % 2) * T + j * P:(kt % 2) * T + (j + 1) * P],
                                  h2p[:, j, kt * P:(kt + 1) * P], ident)
                        if kt % 2 and j == NT - 1:
                            last.then_inc(s["h2T_done"], 1)
                pe.wait_ge(s["h2T_ready"], (l + 1) * 4)
                pe.wait_ge(s["router_in"], (l + 1) * 16)
                for j in range(NT):
                    for kt in range(KT):
                        last = mm(ps[:, 4, j * E:(j + 1) * E], xT3[:, kt, j * P:(j + 1) * P], router3[:, kt, :],
                                  start=kt == 0, stop=kt == KT - 1)
                last.then_inc(s["logits_done"], 1)
                pe.wait_ge(s["sh_landed"], (l + 1) * 48)

                def shared(w, bank, f):
                    for kt in range(KT):
                        last = mm(ps[:, bank, f * T:(f + 1) * T], w[:, kt, f * P:(f + 1) * P], xT3[:, kt, :],
                                  start=kt == 0, stop=kt == KT - 1)
                    return last

                shared(gate_w(3), 5, 0)
                shared(gate_w(3), 5, 1).then_inc(s["sh_gate_done"], 1)
                pe.wait_ge(s["sel_ready"], l + 1)
                mm(ps[:, 7, 0:E], upper, sel[:, 0, :], start=True, stop=True)
                mm(ps[:, 7, E:2 * E], ones, sel[:, 0, :], start=True, stop=False)
                mm(ps[:, 7, E:2 * E], upper, sel[:, 1, :], start=False, stop=True)
                for j in range(NT):
                    mm(ps[0:E, 7, 2 * E:3 * E], ones[:, 0:E], sel[:, j, :], start=j == 0, stop=j == 1)
                for j in range(NT):
                    last = mm(ps[0:E, 7, 3 * E:3 * E + 1], sel[:, j, :], ones[:, 0:1], start=j == 0, stop=j == 1)
                last.then_inc(s["rank_done"], 1)
                shared(up_w(3), 6, 0)
                pe.wait_ge(s["place_ready"], l + 1)
                passed(pe)
                mm(ps[0:1, 7, 4 * E:5 * E], ecol[0:E, 2:3], place[0:E, :], start=True, stop=True)
                mm(ps[0:1, 7, 5 * E:6 * E], const[0:E, C_NUM:C_NUM + 1], place[0:E, :], start=True, stop=True).then_inc(s["order_done"], 1)
                shared(up_w(3), 6, 1).then_inc(s["sh_up_done"], 1)
                pe.wait_ge(s["shmid_ready"], l + 1)
                for f in range(FT):
                    for j in range(NT):
                        for half in range(2):
                            last = mm(acc3[:, j, half, :], shmid[:, f, j * P:(j + 1) * P],
                                      down_w(3)[:, f, half * 512:(half + 1) * 512], start=f == 0, stop=f == FT - 1)
                last.then_inc(s["sh_free"], 1)

                def gather(b, half, quarters=(0, 1)):
                    for kt in range(4 * half + 2 * quarters[0], 4 * half + 2 * quarters[-1] + 2):
                        for j in range(NT):
                            last = mm(ps[:, B_0 + half, (kt % 4) * P:(kt % 4 + 1) * P], h2p[:, j, kt * P:(kt + 1) * P],
                                      S[:, j, :], start=j == 0, stop=j == NT - 1)
                    if quarters[-1] == 1:
                        last.then_inc(s["gath_done"], 1)


                def turned(b):
                    for j in range(NT):
                        last = mm(ps[:, B_T, j * TW:(j + 1) * TW], S[:, j, :],
                                  ident_gates, start=True, stop=True)
                    last.then_inc(s["ST_done"], 1)

                pe.wait_ge(s["table_ready"], l + 2)
                pe.wait_ge(s["shmid_ready"], l + 1)
                passed(pe)
                b0 = pe.value_load(btab[0:1, 0:1], min_val=B0, max_val=MAXB)
                pe.wait_ge(s["S_ready"], b0 + l + 1)
                gather(b0, 0)
                turned(b0)
                gather(b0, 1)
                with pe.Fori(0, CYCLES) as i:
                    end = btab_value(pe, i * ROUNDS)
                    for rd, slots in enumerate(((0, 1), (2, 3), (0, 1, 2, 3))):
                        begin, end = end, btab_value(pe, i * ROUNDS + rd + 1)
                        unit = P // len(slots)
                        halves = (rd,) if rd < 2 else (0, 1)
                        loads = (l * CYCLES + i) * 2 + (1 if rd < 2 else 2)
                        for q in halves:
                            pe.wait_ge(gu_landed[0][q], loads * 64)
                        passed(pe)
                        with pe.Fori(begin, end) as b:
                            pe.wait_ge(s["hT_ready"], (b + l + 1) * 2)
                            pe.wait_ge(s["y1_ready"], b)
                            passed(pe)
                            for kt in range(KT):
                                if kt == KT // 2:
                                    last.then_inc(s["gu_half_done"], 1)
                                    for q in halves:
                                        pe.wait_ge(gu_landed[1][q], loads * 64)
                                    passed(pe)
                                for g, k in enumerate(slots):
                                    last = mm(ps[unit * g:unit * g + unit, B_F, :].rearrange("p (q f) -> p q f", q=2),
                                              hTb[:, kt, unit * g:unit * g + unit], gate_up(k)[:, :, kt, :],
                                              start=kt == 0, stop=kt == KT - 1)
                            last.then_inc(s["gu_done"], 1)
                            pe.wait_ge(s["S_ready"], b + l + 2)
                            gather(b + 1, 0, (0,))
                            pe.wait_ge(s["mid_ready"], b + 1)
                            pe.wait_ge(s["ST_ready"], b + l + 1)
                            for f in range(FT):
                                last = tr(ps[:, B_T, f * P:(f + 1) * P], mid[:, f * P:(f + 1) * P], ident)
                            last.then_inc(s["midT_done"], 1)
                            gather(b + 1, 0, (1,))

                            def down(half, bank):
                                for f in range(FT):
                                    for g, k in enumerate(slots):
                                        last = mm(ps[unit * g:unit * g + unit, bank, :], midT[:, f, unit * g:unit * g + unit],
                                                  down_w(k)[:, f, half * 512:(half + 1) * 512], start=f == 0, stop=f == FT - 1)
                                last.then_inc(s["down_done"], 1)

                            for q in halves:
                                pe.wait_ge(down_landed[q], loads * 32)
                            passed(pe)
                            pe.wait_ge(s["midT_ready"], b + 1)
                            down(0, B_1)
                            turned(b + 1)
                            down(1, B_F)
                            pe.wait_ge(s["y0_ready"], b + 1)
                            gather(b + 1, 1)
                            for half in range(2):
                                if half == 1:
                                    pe.wait_ge(s["y1_ready"], b + 1)
                                for j in range(NT):
                                    for part in (y_hi, y_lo):
                                        last = mm(acc3[:, j, half, :], ST[:, j * P:(j + 1) * P],
                                                  part[:, half * 512:(half + 1) * 512], start=False, stop=True,
                                                  skip_group_check=True)
                            last.then_inc(s["scat_done"], 1)
                last = btab_value(pe, CYCLES * ROUNDS)
                pe.wait_ge(s["hT_ready"], (last + l + 1) * 2)

        @block.scalar
        def _(act):
            fn = nc.scalar.activation
            start_counts(act, "sil_ready", "hT_ready")
            act.wait_ge(s["cT_done"], 1)
            fn(c32v, ps[:, 4, 0:KT].unsqueeze(2).to_broadcast([P, KT, 32]), ACT.Silu).then_inc(s["c32_ready"], 1)
            act.wait_ge(s["ang_ready"], 1)
            fn(sinv, ang, ACT.Sin)
            fn(cosv, red, ACT.Sin).then_inc(s["rope_ready"], 1)

            with act.Fori(0, L) as l:
                act.wait_ge(s["modl_ready"], l + 1)
                for kt in range(KT):
                    act.wait_ge(s["xT_done"], l * (KT // 2) + kt // 2 + 1)
                    fn(xT3[:, kt, :], ps[:, 4 + kt // 2, (kt % 2) * T:(kt % 2 + 1) * T], ACT.Identity,
                       scale=modl[:, KT + kt:KT + kt + 1], bias=modl[:, kt:kt + 1]).then_inc(s["xT_ready"], 1)
                act.wait_ge(s["proj_done"], l + 1)
                fn(proj3[:, 0, :].rearrange("p (b n) -> p b n", b=2), ps[:, 0:2, 0:HW], ACT.Copy).then_inc(s["projA_ready"], 1)
                act.wait_ge(s["mod1_summed"], l + 1)
                act.wait_ge(s["projA_ready"], l + 1)
                act.wait_ge(s["projD_ready"], l + 1)
                for j in range(NT):
                    fn(junk, proj3[:, j, POOL:POOL + QL], ACT.Square, accum_out=ssq[:, j, 0:1]).then_inc(s["ssq_ready"], 1)
                    act.wait_ge(s["ssq_ready"], l * 4 + 2 * j + 1)
                    fn(junk[:, 0:KVL], proj3[:, j, POOL + QL:POOL + QL + KVL], ACT.Square, accum_out=ssq[:, j, 1:2]).then_inc(s["ssq_ready"], 1)
                    act.wait_ge(s["ssq_ready"], l * 4 + 2 * j + 2)
                fn(rms[:, :, 0], ssq[:, :, 0], ACT.Sqrt, scale=1.0 / QL, bias=eps_rms)
                fn(rms[:, :, 1], ssq[:, :, 1], ACT.Sqrt, scale=1.0 / KVL, bias=eps_rms).then_inc(s["std_ready"], 1)
                act.wait_ge(s["lat_done"], l + 1)
                act.wait_ge(s["vec_in"], (l + 1) * 48)
                for k in range(5):
                    fn(latT3[:, k, :], ps[:, 5 + k // 2, (k % 2) * T:(k % 2 + 1) * T], ACT.Copy,
                       scale=colv[:, k:k + 1]).then_inc(s["latT_ready"], 1)
                act.wait_ge(s["krT_done"], l + 1)
                fn(krT3, ps[:, 0, :].rearrange("p (v t) -> p v t", v=2), ACT.Copy).then_inc(s["krT_ready"], 1)
                for n in range(2, 12):
                    act.wait_ge(s["jobs_done"], l * 12 + n + 1)
                    b = ps[:, 2 + n % 6, :]
                    if n < 5:
                        dst, src = qT3[:, 2 * (n - 2):2 * (n - 2) + 2, :], b.rearrange("p (h t) -> p h t", h=2)
                    elif n < 8:
                        dst, src = kT3[:, 2 * (n - 5):2 * (n - 5) + 2, :], b.rearrange("p (h t) -> p h t", h=2)
                    else:
                        j, hh = divmod(n - 8, 2)
                        dst, src = v3[:, j, hh * 3 * VH:(hh + 1) * 3 * VH], b[:, 0:3 * VH]
                    fn(dst, src, ACT.Copy).then_inc(s["jobsA_ready"], 1)
                act.wait_ge(s["qrT_done"], l + 1)
                fn(qrT3.rearrange("p h t -> p (h t)"), ps[:, 0:2, :].rearrange("p b n -> p (b n)")[:, 0:3 * T], ACT.Copy).then_inc(s["qrT_ready"], 1)

                def exps(h):
                    act.wait_ge(s["s_ready"], l * H + h + 1)
                    fn(sP[:, h % 2, 0:P], sP[:, h % 2, 0:P], ACT.Exp, scale=SCALE, bias=nmx[:, h, 0:1], accum_out=sm[:, h, 0:1])
                    fn(sP[:, h % 2, P:3 * P], sP[:, h % 2, P:3 * P], ACT.Exp, scale=SCALE, bias=nmx[:, h, 1:2],
                       accum_out=sm[:, h, 1:2]).then_inc(s["exp_ready"], 1)

                def mixed(h):
                    act.wait_ge(s["pv_done"], l * H + h + 1)
                    fn(xT3[:, 2 + h, :], ps[:, h, 0:T], ACT.Copy).then_inc(s["pv_ready"], 1)

                exps(0)
                for h in range(H):
                    if h + 1 < H:
                        exps(h + 1)
                    act.wait_ge(s["pT_done"], l * H + h + 1)
                    if h >= 2:
                        act.wait_ge(s["pv_done"], l * H + h - 1)
                    fn(PT[:, h % 2, :], ps[:, h, 0:3 * P], ACT.Copy).then_inc(s["PT_ready"], 1)
                    if h >= 1:
                        mixed(h - 1)
                mixed(H - 1)

                def norm(which):
                    for j in range(NT):
                        count = (2 * l + which) * NT + j + 1
                        act.wait_ge(s["ln_stats"], count)
                        fn(std[:, j:j + 1], mv[:, j, 1:2], ACT.Sqrt, bias=eps_ln).then_inc(s["ln_std"], 1)

                norm(0)
                for b in range(4):
                    act.wait_ge(s["h2T_done"], l * 4 + b + 1)
                    fn(xT3[:, 2 * b:2 * b + 2, :], ps[:, 4 + b, :].rearrange("p (k t) -> p k t", k=2), ACT.Copy).then_inc(s["h2T_ready"], 1)
                act.wait_ge(s["x1_ready"], l + 1)
                act.wait_ge(s["logits_done"], l + 1)
                fn(score.rearrange("p j e -> p (j e)"), ps[:, 4, 0:NT * E], ACT.Exp, scale=-1.0).then_inc(s["esc_ready"], 1)
                act.wait_ge(s["sh_gate_done"], l + 1)
                fn(shsil, ps[:, 5, :], ACT.Silu).then_inc(s["shsil_ready"], 1)

                def gathered(b, half):
                    act.wait_ge(s["gath_done"], (b + l) * 2 + half + 1)
                    fn(hTb[:, 4 * half:4 * half + 4, :], ps[:, B_0 + half, :].rearrange("p (k n) -> p k n", k=4), ACT.Copy).then_inc(s["hT_ready"], 1)

                act.wait_ge(s["table_ready"], l + 2)
                passed(act)
                b0 = act.value_load(btab[0:1, 0:1], min_val=B0, max_val=MAXB)
                gathered(b0, 0)
                gathered(b0, 1)
                with act.Fori(0, CYCLES * ROUNDS) as r:
                    begin, end = blocks(act, r)
                    with act.Fori(begin, end) as b:
                        act.wait_ge(s["gu_done"], b + 1)
                        act.wait_ge(s["mid_ready"], b)
                        fn(sil, ps[:, B_F, 0:F], ACT.Silu).then_inc(s["sil_ready"], 1)
                        gathered(b + 1, 0)
                        gathered(b + 1, 1)
                norm(1)

        @block.gpsimd
        def _(pool):
            eng = nc.gpsimd
            start_counts(pool, "S_ready rc_ready dist_ready")
            eng.memset(eps_ln, LN_EPS)
            eng.memset(eps_rms, RMS_EPS).then_inc(s["eps_set"], 1)
            pool.wait_ge(s["consts_in"], 16)
            with pool.Fori(0, L) as l:
                def one_hot(count, n):
                    shape = [P, NT, n, P // n]
                    iota = const[:, C_IOTA:C_IOTA + P // n].unsqueeze(1).unsqueeze(1).to_broadcast(shape)
                    eng.tensor_tensor(S.rearrange("p j (g n) -> p j g n", g=n), iota,
                                      Rc[:, :, 0:n].unsqueeze(3).to_broadcast(shape), ALU.subtract).then_inc(s["dist_ready"], 1)
                    pool.wait_ge(s["dist_ready"], count)
                    passed(pool)
                    return eng.tensor_scalar(S, S, 0.0, None, ALU.is_equal)

                product = hTb.rearrange("p k n -> p (k n)")
                pool.wait_ge(s["rows1_in"], (l + 1) * 80)
                pool.wait_ge(s["jobs_done"], (l + 1) * 12)
                passed(pool)
                eng.tensor_tensor(product, lnb_row, sc_row, ALU.mult).then_inc(s["fold_link"], 1)
                pool.wait_ge(s["fold_link"], l + 1)
                passed(pool)
                eng.tensor_tensor(sh_row, sh_row, product, ALU.add)
                eng.tensor_tensor(sc_row, sc_row, lng_row, ALU.mult).then_inc(s["folded"], 1)

                pool.wait_ge(s["table_ready"], l + 2)
                passed(pool)
                with pool.Fori(0, CYCLES) as i:
                    end = btab_value(pool, i * ROUNDS)
                    for rd in range(ROUNDS):
                        begin, end = end, btab_value(pool, i * ROUNDS + rd + 1)
                        copies = l * (CYCLES * ROUNDS) + i * ROUNDS + rd
                        experts = [placed(pool, i * CYCLE + 2 * rd + g) for g in range(2 if rd < 2 else 4)]
                        pool.wait_ge(s["ST_done"], begin + l)
                        pool.wait_ge(s["rc_ready"], copies + begin)
                        passed(pool)
                        width = 4 // len(experts)
                        for g, e in enumerate(experts):
                            cols = slice(g * width, (g + 1) * width)
                            eng.tensor_copy(Gc[:, :, cols], G[:, :, ds(e, 1)].to_broadcast([P, NT, width]))
                            last = eng.tensor_copy(Rc[:, :, g:g + 1], R[:, :, ds(e, 1)])
                        last.then_inc(s["rc_ready"], 1)
                        with pool.Fori(begin, end) as b:
                            pool.wait_ge(s["rc_ready"], copies + 1 + b)
                            pool.wait_ge(s["gath_done"], (b + l) * 2)
                            one_hot(b + l + 1, len(experts)).then_inc(s["S_ready"], 1)
                            eng.tensor_scalar(Rc[:, :, 0:len(experts)], Rc[:, :, 0:len(experts)], -float(width * QUAD_UNIT), None, ALU.add).then_inc(s["rc_ready"], 1)
                last = btab_value(pool, CYCLES * ROUNDS)
                pool.wait_ge(s["rc_ready"], (l + 1) * (CYCLES * ROUNDS) + last)
                pool.wait_ge(s["gath_done"], (last + l) * 2)
                one_hot(last + l + 1, 4).then_inc(s["S_ready"], 1)

        @block.vector
        def _(dve):
            v = nc.vector
            links = [0, 0]
            start_counts(dve, "mid_ready midT_ready ST_ready y0_ready y1_ready", "hi_ready")

            def plink(ins):
                links[0] += 1
                ins.then_inc(s["pro_link"], 1)
                dve.wait_ge(s["pro_link"], links[0])

            plink(v.memset(ubase, float(B0)))
            v.tensor_copy(btab[0:1, CYCLES * ROUNDS:CYCLES * ROUNDS + 1], ubase).then_inc(s["table_ready"], 1)
            dve.wait_ge(s["pos_in"], 16)
            dve.wait_ge(s["consts_in"], 16)
            plink(v.tensor_copy(posf, posi))
            for j in range(NT):
                ins = v.tensor_scalar(ang[:, j, :], freq, posf[:, j:j + 1], None, ALU.mult)
            plink(ins)

            def reduce_angle(dst, quarter):
                plink(v.tensor_scalar(turns, ang, 0.15915494309189535, 0.25 * quarter, ALU.mult, ALU.add))
                plink(v.tensor_scalar(turns, turns, MAGIC, None, ALU.add))
                plink(v.tensor_scalar(turns, turns, -MAGIC, None, ALU.add))
                src = ang
                for part in TWO_PI_PARTS:
                    plink(v.scalar_tensor_tensor(dst, turns, -part, src, ALU.mult, ALU.add))
                    src = dst
                if quarter:
                    plink(v.tensor_scalar(dst, dst, 1.5707963267948966, None, ALU.add))
                return v.tensor_scalar(dst, dst, 3.1415925, -3.1415925, ALU.min, ALU.max)

            plink(reduce_angle(red, 1))
            reduce_angle(ang, 0).then_inc(s["ang_ready"], 1)
            dve.wait_ge(s["rope_ready"], 1)
            dve.wait_ge(s["eps_set"], 1)
            dve.wait_ge(s["c32_ready"], 1)
            dve.wait_ge(s["x_in"], 16)

            with dve.Fori(0, L) as l:
                def link(ins, own=False):
                    links[1] += 1
                    ins.then_inc(s["dve_link"], 1)
                    dve.wait_ge(s["dve_link"], l * DVE_LINKS + links[1])
                    if own:
                        passed(dve)

                def mod_value(part, plus_one):
                    if part == 1:
                        dve.wait_ge(s["mod1_summed"], l + 1)
                    else:
                        dve.wait_ge(ada_used[(part * KT + KT - 1) % ADA_BUFS], l * ADA_USES + (part * KT + KT - 1) // ADA_BUFS + 2)
                    dve.wait_ge(s["bias_in"], (l * 3 + part + 1) * 64)
                    first = v.tensor_tensor(mod_val[part], ps[:, MOD_BANK[part], :], mod_bias[part], ALU.add)
                    if plus_one is None:
                        return first
                    link(first)
                    return v.tensor_scalar(mod_val[part][plus_one, :], mod_val[part][plus_one, :], 1.0, None, ALU.add)

                dve.sem_inc(s["layer_ready"], 1)
                mod_value(0, slice(64, 128)).then_inc(s["mod_val_ready"], 1)
                dve.wait_ge(s["modT_done"], l + 1)
                v.tensor_copy(modl[:, :].rearrange("p (g k) -> p g k", g=4),
                              ps[:, 6, :].rearrange("p (k g n) -> p g k n", k=4, g=4)[:, :, :, 0]).then_inc(s["modl_ready"], 1)
                for kt in range(KT):
                    buf, use = (KT + kt) % ADA_BUFS, l * ADA_USES + (KT + kt) // ADA_BUFS
                    dve.wait_ge(ada_landed[buf], (use + 1) * 16)
                    passed(dve)
                    tile = ada[buf].rearrange("p g n -> p (g n)")
                    if kt == 0:
                        ins = v.tensor_scalar(temp[:, :], tile, c32v[:, kt, 0:1], None, ALU.mult)
                    else:
                        ins = v.scalar_tensor_tensor(temp[:, :], tile, c32v[:, kt, 0:1], temp[:, :], ALU.mult, ALU.add)
                    ins.then_inc(ada_used[buf], 1)
                    dve.wait_ge(ada_used[buf], use + 2)
                dve.wait_ge(s["proj_done"], l + 1)
                v.tensor_copy(proj3[:, 1, :].rearrange("p (b n) -> p b n", b=2), ps[:, 2:4, 0:HW]).then_inc(s["projD_ready"], 1)
                dve.wait_ge(s["std_ready"], l + 1)
                link(v.reciprocal(ssq, rms))
                for j in range(NT):
                    for a, n, k in ((POOL, QL, 0), (POOL + QL, KVL, 1)):
                        ins = v.tensor_scalar(proj3[:, j, a:a + n], proj3[:, j, a:a + n], ssq[:, j, k:k + 1], None, ALU.mult)
                ins.then_inc(s["lat_ready"], 1)
                dve.wait_ge(s["mod1_summed"], l + 1)
                k1, k2 = proj3[:, :, INW - ROPE:INW - HALF], proj3[:, :, INW - HALF:INW]
                o1, o2 = krp[:, :, 0, 0:HALF], krp[:, :, 0, HALF:ROPE]
                v.memset(krp[:, :, 0, ROPE:P], 0.0)
                v.memset(krp[:, :, 1, 0:ROPE], 0.0)
                v.tensor_tensor(o1, k1, cosv, ALU.mult)
                v.tensor_tensor(o2, k2, cosv, ALU.mult)
                link(v.tensor_tensor(ktmp, k2, sinv, ALU.mult))
                link(v.tensor_tensor(o1, o1, ktmp, ALU.subtract))
                link(v.tensor_tensor(ktmp, k1, sinv, ALU.mult))
                link(v.tensor_tensor(o2, o2, ktmp, ALU.add))
                v.tensor_copy(krp[:, :, 1, ROPE:P], krp[:, :, 0, 0:ROPE]).then_inc(s["krp_ready"], 1)
                mod_value(1, None).then_inc(s["mod_val_ready"], 1)
                dve.wait_ge(s["tm_done"], l + 1)
                v.tensor_copy(tmT3, ps[:, 1, :].rearrange("p (g t) -> p g t", g=2)).then_inc(s["tm_ready"], 1)
                dve.wait_ge(s["pool_done"], l + 1)
                dve.wait_ge(s["vec_in"], (l + 1) * 48)
                for g in range(2):
                    ins = v.tensor_scalar(xT3[:, g, :], ps[:, 1, g * T:(g + 1) * T], colv[:, 5 + g:6 + g], None, ALU.mult)
                ins.then_inc(s["pool_ready"], 1)
                for j in range(NT):
                    dve.wait_ge(s["jobs_done"], l * 12 + j + 1)
                    b = ps[:, 2 + j, 0:H * ROPE].rearrange("p (h r) -> p h r", h=H)
                    q1, q2 = b[:, :, 0:HALF], b[:, :, HALF:ROPE]
                    o1, o2 = qr4[:, j, :, 0:HALF], qr4[:, j, :, HALF:ROPE]
                    co = cosv[:, j, :].unsqueeze(1).to_broadcast([P, H, HALF])
                    si = sinv[:, j, :].unsqueeze(1).to_broadcast([P, H, HALF])
                    v.tensor_tensor(o1, q1, co, ALU.mult)
                    v.tensor_tensor(o2, q2, co, ALU.mult)
                    link(v.tensor_tensor(rtmp[:, j], q2, si, ALU.mult))
                    link(v.tensor_tensor(o1, o1, rtmp[:, j], ALU.subtract))
                    v.tensor_tensor(rtmp[:, j], q1, si, ALU.mult).then_inc(s["jobsD_ready"], 1)
                    dve.wait_ge(s["jobsD_ready"], l * NT + j + 1)
                    v.tensor_tensor(o2, o2, rtmp[:, j], ALU.add).then_inc(s["qr_ready"], 1)
                dve.wait_ge(s["qrT_done"], l + 1)

                def scores(h):
                    dve.wait_ge(s["scores_done"], l * H + h + 1)
                    if h >= 2:
                        dve.wait_ge(s["pT_done"], l * H + h - 1)
                    link(v.tensor_tensor(sP[:, h % 2, :], ps[:, h, 0:3 * P], mask, ALU.add))
                    v.reduce_max(mx[:, h, 0:1], sP[:, h % 2, 0:P], AX_X)
                    link(v.reduce_max(mx[:, h, 1:2], sP[:, h % 2, P:3 * P], AX_X))
                    v.tensor_scalar(nmx[:, h, :], mx[:, h, :], -SCALE, None, ALU.mult).then_inc(s["s_ready"], 1)

                scores(0)
                for h in range(H):
                    if h + 1 < H:
                        scores(h + 1)
                    dve.wait_ge(s["exp_ready"], l * H + h + 1)
                    link(v.reciprocal(rsm[:, h, :], sm[:, h, :]))
                    v.tensor_scalar(sP[:, h % 2, 0:P], sP[:, h % 2, 0:P], rsm[:, h, 0:1], None, ALU.mult)
                    v.tensor_scalar(sP[:, h % 2, P:3 * P], sP[:, h % 2, P:3 * P], rsm[:, h, 1:2], None, ALU.mult).then_inc(s["probs_ready"], 1)

                def norm_stats(which, j):
                    for half in range(2):
                        q = slice(half * 512, (half + 1) * 512)
                        if which == 0:
                            dve.wait_ge(s["mix_done"], (l * NT + j) * 2 + half + 1)
                        link(v.tensor_tensor(t3[:, j, q], acc3[:, j, half, :], g_row[:, q], ALU.mult))
                        link(v.scalar_tensor_tensor(t3[:, j, q], x3[:, j, q], ALPHA, t3[:, j, q], ALU.mult, ALU.add))
                        ins = v.bn_stats(bn[:, j, 6 * half:6 * half + 6], t3[:, j, q])
                    link(ins, own=True)
                    v.bn_aggr(mv[:, j, :], bn[:, j, :]).then_inc(s["ln_stats"], 1)

                def normalise(which, j):
                    dve.wait_ge(s["ln_std"], (2 * l + which) * NT + j + 1)
                    link(v.reciprocal(rstd[:, j:j + 1], std[:, j:j + 1]))
                    link(v.tensor_scalar(t3[:, j, :], t3[:, j, :], mv[:, j, 0:1], rstd[:, j:j + 1], ALU.subtract, ALU.mult))

                def norm_x(j):
                    link(v.tensor_tensor(x3[:, j, :], t3[:, j, :], lng_row, ALU.mult))
                    return v.tensor_tensor(x3[:, j, :], x3[:, j, :], lnb_row, ALU.add)

                mod_value(2, slice(0, 64)).then_inc(s["mod_val_ready"], 1)
                dve.wait_ge(s["rows1_in"], (l + 1) * 80)
                for j in range(NT):
                    norm_stats(0, j)
                    normalise(0, j)
                    dve.wait_ge(s["folded"], l + 1)
                    nv, gain, offset = (r.rearrange("p (q k) -> p q k", k=KT) for r in (t3[:, j, :], sc_row, sh_row))
                    for part in range(2):
                        ks = slice(part * KT // 2, (part + 1) * KT // 2)
                        hv = h2p[:, j, :].rearrange("p (k q) -> p q k", k=KT)[:, :, ks]
                        link(v.tensor_tensor(hv, nv[:, :, ks], gain[:, :, ks], ALU.mult))
                        v.tensor_tensor(hv, hv, offset[:, :, ks], ALU.add).then_inc(s["h2_ready"], 1)
                norm_x(0)
                norm_x(1).then_inc(s["x1_ready"], 1)

                dve.wait_ge(s["esc_ready"], l + 1)
                dve.wait_ge(s["rbias_in"], (l + 1) * 16)
                link(v.tensor_scalar(score, score, 1.0, None, ALU.add))
                link(v.reciprocal(score, score))
                link(v.tensor_tensor(choice, score, rbias.unsqueeze(1).to_broadcast([P, NT, E]), ALU.add), own=True)
                ch = choice.rearrange("p j (g n) -> p (j g) n", g=NG)
                t2 = top2.rearrange("p (g n) -> p g n", n=8)
                for k in range(NT * NG):
                    ins = v.max(t2[:, k, :], ch[:, k, :])
                link(ins)
                link(v.tensor_tensor(gs.rearrange("p j g -> p (j g)"), t2[:, :, 0], t2[:, :, 1], ALU.add))
                other = gs.unsqueeze(2).to_broadcast([P, NT, NG, NG])
                own = gs.unsqueeze(3).to_broadcast([P, NT, NG, NG])
                lower = const[:, C_LT:C_LT + NG * NG].rearrange("p (a b) -> p a b", a=NG)
                v.tensor_tensor(cmp1, other, own, ALU.is_gt)
                link(v.tensor_tensor(cmp2, other, own, ALU.is_equal))
                for j in range(NT):
                    ins = v.tensor_tensor(cmp2[:, j], cmp2[:, j], lower, ALU.mult)
                link(ins)
                link(v.tensor_tensor(cmp1, cmp1, cmp2, ALU.add))
                link(v.tensor_reduce(grank, cmp1, AX_X, ALU.add))
                link(v.tensor_scalar(grank, grank, TOPG - 0.5, None, ALU.is_lt))
                link(v.tensor_scalar(gs, grank, -NEG, NEG, ALU.mult, ALU.add))
                m4 = masked.rearrange("p j (g n) -> p (j g) n", g=NG)
                keep = grank.rearrange("p j g -> p (j g)").unsqueeze(2).to_broadcast([P, NT * NG, 8])
                drop = gs.rearrange("p j g -> p (j g)").unsqueeze(2).to_broadcast([P, NT * NG, 8])
                link(v.tensor_tensor(m4, ch, keep, ALU.mult))
                link(v.tensor_tensor(m4, m4, drop, ALU.add), own=True)
                for j in range(NT):
                    ins = v.max(top8[:, j, :], masked[:, j, :])
                link(ins, own=True)
                for j in range(NT):
                    ins = v.match_replace(sel[:, j, :], top8[:, j, :], masked[:, j, :], -3e38)
                link(ins)
                v.tensor_tensor(sel, sel, masked, ALU.not_equal).then_inc(s["sel_ready"], 1)
                dve.wait_ge(s["sel_ready"], l + 1)
                link(v.tensor_tensor(G, sel, score, ALU.mult))
                link(v.tensor_reduce(gsum, G, AX_X, ALU.add))
                link(v.reciprocal(grec, gsum))
                for j in range(NT):
                    v.tensor_scalar(G[:, j, :], G[:, j, :], grec[:, j:j + 1], ROUTED, ALU.mult, ALU.mult)
                dve.wait_ge(s["rank_done"], l + 1)
                rk = ps[:, 7, 0:NT * E].rearrange("p (j e) -> p j e", j=NT)
                v.scalar_tensor_tensor(R, rk, 1024.0, sel, ALU.add, ALU.mult)
                v.tensor_copy(ecol[0:E, 2:3], ps[0:E, 7, 3 * E:3 * E + 1])
                v.scalar_tensor_tensor(ecol[0:E, 0:1], ps[0:E, 7, 3 * E:3 * E + 1], float(E), const[0:E, C_KEYC:C_KEYC + 1], ALU.mult, ALU.add)
                link(v.scalar_tensor_tensor(key[0:E, :], ps[0:E, 7, 2 * E:3 * E], float(E), const[0:E, C_KEY:C_KEY + E], ALU.mult, ALU.add))
                link(v.tensor_scalar(above[0:E, :], key[0:E, :], ecol[0:E, 0:1], None, ALU.is_gt))
                link(v.tensor_reduce(ecol[0:E, 1:2], above[0:E, :], AX_X, ALU.add))
                v.tensor_scalar(place[0:E, :], const[0:E, C_ORDER:C_ORDER + E], ecol[0:E, 1:2], None, ALU.is_equal).then_inc(s["place_ready"], 1)
                v.tensor_scalar(R, R, -1024.0, None, ALU.add)
                dve.wait_ge(s["order_done"], l + 1)
                cnt = ps[0:1, 7, 4 * E:5 * E]
                v.tensor_copy(otab[0:1, :], ps[0:1, 7, 5 * E:6 * E])
                link(v.tensor_tensor(kweighted, cnt, const[0:1, C_WEIGHT:C_WEIGHT + E], ALU.mult))
                steps = T // QUAD_UNIT
                link(v.tensor_tensor(kabove, kweighted.unsqueeze(2).to_broadcast([1, E, steps]),
                                     const[0:1, C_STEP:C_STEP + steps].unsqueeze(1).to_broadcast([1, E, steps]), ALU.is_gt))
                link(v.tensor_reduce(kcnt, kabove, AX_X, ALU.add))
                k8 = kcnt.rearrange("p (c n) -> p c n", n=CYCLE)
                km = kmax.rearrange("p (c r) -> p c r", r=ROUNDS)
                for rd, (a, b) in enumerate(((0, 2), (2, 4), (4, 8))):
                    ins = v.tensor_reduce(km[:, :, rd:rd + 1], k8[:, :, a:b].unsqueeze(2), AX_X, ALU.max)
                link(ins)
                link(v.tensor_tensor_scan(kcum, ones[0:1, 0:CYCLES * ROUNDS], kmax, ubase, ALU.mult, ALU.add))
                v.tensor_copy(btab[0:1, 1:CYCLES * ROUNDS + 1], kcum)
                link(v.tensor_copy(btab[0:1, 0:1], ubase))
                v.tensor_copy(ubase, kcum[:, CYCLES * ROUNDS - 1:CYCLES * ROUNDS]).then_inc(s["table_ready"], 1)
                dve.wait_ge(s["shsil_ready"], l + 1)
                dve.wait_ge(s["sh_up_done"], l + 1)
                v.tensor_tensor(shmid.rearrange("p k t -> p (k t)"), shsil, ps[:, 6, :], ALU.mult).then_inc(s["shmid_ready"], 1)
                dve.wait_ge(s["table_ready"], l + 2)
                passed(dve)
                b0 = dve.value_load(btab[0:1, 0:1], min_val=B0, max_val=MAXB)

                def turned(b):
                    dve.wait_ge(s["ST_done"], b + l + 1)
                    passed(dve)
                    for g in range(4):
                        q = slice(g * QUAD_UNIT, (g + 1) * QUAD_UNIT)
                        v.tensor_scalar(gslot[q, :], ps[q, B_T, P + g:P + g + 1],
                                        ps[q, B_T, TW + P + 4 + g:TW + P + 5 + g], None, ALU.add)
                    return v.tensor_copy(ST.rearrange("p (j n) -> p j n", j=NT),
                                         ps[:, B_T, 0:NT * TW].rearrange("p (j n) -> p j n", j=NT)[:, :, 0:P])

                def parts(b, half, bank):
                    hi, lo = (y[:, half * 512:(half + 1) * 512] for y in (y_hi, y_lo))
                    dve.wait_ge(s["down_done"], b * 2 + half + 1)
                    v.tensor_copy(hi, ps[:, bank, :]).then_inc(s["hi_ready"], 1)
                    dve.wait_ge(s["hi_ready"], b * 2 + half + 1)
                    return v.tensor_tensor(lo, ps[:, bank, :], hi.bitcast(F32), ALU.subtract)

                turned(b0).then_inc(s["ST_ready"], 1)
                with dve.Fori(0, CYCLES * ROUNDS) as r:
                    begin, end = blocks(dve, r)
                    with dve.Fori(begin, end) as b:
                        dve.wait_ge(s["sil_ready"], b + 1)
                        dve.wait_ge(s["midT_done"], b)
                        dve.wait_ge(s["ST_ready"], b + l + 1)
                        passed(dve)
                        v.scalar_tensor_tensor(mid, ps[:, B_F, F:2 * F], gslot, sil, ALU.mult, ALU.mult).then_inc(s["mid_ready"], 1)
                        dve.wait_ge(s["midT_done"], b + 1)
                        dve.wait_ge(s["down_done"], b * 2)
                        v.tensor_copy(midT.rearrange("p k n -> p (k n)"), ps[:, B_T, 0:FT * P]).then_inc(s["midT_ready"], 1)
                        parts(b, 0, B_1).then_inc(s["y0_ready"], 1)
                        parts(b, 1, B_F).then_inc(s["y1_ready"], 1)
                        dve.wait_ge(s["scat_done"], b + 1)
                        turned(b + 1).then_inc(s["ST_ready"], 1)
                total = btab_value(dve, CYCLES * ROUNDS)
                dve.wait_ge(s["scat_done"], total)
                dve.wait_ge(s["hT_ready"], (total + l + 1) * 2)
                dve.wait_ge(s["rows2_in"], (l + 1) * 48)
                for j in range(NT):
                    norm_stats(1, j)
                for j in range(NT):
                    normalise(1, j)
                    norm_x(j).then_inc(s["x2_ready"], 1)
                dve.wait_ge(s["x2_ready"], (l + 1) * NT)
            assert links[1] == DVE_LINKS, links


_INS = ["x", "c", "positions", "w_ada", "b_ada", "w_in", "q_norm_g", "kv_norm_g", "w_uq", "w_ukv", "w_pool",
        "pool_scale", "w_out", "ln1_g", "ln1_b", "w_router", "router_bias", "w_exp_gate", "w_exp_up",
        "w_exp_down", "w_sh_gate", "w_sh_up", "w_sh_down", "ln2_g", "ln2_b"]


def kernel(**inputs):
    import concourse.bacc as _bacc
    from concourse.bass_utils import run_bass_kernel_spmd as _run

    nc = _bacc.Bacc("TRN2", target_bir_lowering=False, num_devices=1)
    arrays, args = {}, []
    consts, band = shape_constants()
    for name in _INS + ["consts", "band"]:
        a = np.ascontiguousarray({"consts": consts, "band": band}[name] if name in ("consts", "band") else inputs[name])
        arrays[f"in_{name}"] = a
        args.append(nc.dram_tensor(f"in_{name}", a.shape, mybir.dt.from_np(a.dtype), kind="ExternalInput").ap())
    out = nc.dram_tensor("out_x", (1, T, D), F32, kind="ExternalOutput").ap()
    decoder_trunk(nc, *args, out)
    r = _run(nc, [arrays], core_ids=[0])
    return r.results[0]["out_x"]
```
